# Optimizing a Trainium2 kernel written in Bass

```python
import math
import jax
import jax.numpy as jnp
from jax import lax
import numpy as np
import jax, jax.numpy as jnp

D_MODEL = 1024
BATCH = 1
SEQ = 256
DEPTH = 2

MIX_A = D_MODEL // 2
RET_HEADS = 4
RET_HEAD_DIM = (D_MODEL - MIX_A) // RET_HEADS
RET_WIDTH = RET_HEADS * RET_HEAD_DIM
IN_COLS = 2 * MIX_A + 4 * RET_WIDTH
CONV_WIDTH = 31
RET_CHUNK = 128
ROPE_BASE = 10000.0
S5_GROUP = 16
S5_GROUPS = D_MODEL // S5_GROUP
S5_STATE = 64
D_FF = 4 * D_MODEL
N_EVEN = (DEPTH + 1) // 2
N_ODD = DEPTH // 2
EPS = 1e-6


def _rmsnorm(x, g):
    xf = x.astype(jnp.float32)
    y = xf * lax.rsqrt(jnp.mean(xf * xf, axis=-1, keepdims=True) + EPS)
    return (y * g.astype(jnp.float32)).astype(x.dtype)

def _head_rmsnorm(x):
    xf = x.astype(jnp.float32)
    y = xf * lax.rsqrt(jnp.mean(xf * xf, axis=-1, keepdims=True) + EPS)
    return y.astype(x.dtype)

def _layernorm(x, g, b):
    xf = x.astype(jnp.float32)
    mu = jnp.mean(xf, axis=-1, keepdims=True)
    xc = xf - mu
    var = jnp.mean(xc * xc, axis=-1, keepdims=True)
    y = xc * lax.rsqrt(var + EPS) * g.astype(jnp.float32) + b.astype(jnp.float32)
    return y.astype(x.dtype)

def _rotary(t, cos, sin):
    half = t.shape[-1] // 2
    t1, t2 = t[..., :half], t[..., half:]
    cos = cos.astype(t.dtype)
    sin = sin.astype(t.dtype)
    return jnp.concatenate([t1 * cos - t2 * sin, t1 * sin + t2 * cos], axis=-1)

def _retention_bidir(q, k, v):
    bsz, seq, nh, dh = q.shape
    L = RET_CHUNK
    n = seq // L
    dt = q.dtype
    q = q.reshape(bsz, n, L, nh, dh)
    k = k.reshape(bsz, n, L, nh, dh)
    v = v.reshape(bsz, n, L, nh, dh)
    log_g = jnp.log1p(-jnp.exp2(-5.0 - jnp.arange(nh, dtype=jnp.float32)))
    idx = jnp.arange(L, dtype=jnp.float32)
    dist = jnp.abs(idx[:, None] - idx[None, :])
    dmat = jnp.exp(log_g[:, None, None] * dist).astype(dt)
    scores = jnp.einsum('bnihd,bnjhd->bnhij', q, k) * dmat[None, None]
    intra = jnp.einsum('bnhij,bnjhe->bnihe', scores, v)
    w_kf = jnp.exp(log_g[None, :] * (L - 1.0 - idx)[:, None]).astype(dt)
    w_kb = jnp.exp(log_g[None, :] * idx[:, None]).astype(dt)
    kv_f = jnp.einsum('bnjhd,jh,bnjhe->nbhde', k, w_kf, v)
    kv_b = jnp.einsum('bnjhd,jh,bnjhe->nbhde', k, w_kb, v)
    g_L = jnp.exp(log_g * L).astype(dt)[None, :, None, None]

    def step(state, kv):
        return g_L * state + kv, state

    init = jnp.zeros((bsz, nh, dh, dh), dtype=kv_f.dtype)
    _, s_f = lax.scan(step, init, kv_f)
    _, s_b = lax.scan(step, init, kv_b, reverse=True)
    w_qf = jnp.exp(log_g[None, :] * (idx + 1.0)[:, None]).astype(dt)
    w_qb = jnp.exp(log_g[None, :] * (L - idx)[:, None]).astype(dt)
    inter = (jnp.einsum('bnihd,ih,nbhde->bnihe', q, w_qf, s_f)
             + jnp.einsum('bnihd,ih,nbhde->bnihe', q, w_qb, s_b))
    return (intra + inter).reshape(bsz, seq, nh, dh)

def _mixer_conv_retention(h, w_in, conv_w, conv_b, cln_g, cln_b, w_out):
    bsz, seq, _ = h.shape
    proj = h @ w_in
    splits = [MIX_A, 2 * MIX_A, 2 * MIX_A + RET_WIDTH,
              2 * MIX_A + 2 * RET_WIDTH, 2 * MIX_A + 3 * RET_WIDTH]
    a_val, a_gate, q, k, v, g = jnp.split(proj, splits, axis=-1)
    a = a_val * jax.nn.sigmoid(a_gate)
    a = lax.conv_general_dilated(
        a, conv_w[:, None, :].astype(a.dtype), window_strides=(1,), padding='SAME',
        dimension_numbers=('NWC', 'WIO', 'NWC'), feature_group_count=MIX_A)
    a = jax.nn.silu(_layernorm(a + conv_b, cln_g, cln_b))
    q = q.reshape(bsz, seq, RET_HEADS, RET_HEAD_DIM)
    k = k.reshape(bsz, seq, RET_HEADS, RET_HEAD_DIM)
    v = v.reshape(bsz, seq, RET_HEADS, RET_HEAD_DIM)
    inv = ROPE_BASE ** (-jnp.arange(0, RET_HEAD_DIM, 2, dtype=jnp.float32) / RET_HEAD_DIM)
    ang = jnp.arange(seq, dtype=jnp.float32)[:, None] * inv[None, :]
    cos, sin = jnp.cos(ang)[:, None, :], jnp.sin(ang)[:, None, :]
    q = _rotary(q, cos, sin) * (RET_HEAD_DIM ** -0.5)
    k = _rotary(k, cos, sin)
    r = _head_rmsnorm(_retention_bidir(q, k, v)).reshape(bsz, seq, RET_WIDTH)
    r = jax.nn.silu(g) * r
    return jnp.concatenate([a, r], axis=-1) @ w_out

def _s5_combine(e1, e2):
    a1r, a1i, b1r, b1i = e1
    a2r, a2i, b2r, b2i = e2
    ar = a2r * a1r - a2i * a1i
    ai = a2r * a1i + a2i * a1r
    br = a2r * b1r - a2i * b1i + b2r
    bi = a2r * b1i + a2i * b1r + b2i
    return ar, ai, br, bi

def _mixer_s5(h, lam_re, lam_im, log_step, b_re, b_im, c_re, c_im, d_skip, w_glu_a, w_glu_b):
    bsz, seq, dm = h.shape
    f32 = jnp.float32
    u = h.astype(f32)
    ug = u.reshape(bsz, seq, S5_GROUPS, S5_GROUP)
    lr = jnp.minimum(lam_re.astype(f32), -1e-4)
    li = lam_im.astype(f32)
    dt = jnp.exp(log_step.astype(f32))[..., None]
    mag = jnp.exp(lr * dt)
    ab_re, ab_im = mag * jnp.cos(li * dt), mag * jnp.sin(li * dt)
    den = lr * lr + li * li
    nr, ni = ab_re - 1.0, ab_im
    f_re = (nr * lr + ni * li) / den
    f_im = (ni * lr - nr * li) / den
    br_, bi_ = b_re.astype(f32), b_im.astype(f32)
    bb_re = f_re[..., None] * br_ - f_im[..., None] * bi_
    bb_im = f_re[..., None] * bi_ + f_im[..., None] * br_
    cr, ci = c_re.astype(f32), c_im.astype(f32)

    def one_sequence(us):
        y = jnp.zeros_like(us)
        for direction in (0, 1):
            bu_re = jnp.einsum('sgc,gpc->sgp', us, bb_re[direction])
            bu_im = jnp.einsum('sgc,gpc->sgp', us, bb_im[direction])
            a_re = jnp.broadcast_to(ab_re[direction], bu_re.shape)
            a_im = jnp.broadcast_to(ab_im[direction], bu_re.shape)
            _, _, h_re, h_im = lax.associative_scan(
                _s5_combine, (a_re, a_im, bu_re, bu_im), reverse=(direction == 1), axis=0)
            y = y + (jnp.einsum('sgp,gcp->sgc', h_re, cr[direction])
                     - jnp.einsum('sgp,gcp->sgc', h_im, ci[direction]))
        return y

    y = lax.map(one_sequence, ug).reshape(bsz, seq, dm)
    y = (y + d_skip.astype(f32) * u).astype(h.dtype)
    z = jax.nn.gelu(y)
    return (z @ w_glu_a) * jax.nn.sigmoid(z @ w_glu_b)

def first_inputs(seed: int = 0) -> dict:
    key = jax.random.key(seed)
    ks = jax.random.split(key, 32)
    f32 = jnp.float32

    def nrm(k, shape, scale):
        return jax.random.normal(k, shape, f32) * scale

    P, G, Cg = S5_STATE, S5_GROUPS, S5_GROUP
    return {
        "x": nrm(ks[0], (BATCH, SEQ, D_MODEL), 1.0),
        "c": nrm(ks[1], (BATCH, D_MODEL), 1.0),
        "norm_g": 1.0 + nrm(ks[2], (DEPTH, 2, D_MODEL), 0.05),
        "ada_w": nrm(ks[3], (DEPTH, D_MODEL, 6 * D_MODEL), 0.5 * D_MODEL ** -0.5),
        "ada_b": nrm(ks[4], (DEPTH, 6 * D_MODEL), 0.02),
        "w_in": nrm(ks[5], (N_EVEN, D_MODEL, IN_COLS), D_MODEL ** -0.5),
        "conv_w": nrm(ks[6], (N_EVEN, CONV_WIDTH, MIX_A), CONV_WIDTH ** -0.5),
        "conv_b": nrm(ks[7], (N_EVEN, MIX_A), 0.02),
        "cln_g": 1.0 + nrm(ks[8], (N_EVEN, MIX_A), 0.05),
        "cln_b": nrm(ks[9], (N_EVEN, MIX_A), 0.02),
        "w_out": nrm(ks[10], (N_EVEN, MIX_A + RET_WIDTH, D_MODEL), (MIX_A + RET_WIDTH) ** -0.5),
        "s5_lam_re": -0.5 + nrm(ks[11], (N_ODD, 2, G, P), 0.01),
        "s5_lam_im": math.pi * jnp.arange(P, dtype=f32) + nrm(ks[12], (N_ODD, 2, G, P), 0.01),
        "s5_log_step": jax.random.uniform(ks[13], (N_ODD, 2, G), f32,
                                          math.log(1e-3), math.log(1e-1)),
        "s5_b_re": nrm(ks[14], (N_ODD, 2, G, P, Cg), (2 * Cg) ** -0.5),
        "s5_b_im": nrm(ks[15], (N_ODD, 2, G, P, Cg), (2 * Cg) ** -0.5),
        "s5_c_re": nrm(ks[16], (N_ODD, 2, G, Cg, P), 0.5),
        "s5_c_im": nrm(ks[17], (N_ODD, 2, G, Cg, P), 0.5),
        "s5_d": nrm(ks[18], (N_ODD, D_MODEL), 1.0),
        "w_glu_a": nrm(ks[19], (N_ODD, D_MODEL, D_MODEL), D_MODEL ** -0.5),
        "w_glu_b": nrm(ks[20], (N_ODD, D_MODEL, D_MODEL), D_MODEL ** -0.5),
        "w_fc1": nrm(ks[21], (DEPTH, D_MODEL, D_FF), D_MODEL ** -0.5),
        "w_fc2": nrm(ks[22], (DEPTH, D_FF, D_MODEL), D_FF ** -0.5),
        "norm_f": 1.0 + nrm(ks[23], (D_MODEL,), 0.05),
    }

def first_block(x, c, norm_g, ada_w, ada_b, w_in, conv_w, conv_b, cln_g, cln_b, w_out,
              s5_lam_re, s5_lam_im, s5_log_step, s5_b_re, s5_b_im, s5_c_re, s5_c_im, s5_d,
              w_glu_a, w_glu_b, w_fc1, w_fc2, norm_f):
    c_act = jax.nn.silu(c)
    for layer in range(DEPTH):
        mod = (c_act @ ada_w[layer] + ada_b[layer])[:, None, :]
        shift_m, scale_m, gate_m, shift_f, scale_f, gate_f = jnp.split(mod, 6, axis=-1)
        h = _rmsnorm(x, norm_g[layer, 0]) * (1.0 + scale_m) + shift_m
        if layer % 2 == 0:
            i = layer // 2
            mix = _mixer_conv_retention(h, w_in[i], conv_w[i], conv_b[i], cln_g[i],
                                        cln_b[i], w_out[i])
        else:
            i = layer // 2
            mix = _mixer_s5(h, s5_lam_re[i], s5_lam_im[i], s5_log_step[i], s5_b_re[i],
                            s5_b_im[i], s5_c_re[i], s5_c_im[i], s5_d[i],
                            w_glu_a[i], w_glu_b[i])
        x = x + gate_m * mix
        h = _rmsnorm(x, norm_g[layer, 1]) * (1.0 + scale_f) + shift_f
        x = x + gate_f * (jnp.square(jax.nn.relu(h @ w_fc1[layer])) @ w_fc2[layer])
    return _rmsnorm(x, norm_f)


DEPTH_2 = 1

MEM_LEN = 256
GLA_HEADS = 4
GLA_DK = 64
GLA_DV = 128
GLA_RANK = 16
GLA_TAU = 16.0
GLA_CHUNK = 64
GLA_QK = GLA_HEADS * GLA_DK
GLA_V = GLA_HEADS * GLA_DV
FOX_HEADS = 4
FOX_HD = 128
FOX_W = FOX_HEADS * FOX_HD
FOX_BLOCK = 128
MEM_HEADS = 4
MEM_HD = 128
MEM_W = MEM_HEADS * MEM_HD
N_BRANCH = 3
BRANCH_W = 512
D_FF_2 = -(-8 * D_MODEL // (3 * 256)) * 256

IN_SIZES = (GLA_QK, GLA_QK, GLA_V, GLA_V, GLA_RANK,
            FOX_W, FOX_W, FOX_W, FOX_HEADS,
            MEM_W,
            N_BRANCH * D_MODEL)
IN_WIDTH = sum(IN_SIZES)
IN_OFFSETS = tuple(int(o) for o in np.cumsum(IN_SIZES)[:-1])


def _rmsnorm_2(x, g):
    xf = x.astype(jnp.float32)
    y = xf * lax.rsqrt(jnp.mean(xf * xf, axis=-1, keepdims=True) + EPS)
    return (y * g.astype(jnp.float32)).astype(x.dtype)

def _heads(t, n):
    b, s, w = t.shape
    return t.reshape(b, s, n, w // n).transpose(0, 2, 1, 3)

def _merge(t):
    b, h, s, d = t.shape
    return t.transpose(0, 2, 1, 3).reshape(b, s, h * d)

def _gla(q, k, v, log_a):
    out_dtype = v.dtype
    b, h, s, dk = q.shape
    dv = v.shape[-1]
    c = GLA_CHUNK
    n = s // c
    qc = (q.astype(jnp.float32) * (GLA_DK ** -0.5)).reshape(b, h, n, c, dk)
    kc = k.astype(jnp.float32).reshape(b, h, n, c, dk)
    vc = v.astype(jnp.float32).reshape(b, h, n, c, dv)
    cum = jnp.cumsum(log_a.astype(jnp.float32).reshape(b, h, n, c, dk), axis=-2)
    cum_last = cum[..., -1:, :]
    q_in = qc * jnp.exp(cum)
    k_in = kc * jnp.exp(-cum)
    k_out = kc * jnp.exp(cum_last - cum)
    tril = jnp.tril(jnp.ones((c, c), dtype=bool))
    attn = jnp.where(tril, jnp.einsum('bhncd,bhnsd->bhncs', q_in, k_in), 0.0)
    o_intra = jnp.einsum('bhncs,bhnsv->bhncv', attn, vc)
    chunk_state = jnp.einsum('bhncd,bhncv->bhndv', k_out, vc)
    decay = jnp.exp(cum_last[..., 0, :])

    def step(state, inp):
        d, cs = inp
        return d[..., None] * state + cs, state

    _, s_in = lax.scan(step, jnp.zeros((b, h, dk, dv), jnp.float32),
                       (jnp.moveaxis(decay, 2, 0), jnp.moveaxis(chunk_state, 2, 0)))
    s_in = jnp.moveaxis(s_in, 0, 2)
    o_inter = jnp.einsum('bhncd,bhndv->bhncv', q_in, s_in)
    return (o_intra + o_inter).reshape(b, h, s, dv).astype(out_dtype)

def _fox(q, k, v, log_f):
    b, h, s, hd = q.shape
    nb = s // FOX_BLOCK
    scale = hd ** -0.5
    cum = jnp.cumsum(log_f, axis=-1)
    qb = jnp.moveaxis(q.reshape(b, h, nb, FOX_BLOCK, hd), 2, 0)
    cb = jnp.moveaxis(cum.reshape(b, h, nb, FOX_BLOCK), 2, 0)
    starts = jnp.arange(nb, dtype=jnp.int32) * FOX_BLOCK
    kpos = jnp.arange(s, dtype=jnp.int32)

    def block(args):
        q_i, c_i, i0 = args
        logits = (jnp.einsum('bhqd,bhkd->bhqk', q_i, k).astype(jnp.float32) * scale
                  + c_i[..., None] - cum[:, :, None, :])
        qpos = i0 + jnp.arange(FOX_BLOCK, dtype=jnp.int32)
        mask = kpos[None, :] <= qpos[:, None]
        p = jax.nn.softmax(jnp.where(mask, logits, -jnp.inf), axis=-1)
        return jnp.einsum('bhqk,bhkd->bhqd', p.astype(v.dtype), v)

    out = lax.map(block, (qb, cb, starts))
    return jnp.moveaxis(out, 0, 2).reshape(b, h, s, hd)

def _cross(q, k, v):
    logits = jnp.einsum('bhqd,bhkd->bhqk', q, k).astype(jnp.float32) * (q.shape[-1] ** -0.5)
    p = jax.nn.softmax(logits, axis=-1)
    return jnp.einsum('bhqk,bhkd->bhqd', p.astype(v.dtype), v)

def second_inputs(seed: int = 0) -> dict:
    key = jax.random.key(seed)
    ks = jax.random.split(key, 24)
    L, D = DEPTH_2, D_MODEL

    def nrm(k, shape, scale):
        return jax.random.normal(k, shape, jnp.float32) * scale

    def gain(k, shape):
        return 1.0 + 0.02 * jax.random.normal(k, shape, jnp.float32)

    return {
        "x": nrm(ks[0], (BATCH, SEQ, D), 1.0),
        "mem": nrm(ks[1], (BATCH, MEM_LEN, D), 1.0),
        "g_mix": gain(ks[2], (L, D)),
        "w_in": nrm(ks[3], (L, D, IN_WIDTH), D ** -0.5),
        "w_gla_a2": nrm(ks[4], (L, GLA_RANK, GLA_QK), GLA_RANK ** -0.5),
        "b_gla_a": nrm(ks[5], (L, GLA_QK), 0.1),
        "g_gla_out": gain(ks[6], (L, GLA_V)),
        "b_fox_f": nrm(ks[7], (L, FOX_HEADS), 0.1),
        "g_fox_q": gain(ks[8], (L, FOX_HD)),
        "g_fox_k": gain(ks[9], (L, FOX_HD)),
        "g_mem": gain(ks[10], (L, D)),
        "w_mem_kv": nrm(ks[11], (L, D, 2 * MEM_W), D ** -0.5),
        "g_mem_q": gain(ks[12], (L, MEM_HD)),
        "g_mem_k": gain(ks[13], (L, MEM_HD)),
        "b_gate": nrm(ks[14], (L, N_BRANCH * D), 0.1),
        "w_branch": nrm(ks[15], (L, N_BRANCH, BRANCH_W, D), BRANCH_W ** -0.5),
        "w_out": nrm(ks[16], (L, D, D), D ** -0.5),
        "g_ffn": gain(ks[17], (L, D)),
        "w_ffn_gate": nrm(ks[18], (L, D, D_FF_2), D ** -0.5),
        "w_ffn_up": nrm(ks[19], (L, D, D_FF_2), D ** -0.5),
        "w_ffn_down": nrm(ks[20], (L, D_FF_2, D), D_FF_2 ** -0.5),
    }

def second_block(x, mem, g_mix, w_in, w_gla_a2, b_gla_a, g_gla_out, b_fox_f, g_fox_q, g_fox_k,
              g_mem, w_mem_kv, g_mem_q, g_mem_k, b_gate, w_branch, w_out,
              g_ffn, w_ffn_gate, w_ffn_up, w_ffn_down):
    for l in range(DEPTH_2):
        h = _rmsnorm_2(x, g_mix[l])
        proj = h @ w_in[l]
        (gq, gk, gv, gg, ga1, fq, fk, fv, ff, mq, bg) = jnp.split(proj, IN_OFFSETS, axis=-1)

        log_a = jax.nn.log_sigmoid((ga1 @ w_gla_a2[l] + b_gla_a[l]).astype(jnp.float32)) / GLA_TAU
        o_gla = _gla(_heads(gq, GLA_HEADS), _heads(gk, GLA_HEADS), _heads(gv, GLA_HEADS),
                     _heads(log_a, GLA_HEADS))
        o_gla = _rmsnorm_2(o_gla, g_gla_out[l].reshape(GLA_HEADS, 1, GLA_DV))
        y_gla = _merge(o_gla) * jax.nn.silu(gg)

        log_f = jax.nn.log_sigmoid((ff + b_fox_f[l]).astype(jnp.float32)).transpose(0, 2, 1)
        o_fox = _fox(_rmsnorm_2(_heads(fq, FOX_HEADS), g_fox_q[l]),
                     _rmsnorm_2(_heads(fk, FOX_HEADS), g_fox_k[l]),
                     _heads(fv, FOX_HEADS), log_f)
        y_fox = _merge(o_fox)

        mkv = _rmsnorm_2(mem, g_mem[l]) @ w_mem_kv[l]
        mk, mv = jnp.split(mkv, 2, axis=-1)
        o_mem = _cross(_rmsnorm_2(_heads(mq, MEM_HEADS), g_mem_q[l]),
                       _rmsnorm_2(_heads(mk, MEM_HEADS), g_mem_k[l]),
                       _heads(mv, MEM_HEADS))
        y_mem = _merge(o_mem)

        gates = jax.nn.sigmoid(bg + b_gate[l])
        merged = None
        for i, y_b in enumerate((y_gla, y_fox, y_mem)):
            term = gates[..., i * D_MODEL:(i + 1) * D_MODEL] * (y_b @ w_branch[l, i])
            merged = term if merged is None else merged + term
        x = x + merged @ w_out[l]

        h2 = _rmsnorm_2(x, g_ffn[l])
        x = x + (jax.nn.silu(h2 @ w_ffn_gate[l]) * (h2 @ w_ffn_up[l])) @ w_ffn_down[l]
    return x


def setup_inputs(seed=0):
    out = dict(first_inputs(seed))
    for name, value in second_inputs(seed + 1).items():
        if name != "x":
            out[name + "_2"] = value
    return out


def reference(
    x, c, norm_g, ada_w, ada_b, w_in, conv_w, conv_b, cln_g, cln_b, w_out, s5_lam_re, s5_lam_im,
    s5_log_step, s5_b_re, s5_b_im, s5_c_re, s5_c_im, s5_d, w_glu_a, w_glu_b, w_fc1, w_fc2,
    norm_f, mem_2, g_mix_2, w_in_2, w_gla_a2_2, b_gla_a_2, g_gla_out_2, b_fox_f_2, g_fox_q_2,
    g_fox_k_2, g_mem_2, w_mem_kv_2, g_mem_q_2, g_mem_k_2, b_gate_2, w_branch_2, w_out_2,
    g_ffn_2, w_ffn_gate_2, w_ffn_up_2, w_ffn_down_2,
):
    x = first_block(
        x, c, norm_g, ada_w, ada_b, w_in, conv_w, conv_b, cln_g, cln_b, w_out, s5_lam_re,
        s5_lam_im, s5_log_step, s5_b_re, s5_b_im, s5_c_re, s5_c_im, s5_d, w_glu_a, w_glu_b,
        w_fc1, w_fc2, norm_f,
    )
    return second_block(
        x, mem_2, g_mix_2, w_in_2, w_gla_a2_2, b_gla_a_2, g_gla_out_2, b_fox_f_2, g_fox_q_2,
        g_fox_k_2, g_mem_2, w_mem_kv_2, g_mem_q_2, g_mem_k_2, b_gate_2, w_branch_2, w_out_2,
        g_ffn_2, w_ffn_gate_2, w_ffn_up_2, w_ffn_down_2,
    )


_drawn_inputs = setup_inputs


def setup_inputs(seed=0):
    import zlib

    import numpy as np

    out = dict(_drawn_inputs(seed))
    spreads = {}
    factors = {'conv_b': 8.0,
     'cln_g': 5.587,
     'cln_b': 8.0,
     's5_lam_re': 64.0,
     'g_mix_2': 3.464,
     'b_gla_a_2': 3.838,
     'g_gla_out_2': 8.0,
     'b_fox_f_2': 5.384,
     'g_fox_q_2': 8.0,
     'g_fox_k_2': 23.315,
     'g_mem_2': 8.0,
     'g_mem_q_2': 8.0,
     'g_mem_k_2': 8.0,
     'b_gate_2': 2.913,
     'g_ffn_2': 11.907}
    for name, (base, spread) in spreads.items():
        noise = np.random.default_rng([zlib.crc32(name.encode()), seed]).standard_normal(out[name].shape)
        drawn = base * np.exp(spread * noise) if base else spread * noise
        out[name] = jnp.asarray(drawn.astype(out[name].dtype))
    for name, factor in factors.items():
        out[name] = (out[name] * factor).astype(out[name].dtype)
    return out
```

```python
from contextlib import ExitStack

import numpy as np

import concourse.bass as bass
from concourse import mybir

F32 = mybir.dt.float32
I32 = mybir.dt.int32
ALU = mybir.AluOpType
ACT = mybir.ActivationFunctionType
AX_X = mybir.AxisListType.X

P = 128
T = 256
D = 1024
KT = D // P
EPS = 1e-6
RING = 4
SLOT = 4096
FF1 = 4096
FF2 = 2816
TAPS = 31
HEADS = 4
DK = 64
CHUNK = 64
NEG = -3.0e38
TWO_PI_A = 6.28125
TWO_PI_B = float(np.float32(np.round((2 * np.pi - 6.28125) * 2.0 ** 21) / 2.0 ** 21))
TWO_PI_C = 2 * np.pi - TWO_PI_A - TWO_PI_B
ROUND = 12582912.0
ADA = 12
PI_SAFE = 3.1415925
SW_ADA = 10

COLS = {}
_at = 0
for _name, _n in (("c", 8), ("norm_g", 32), ("ada_b", 96), ("conv_w", 4 * TAPS), ("conv_b", 4), ("cln_g", 4),
                  ("cln_b", 4), ("s5_d", 8), ("norm_f", 8), ("g_mix", 8), ("b_gla", 2), ("g_gla", 4),
                  ("g_fq", 1), ("g_fk", 1), ("g_mem", 8), ("g_mq", 1), ("g_mk", 1), ("b_gate", 24),
                  ("g_ffn", 8), ("b_fox", 1)):
    COLS[_name] = _at
    _at += _n
NCOLS = _at
GQ, GV, GG, GA, FQ, FK, FV, FFG, MQ, BG = 0, 512, 1024, 1536, 1552, 2064, 2576, 3088, 3092, 3604


def job_order():
    jobs = [f"ada{k}" for k in range(4)] + ["ms0"]
    jobs += ["av0", "ada4", "av1", "ada5", "ag0", "ada6", "ag1", "ada7", "q0", "ada8", "q1", "k0", "k1",
             "v0", "v1", "mu", "rot0", "rot1", "rot2", "rot3", "g0", "var", "g1"]
    jobs += ["sc0", "sc1", "sc2", "sc3", "ada9", "ro0", "rr0", "ro1", "rr1"] + [f"wo0.{p}" for p in range(4)] + ["ms1"]
    for j in range(16):
        jobs.append(f"f1.0.{j}")
        if 2 <= j < 16:
            jobs.append(f"ada{8 + j}")
    jobs += [f"f2.0.{p}" for p in range(4)] + ["ms2"]
    fill = {8: "mms", 16: "mk0", 18: "mkr0", 24: "mk1", 26: "mkr1", 32: "mv0", 40: "mv1"}
    for n in range(64):
        jobs.append(f"bu{n}")
        if n in fill:
            jobs.append(fill[n])
    jobs += ["ga0", "ga1", "gb0", "gb1", "ga2", "ga3", "gb2", "gb3", "ms3"]
    jobs += [f"f1.1.{j}" for j in range(16)] + [f"f2.1.{p}" for p in range(4)] + ["ms4", "ms5"]
    jobs += ["gq0", "gk0", "ga1r", "ff", "gv0", "gv1", "la", "gg0", "gg1", "fq0", "fq1", "kot", "cs0", "cs1",
             "nr0", "nr1", "at0", "at1", "fk0", "fk1", "go0", "gor0", "nr2", "nr3", "go1", "gor1",
             "fv0", "fv1", "mq0", "mq1"]
    bg = 0
    for u in range(10):
        if u < 8:
            jobs.append(f"us{u}")
        jobs.append(f"bg{bg}")
        bg += 1
        if u == 0:
            jobs += ["nr4", "nr5"]
        if 1 <= u <= 8:
            jobs.append(f"ut{u - 1}")
        if u >= 3 and u % 2 == 1:
            jobs.append(f"uo{(u - 3) // 2}")
    jobs += ["bg10", "bg11"]
    jobs += [f"br{i}.{p}" for i in range(3) for p in range(4)] + [f"w2o.{p}" for p in range(4)] + ["ms6"]
    for p in range(6):
        n = 2 if p < 5 else 1
        jobs += [f"fg{2 * p + i}" for i in range(n)] + [f"fu{2 * p + i}" for i in range(n)]
    jobs += [f"fd.{p}" for p in range(4)]
    return jobs


JOBS = job_order()
INDEX = {name: i for i, name in enumerate(JOBS)}
ROOTS = ["ms0", "var", "rr0", "rr1", "ms1", "ms2", "mms", "mkr0", "mkr1", "ms3", "ms4", "ms5", "nr0", "nr1", "gor0",
         "nr2", "nr3", "gor1", "nr4", "nr5", "ms6"]
BANKS = 6
ROTATING = [name for name in JOBS if not name.startswith("ada")]
TURN = {name: i for i, name in enumerate(ROTATING)}


def build(nc, a, out):
    ctx = ExitStack()
    with ctx:
        def sb(name, free, dt=F32, parts=P):
            return ctx.enter_context(nc.sbuf_tensor(name, [parts, free], dt))

        sems = {}

        def s(name):
            if name not in sems:
                sems[name] = ctx.enter_context(nc.semaphore("s_" + name))
            return sems[name]

        ring = [sb(f"ring{i}", SLOT) for i in range(RING)]
        adas = [sb(f"ada_slot{i}", SLOT) for i in range(2)]
        x = sb("x_res", KT * T)[:, :].rearrange("p (k t) -> p k t", k=KT)
        h = sb("h_in", KT * T)[:, :].rearrange("p (k t) -> p k t", k=KT)
        sq = sb("squares", KT * T)
        tmp = sb("tmp", KT * T)
        yt = sb("y_cat", KT * T)
        big = sb("big", 32 * T)
        dreg = sb("decay_or_mem", 2048)
        tabw = sb("tabw", 3072)
        accb = sb("ada_acc", 1024)
        rs = sb("rstd", 512)
        early = sb("early", 1984)
        scanmask = sb("scanmask", T)
        ident = sb("ident", P)
        inv = sb("inv", 3 * P)
        one = sb("one", 1)
        eps = sb("eps", 1)
        cols = sb("cols", NCOLS)
        mod = sb("mod", 96)
        gs = sb("gs", 8)
        cact = sb("cact", 8)
        gsc = sb("gsc", 2)
        small = sb("small", 8)
        bank = [ctx.enter_context(nc.psum_tensor(f"bank{i}", [P, 512], F32)) for i in range(8)]

        def col(name, i=0, n=1):
            return cols[:, COLS[name] + i:COLS[name] + i + n]

        inv1024, inv512, inv128 = (inv[:, i * P:(i + 1) * P] for i in range(3))
        sq3 = sq[:, :].rearrange("p (k t) -> p k t", k=KT)
        yt3 = yt[:, :].rearrange("p (k t) -> p k t", k=KT)
        big3 = big[:, :].rearrange("p (k t) -> p k t", k=32)
        tmp3 = tmp[:, :].rearrange("p (k t) -> p k t", k=KT)

        def ps(name):
            return bank[TURN[name] % BANKS] if name in TURN else bank[BANKS + int(name[3:]) % 2]

        def ps2(name):
            return ps(name)[:, :].rearrange("p (k t) -> p k t", k=2)

        APW = T + TAPS - 1
        a_pad = big[:, 0:4 * APW].rearrange("p (k t) -> p k t", k=4)
        conv = big[:, 1152:2176].rearrange("p (k t) -> p k t", k=4)
        a_sig = big[:, 2176:3200].rearrange("p (k t) -> p k t", k=4)
        qk = big[:, 3200:5248].rearrange("p (k t) -> p k t", k=8)
        v_nat = big[:, 5248:6272].rearrange("p (k t) -> p k t", k=2)
        g_silu = big[:, 6272:7296].rearrange("p (k t) -> p k t", k=4)
        cos_t, sin_t = early[:, 1344:1600], early[:, 1600:1856]
        perm = early[:, 1856:1984]
        dtab = dreg[:, :].rearrange("p (h k t) -> p h k t", h=4, k=2)
        sd = tmp[:, :].rearrange("p (h k t) -> p h k t", h=4, k=2)
        mag, f_re, f_im, nf_re, nf_im = (early[:, 64 * i:64 * i + 64] for i in range(5))
        rotp = early[:, 320:1344].rearrange("p (j c s) -> p j c s", j=8, c=2)
        sc = [tabw[:, 64 * i:64 * i + 64] for i in range(20)]
        tb = tabw[:, 0:2048].rearrange("p (s c t) -> p s c t", s=4, c=2)
        tm = tabw[:, 2048:3072].rearrange("p (f s c t) -> p f s c t", f=2, s=4, c=2)
        b_w = adas[0][:, :].rearrange("p (k d c m) -> p k d c m", k=8, d=2, c=2)
        c_w = adas[1][:, :].rearrange("p (s c m) -> p s c m", s=64, c=2)
        tabs = [big[:, 512 * i:512 * i + 512].rearrange("p (c t) -> p c t", c=2) for i in range(4)]
        pbuf = [big[:, 2048 + 1024 * i:3072 + 1024 * i].rearrange("p (f c t) -> p f c t", f=2, c=2) for i in range(2)]
        qbuf = [big[:, 4096 + 1024 * i:5120 + 1024 * i].rearrange("p (f c t) -> p f c t", f=2, c=2) for i in range(2)]
        wbuf = [big[:, 6144 + 512 * i:6656 + 512 * i].rearrange("p (c t) -> p c t", c=2) for i in range(2)]
        gbuf = [big[:, 7168 + 512 * i:7680 + 512 * i].rearrange("p (c t) -> p c t", c=2) for i in range(2)]
        hbuf = [tmp[:, 512 * i:512 * i + 512].rearrange("p (c t) -> p c t", c=2) for i in range(2)]
        u_rev = sq3
        mk_n = dreg[:, 0:1024].rearrange("p (k t) -> p k t", k=4)
        mv_nat = dreg[:, 1024:2048].rearrange("p (k t) -> p k t", k=2)
        A0, A1 = adas
        gq_s, gk_s = A0[:, 0:512], A0[:, 512:1024]
        la_x, la_c = A0[:, 1024:1536], A0[:, 1536:2048]
        e_pos, e_neg, e_out, k_in = (A0[:, 2048 + 512 * i:2560 + 512 * i] for i in range(4))
        go_n = A0[:, 1024:2048].rearrange("p (k t) -> p k t", k=4)
        go_sq = A0[:, 2560:3584]
        mq_n = accb[:, :].rearrange("p (k t) -> p k t", k=4)
        ys = [A1[:, 1024 * i:1024 * i + 1024].rearrange("p (k t) -> p k t", k=4) for i in range(3)]
        state = A1[:, 3072:3840].rearrange("p (c m v) -> p c m v", c=3, m=2)
        ga1_s = A1[0:16, 3840:4096]
        gv_nat = big[:, 6144:7168].rearrange("p (k t) -> p k t", k=2)
        gg_s = big[:, 7168:8192].rearrange("p (k t) -> p k t", k=4)
        gates = big3
        att = tmp[:, 0:1024].rearrange("p (k t) -> p k t", k=8)
        ko_nat = tmp[:, 1024:1536]
        ff_x, ff_c = tmp[0:64, 1536:1792], tmp[0:64, 1792:2048]
        fq_n = yt[:, 0:1024].rearrange("p (k t) -> p k t", k=4)
        fk_n = yt[:, 1024:2048].rearrange("p (k t) -> p k t", k=4)
        fv_nat = sq[:, 1024:2048].rearrange("p (k t) -> p k t", k=2)
        wsm = early[:, 0:640].rearrange("p (k c) -> p k c", k=8)
        wa2 = early[0:16, 640:896]
        fb = early[0:64, 896:1152]
        foxmask = early[:, 1152:1664].rearrange("p (k t) -> p k t", k=2)
        glamask = early[:, 1664:1792].bitcast(I32)
        logits = tabw[:, 0:512].rearrange("p (k t) -> p k t", k=2)
        probs = [tabw[:, 512 + 512 * i:1024 + 512 * i].rearrange("p (k t) -> p k t", k=2) for i in range(2)]
        prob_t = [tabw[:, 1536 + 512 * i:2048 + 512 * i].rearrange("p (k t) -> p k t", k=2) for i in range(2)]
        fa = [tabw[0:64, 2560 + 256 * i:2816 + 256 * i] for i in range(2)]

        tab_d = nc.dram_tensor("s5_tables", (64, P, 512), F32, kind="Internal").ap()

        panels = []

        def cols_panel(name, w, c0, n, last_job):
            panels.append((name, w[:, c0:c0 + n].rearrange("(k p) c -> p k c", p=P), KT, n, ("job", last_job)))

        def rows_panels(name, w, rows, last_job):
            k0, i = 0, 0
            while k0 < rows // P:
                nk = min(4, rows // P - k0)
                done = k0 + nk >= rows // P
                panels.append((f"{name}{i}", w[k0 * P:(k0 + nk) * P, :].rearrange("(k p) c -> p k c", p=P), nk, D,
                               ("job", last_job) if done else ("row", None)))
                k0 += nk
                i += 1

        for i, (name, job) in enumerate((("av", "av1"), ("ag", "ag1"), ("q", "q1"), ("k", "k1"), ("v", "v1"), ("g", "g1"))):
            cols_panel(name, a["w_in"], 512 * i, 512, job)
        for i in range(2):
            cols_panel(f"wo{i}", a["w_out"], 512 * i, 512, f"wo0.{2 * i + 1}")

        def ffn_panels(l):
            for i in range(8):
                cols_panel(f"f1.{l}.{i}", a["w_fc1"][l], 512 * i, 512, f"f1.{l}.{2 * i + 1}")
            rows_panels(f"f2.{l}.", a["w_fc2"][l], FF1, f"f2.{l}.3")

        ffn_panels(0)
        panels.append(("mem", a["mem"].rearrange("(k p) t -> p k t", p=P), KT, T, ("job", "mv1")))
        cols_panel("mk", a["w_mem_kv"], 0, 512, "mk1")
        cols_panel("mv", a["w_mem_kv"], 512, 512, "mv1")
        for i in range(2):
            cols_panel(f"ga{i}", a["w_glu_a"], 512 * i, 512, f"ga{2 * i + 1}")
            cols_panel(f"gb{i}", a["w_glu_b"], 512 * i, 512, f"gb{2 * i + 1}")
        ffn_panels(1)
        w2 = a["w_in_2"]
        cols_panel("gqk", w2, GQ, 512, "gk0")
        cols_panel("gv", w2, GV, 512, "gv1")
        cols_panel("gg", w2, GG, 512, "gg1")
        cols_panel("fq", w2, FQ, 512, "fq1")
        cols_panel("fk", w2, FK, 512, "fk1")
        cols_panel("fv", w2, FV, 512, "fv1")
        cols_panel("mq", w2, MQ, 512, "mq1")
        for i in range(6):
            cols_panel(f"bg{i}", w2, BG + 512 * i, 512, f"bg{2 * i + 1}")
        for i in range(3):
            rows_panels(f"br{i}.", a["w_branch"][i], 512, f"br{i}.3")
        for i in range(2):
            cols_panel(f"w2o{i}", a["w_out_2"], 512 * i, 512, f"w2o.{2 * i + 1}")
        for i in range(6):
            n = 512 if i < 5 else 256
            last = 2 * i + 1 if i < 5 else 10
            cols_panel(f"fg{i}", a["w_ffn_gate"], 512 * i, n, f"fg{last}")
            cols_panel(f"fu{i}", a["w_ffn_up"], 512 * i, n, f"fu{last}")
        rows_panels("fd", a["w_ffn_down"], FF2, "fd.3")
        place = {pn[0]: i for i, pn in enumerate(panels)}
        rows_before = []
        count = 0
        for pn in panels:
            count += pn[4][0] == "row"
            rows_before.append(count)

        def panel_view(name):
            i = place[name]
            _, _, k, n, _ = panels[i]
            return ring[i % RING][:, 0:k * n].rearrange("p (k c) -> p k c", k=k)

        mem_x = panel_view("mem")
        mem_sq = ring[place["mem"] % RING][:, 2048:4096]

        freed = {f"ms{n}": ("rstd", n + 1) for n in range(7)}
        for j in range(2):
            freed.update({f"av{j}": ("amul", j + 1), f"ag{j}": ("agsig", j + 1), f"q{j}": ("qkc", j + 1),
                          f"k{j}": ("qkc", j + 3), f"v{j}": ("vc", j + 1), f"g{j}": ("gsilu", j + 1),
                          f"ro{j}": ("rn", j + 1), f"rr{j}": ("rrs", j + 1)})
            freed.update({f"mk{j}": ("mkn", j + 1), f"mkr{j}": ("mkrs", j + 1), f"mv{j}": ("mvc", j + 1)})
            freed.update({f"gv{j}": ("gvc", j + 1), f"gg{j}": ("ggs", j + 1), f"at{j}": ("atc", j + 1),
                          f"go{j}": ("gon", 2 * j + 2), f"gor{j}": ("gors", j + 1), f"fv{j}": ("fvc", j + 1)})
            freed.update({f"fq{j}": ("nq", j + 1), f"fk{j}": ("nq", j + 3), f"mq{j}": ("nq", j + 5)})
        freed.update({"mu": ("lnxc", 2), "var": ("lnrs", 1), "mms": ("mrs", 1)})
        freed.update({f"rot{j}": ("rope", 3 * j + 2) for j in range(4)})
        freed.update({f"sc{j}": ("sd", j + 1) for j in range(4)})
        for r, name in ((0, "wo0"), (1, "f2.0"), (3, "f2.1"), (4, "w2o"), (5, "fd")):
            freed.update({f"{name}.{p}": ("xres", 8 * r + 2 * p + 2) for p in range(4)})
        freed.update({f"f1.{l}.{j}": ("relu", 16 * l + j + 1) for l in range(2) for j in range(16)})
        freed.update({f"bu{n}": ("s5p", 2 * n + 2) for n in range(64)})
        freed.update({f"ga{p}": ("glut", p + 1) for p in range(4)})
        freed.update({f"gb{p}": ("glus", p + 1) for p in range(4)})
        freed.update({"gq0": ("gqk", 1), "gk0": ("gqk", 2), "ga1r": ("ga1c", 1), "ff": ("ffx", 1), "la": ("lax", 2),
                      "kot": ("koc", 1), "cs0": ("gst", 5), "cs1": ("gst", 3)})
        freed.update({f"nr{i}": ("nrs", i + 1) for i in range(6)})
        freed.update({f"us{u}": ("ul", u + 1) for u in range(8)})
        freed.update({f"ut{u}": ("upt", u + 1) for u in range(8)})
        freed.update({f"uo{j}": ("uoc", j + 1) for j in range(4)})
        freed.update({f"bg{j}": ("gate", 2 * j + 2) for j in range(12)})
        freed.update({f"br{i}.{p}": ("mgm", 4 * i + p + 1) for i in range(3) for p in range(4)})
        freed.update({f"fg{i}": ("fsil", i + 1) for i in range(11)})
        freed.update({f"fu{i}": ("fact", i + 1) for i in range(11)})

        def job_wait(eng, name):
            eng.wait_ge(s("job"), INDEX[name] + 1)

        NORM_G = (("norm_g", 0), ("norm_g", 8), ("norm_g", 16), ("norm_g", 24), ("norm_f", 0), ("g_mix", 0), ("g_ffn", 0))
        NCONST = 6
        NLATE = 8

        block = ctx.enter_context(nc.Block())

        @block.sync
        def _(sp):
            sp.dma_start(cols[:, :], a["cols"]).then_inc(s("cols_in"), 16)
            sp.dma_start(x, a["x"].rearrange("(k p) t -> p k t", p=P)).then_inc(s("x_in"), 16)
            for i, (name, src, k, n, _) in enumerate(panels):
                if i >= RING:
                    kind, job = panels[i - RING][4]
                    if kind == "job":
                        job_wait(sp, job)
                    else:
                        sp.wait_ge(s("row_panel"), rows_before[i - RING])
                sp.dma_start(panel_view(name), src).then_inc(s(f"panel{i % RING}"), 16)
            for p in range(4):
                sp.wait_ge(s("xres"), 8 * 5 + 2 * p + 2)
                sp.dma_start(out[2 * p * P:(2 * p + 2) * P, :].rearrange("(k p) t -> p k t", p=P),
                             yt3[:, 2 * p:2 * p + 2, :]).then_inc(s("out"), 16)
            sp.wait_ge(s("out"), 64)

        def ada_in(k):
            return s(f"ada_{'sw' if k < SW_ADA else 'hw'}{k % 2}"), 16 * ((k - SW_ADA if k >= SW_ADA else k) // 2 + 1)

        def ada_load(eng, k):
            if k >= 2:
                eng.wait_ge(s("ada_acc"), k - 1)
            l, c = divmod(k, ADA)
            eng.dma_start(adas[k % 2][:, :].rearrange("p (k c) -> p k c", k=KT),
                          a["ada_w"][l][:, 512 * c:512 * c + 512].rearrange("(k p) c -> p k c", p=P)).then_inc(ada_in(k)[0], 16)

        @block.gpsimd
        def _(pool):
            pool.dma_start(tabw[:, 0:192], a["s5_scal"]).then_inc(s("s5_in"), 16)
            ada_load(pool, 0)
            ada_load(pool, 1)
            pool.dma_start(dreg[:, :], a["decay"]).then_inc(s("const_in"), 16)
            pool.dma_start(early[:, 1344:1984], a["rope"]).then_inc(s("const_in"), 16)
            pool.dma_start(ident[:, :], a["ident"]).then_inc(s("const_in"), 16)
            pool.dma_start(scanmask[:, :], a["scanmask"]).then_inc(s("const_in"), 16)
            for i, n in enumerate((1024, 512, 128)):
                pool.memset(inv[:, i * P:(i + 1) * P], 1.0 / n).then_inc(s("pool_const"), 1)
            pool.memset(one[:, :], 1.0).then_inc(s("pool_const"), 1)
            pool.memset(eps[:, :], EPS).then_inc(s("pool_const"), 1)
            pool.memset(big[:, 0:4 * APW], 0.0).then_inc(s("pool_const"), 1)
            for k in range(2, 9):
                ada_load(pool, k)
            pool.wait_ge(s("s5_scal"), 1)
            done = 0

            def step(ins):
                ins.then_inc(s("tab_step"), 1)

            for b in range(16):
                if b:
                    pool.wait_ge(s("tab_out"), 16 * b)
                if b == 1:
                    ada_load(pool, 9)
                step(pool.memset(tb[:, :, 0, 0:1], 1.0))
                step(pool.memset(tb[:, :, 1, 0:1], 0.0))
                done += 2
                for j in range(8):
                    n = 1 << j
                    for t0 in range(0, n, 64):
                        w = min(64, n)
                        src = tb[:, :, :, t0:t0 + w]
                        pool.wait_ge(s("tab_step"), done)
                        for r in range(2):
                            rot = rotp[:, j, r, 4 * b:4 * b + 4].unsqueeze(2).unsqueeze(3)
                            step(pool.tensor_tensor(tm[:, r, :, :, 0:w], src, rot.broadcast_to([P, 4, 2, w]), ALU.mult))
                        done += 2
                        pool.wait_ge(s("tab_step"), done)
                        step(pool.tensor_tensor(tb[:, :, 0, n + t0:n + t0 + w], tm[:, 0, :, 0, 0:w], tm[:, 1, :, 1, 0:w], ALU.subtract))
                        step(pool.tensor_tensor(tb[:, :, 1, n + t0:n + t0 + w], tm[:, 1, :, 0, 0:w], tm[:, 0, :, 1, 0:w], ALU.add))
                        done += 2
                pool.wait_ge(s("tab_step"), done)
                pool.dma_start(tab_d[4 * b:4 * b + 4].rearrange("s p f -> p s f"),
                               tabw[:, 0:2048].rearrange("p (s f) -> p s f", s=4)).then_inc(s("tab_out"), 16)
            pool.wait_ge(s("tab_out"), 256)
            pool.wait_ge(s("ada_acc"), 24)
            pool.dma_start(adas[0][:, :], a["s5_b"]).then_inc(s("bc_in"), 16)
            pool.dma_start(tmp[:, :], a["s5_c"][:, 0, :]).then_inc(s("bc_in"), 16)
            pool.dma_start(tabw[:, 0:2048], a["s5_c"][:, 1, :]).then_inc(s("bc_in"), 16)
            pool.wait_ge(s("bc_in"), 48)
            n = 0
            for d in range(2):
                c_re = tmp[:, 1024 * d:1024 * d + 1024].rearrange("p (s m) -> p s m", s=32)
                c_im = tabw[:, 1024 * d:1024 * d + 1024].rearrange("p (s m) -> p s m", s=32)
                part = tabw[:, 2048:3072].rearrange("p (s m) -> p s m", s=32)
                o_re, o_im = c_w[:, 32 * d:32 * d + 32, 0, :], c_w[:, 32 * d:32 * d + 32, 1, :]

                def f(v):
                    return v[:, 32 * d:32 * d + 32].unsqueeze(2).broadcast_to([P, 32, 32])

                for o, p0, f0, p1, f1, op in ((o_re, c_re, f_re, c_im, f_im, ALU.subtract),
                                              (o_im, c_re, nf_im, c_im, nf_re, ALU.add)):
                    pool.tensor_tensor(o, p0, f(f0), ALU.mult).then_inc(s("cw"), 1)
                    if n:
                        pool.wait_ge(s("cw"), n)
                    pool.tensor_tensor(part, p1, f(f1), ALU.mult).then_inc(s("cw"), 1)
                    pool.wait_ge(s("cw"), n + 2)
                    pool.tensor_tensor(o, o, part, op).then_inc(s("cw"), 1)
                    n += 3
            for n in range(65):
                if n < 64:
                    pool.wait_ge(s("s5p"), 2 * n + 2)
                    if n >= 2:
                        pool.wait_ge(s("s5g"), 2 * n - 2)
                    pb, w = pbuf[n % 2], wbuf[n % 2]
                    pool.tensor_tensor(w[:, 0, :], pb[:, 0, 0, :], pb[:, 1, 1, :], ALU.add).then_inc(s("s5w"), 1)
                    pool.tensor_tensor(w[:, 1, :], pb[:, 0, 1, :], pb[:, 1, 0, :], ALU.subtract).then_inc(s("s5w"), 1)
                if n >= 1:
                    m = n - 1
                    pool.wait_ge(s("s5q"), 2 * m + 2)
                    if m >= 2:
                        pool.wait_ge(s("s5y"), m - 1)
                    qb, hb = qbuf[m % 2], hbuf[m % 2]
                    o = hb[:, :, ::-1] if m % 2 else hb[:, :, :]
                    pool.tensor_tensor(o[:, 0, :], qb[:, 0, 0, :], qb[:, 1, 1, :], ALU.subtract).then_inc(s("s5h"), 1)
                    pool.tensor_tensor(o[:, 1, :], qb[:, 1, 0, :], qb[:, 0, 1, :], ALU.add).then_inc(s("s5h"), 1)
            for n in range(4, 12):
                p = n % 4
                pool.wait_ge(s("mgm"), n + 1)
                merged = yt3[:, 2 * p:2 * p + 2, :]
                pool.tensor_tensor(merged, merged, tmp3[:, 2 * p:2 * p + 2, :], ALU.add).then_inc(s("mga"), 1)

        @block.scalar
        def _(act):
            act.wait_ge(s("cols_in"), 16)
            act.activation(cact[:, :], col("c", 0, 8), ACT.Silu).then_inc(s("cact"), 1)
            act.wait_ge(s("s5_in"), 16)
            act.activation(sc[3], sc[2], ACT.Exp).then_inc(s("s5a"), 1)
            act.wait_ge(s("s5d"), 2)
            act.activation(mag, sc[5], ACT.Exp).then_inc(s("s5a"), 1)
            act.wait_ge(s("s5d"), 9)
            act.activation(rotp[:, 0, 1, :], sc[7], ACT.Sin).then_inc(s("s5a"), 1)
            act.activation(sc[8], sc[7], ACT.Sin, scale=0.5).then_inc(s("s5a"), 1)

            def root(job, width=T):
                job_wait(act, job)
                act.activation(ps(job)[:, 0:width], ps(job)[:, 0:width], ACT.Sqrt, bias=eps[:, :]).then_inc(s("root"), 1)

            def squares(n):
                for c in range(4):
                    if n == 0:
                        act.wait_ge(s("x_in"), 16)
                    elif n == 5:
                        act.wait_ge(s("hn"), 8 * 4 + 2 * c + 2)
                    else:
                        act.wait_ge(s("xres"), 8 * {1: 0, 2: 1, 3: 2, 4: 3, 6: 4}[n] + 2 * c + 2)
                    act.activation(sq3[:, 2 * c:2 * c + 2, :], x[:, 2 * c:2 * c + 2, :], ACT.Square).then_inc(s("sq"), 1)
                root(f"ms{n}")

            def shift(n):
                act.wait_ge(s("mod"), ADA * (n // 2) + (2 if n % 2 == 0 else 8))
                for k in range(KT):
                    act.wait_ge(s("hn"), 8 * n + k + 1)
                    i = 48 * (n // 2) + 24 * (n % 2) + k
                    act.activation(h[:, k, :], h[:, k, :], ACT.Identity, bias=mod[:, i:i + 1]).then_inc(s("h"), 1)

            act.wait_ge(s("pool_const"), 6)
            squares(0)
            shift(0)
            for j in range(2):
                job_wait(act, f"ag{j}")
                act.activation(a_sig[:, 2 * j:2 * j + 2, :], ps2(f"ag{j}"), ACT.Sigmoid).then_inc(s("agsig"), 1)
            for j, name in enumerate(("q0", "q1", "k0", "k1")):
                job_wait(act, name)
                act.activation(qk[:, 2 * j:2 * j + 2, :], ps2(name), ACT.Copy).then_inc(s("qkc"), 1)
            for j in range(2):
                job_wait(act, f"v{j}")
                act.activation(v_nat[:, j, :], ps(f"v{j}")[:, :], ACT.Copy).then_inc(s("vc"), 1)
            for j in range(2):
                act.wait_ge(s("lnxc"), j + 1)
                act.activation(sq3[:, 2 * j:2 * j + 2, :], conv[:, 2 * j:2 * j + 2, :], ACT.Square).then_inc(s("lnsq"), 1)
            root("var")
            for j in range(2):
                job_wait(act, f"g{j}")
                act.activation(g_silu[:, 2 * j:2 * j + 2, :], ps2(f"g{j}"), ACT.Silu).then_inc(s("gsilu"), 1)
            for i in range(4):
                act.wait_ge(s("lny"), i + 1)
                act.activation(yt3[:, i, :], conv[:, i, :], ACT.Silu, bias=col("cln_b", i)).then_inc(s("yconv"), 1)
            for j in range(2):
                job_wait(act, f"ro{j}")
                act.activation(sq[:, 1024 + 512 * j:1536 + 512 * j], ps(f"ro{j}")[:, :], ACT.Square).then_inc(s("rsq"), 1)
                root(f"rr{j}", 512)
            squares(1)
            shift(1)

            def relus(l, after):
                for j in range(16):
                    job_wait(act, f"f1.{l}.{j}")
                    act.activation(big3[:, 2 * j:2 * j + 2, :], ps2(f"f1.{l}.{j}"), ACT.Relu).then_inc(s("relu"), 1)
                    after(j)

            def next_ada(j):
                if 12 + j < 24:
                    ada_load(act, 12 + j)

            ada_load(act, 10)
            ada_load(act, 11)
            relus(0, next_ada)
            squares(2)
            shift(2)
            for k in range(KT):
                act.wait_ge(s("h"), 16 + k + 1)
                act.activation(u_rev[:, k, :], h[:, k, ::-1], ACT.Copy).then_inc(s("ur"), 1)
            act.wait_ge(s("tab_out"), 256)

            def table(n):
                if n < 64:
                    if n >= 4:
                        act.wait_ge(s("s5q"), 2 * (n - 4) + 2)
                    k, q, d = n // 8, n // 2 % 4, n % 2
                    act.dma_start(big[:, 512 * (n % 4):512 * (n % 4) + 512], tab_d[32 * d + 4 * k + q]).then_inc(s(f"tab{n % 4}"), 16)

            for n in range(4):
                table(n)
            i = place["mem"]
            act.wait_ge(s(f"panel{i % RING}"), 16 * (i // RING + 1))
            for c in range(4):
                act.activation(mem_sq[:, 512 * c:512 * c + 512].rearrange("p (k t) -> p k t", k=2), mem_x[:, 2 * c:2 * c + 2, :], ACT.Square).then_inc(s("msq"), 1)
            for n in range(4, 68):
                table(n)
                m = n - 4
                if m == 9:
                    root("mms")
                if m in (16, 24):
                    j = (m - 16) // 8
                    job_wait(act, f"mk{j}")
                    act.activation(mem_sq[:, 512 * j:512 * j + 512], ps(f"mk{j}")[:, :], ACT.Square).then_inc(s("mksq"), 1)
                if m in (18, 26):
                    root(f"mkr{(m - 18) // 8}", 512)
                if m in (34, 42):
                    j = (m - 34) // 8
                    job_wait(act, f"mv{j}")
                    act.activation(mv_nat[:, j, :], ps(f"mv{j}")[:, :], ACT.Copy).then_inc(s("mvc"), 1)
                if m >= 11 and (m - 11) % 8 == 0:
                    k = (m - 11) // 8
                    act.wait_ge(s("s5z"), k + 1)
                    act.activation(yt3[:, k, :], yt3[:, k, :], ACT.Gelu_apprx_tanh).then_inc(s("z"), 1)
            act.wait_ge(s("s5z"), 8)
            act.activation(yt3[:, 7, :], yt3[:, 7, :], ACT.Gelu_apprx_tanh).then_inc(s("z"), 1)
            act.dma_start(wsm[:, :, 0:64], a["w_fox_f"].rearrange("(k p) c -> p k c", p=P)).then_inc(s("late"), 16)
            act.dma_start(wsm[:, :, 64:80], a["w_in_2"][:, GA:GA + 16].rearrange("(k p) c -> p k c", p=P)).then_inc(s("late"), 16)
            act.dma_start(wa2, a["w_gla_a2"]).then_inc(s("late"), 16)
            act.dma_start(early[:, 1152:1664], a["foxmask"]).then_inc(s("late"), 16)
            act.dma_start(glamask, a["glamask"]).then_inc(s("late"), 16)
            for p in range(4):
                job_wait(act, f"gb{p}")
                act.activation(tmp3[:, 2 * p:2 * p + 2, :], ps2(f"gb{p}"), ACT.Sigmoid).then_inc(s("glus"), 1)
            squares(3)
            shift(3)
            relus(1, lambda j: None)
            squares(4)
            squares(5)
            for j, (name, o) in enumerate((("gq0", gq_s), ("gk0", gk_s))):
                job_wait(act, name)
                act.activation(o, ps(name)[:, :], ACT.Copy).then_inc(s("gqk"), 1)
            job_wait(act, "ga1r")
            act.activation(ga1_s, ps("ga1r")[0:16, 0:T], ACT.Copy).then_inc(s("ga1c"), 1)
            for j in range(2):
                job_wait(act, f"gv{j}")
                act.activation(gv_nat[:, j, :], ps(f"gv{j}")[:, :], ACT.Copy).then_inc(s("gvc"), 1)
            for j in range(2):
                job_wait(act, f"gg{j}")
                act.activation(gg_s[:, 2 * j:2 * j + 2, :], ps2(f"gg{j}"), ACT.Silu).then_inc(s("ggs"), 1)
            act.wait_ge(s("ffa"), 1)
            act.activation(ff_c, ff_c, ACT.Exp, scale=-1.0).then_inc(s("ffe"), 1)
            act.wait_ge(s("ffe"), 1)
            act.activation(ff_c, ff_c, ACT.Ln, bias=1.0).then_inc(s("ffe"), 1)
            act.wait_ge(s("lab"), 1)
            act.activation(la_c, la_c, ACT.Exp, scale=-1.0).then_inc(s("lae"), 1)
            act.wait_ge(s("lae"), 1)
            act.activation(la_c, la_c, ACT.Ln, bias=1.0).then_inc(s("lae"), 1)
            act.wait_ge(s("lac"), 2)
            act.activation(e_pos, la_c, ACT.Exp, scale=1.0 / 16).then_inc(s("lax_e"), 1)
            act.activation(e_neg, la_c, ACT.Exp, scale=-1.0 / 16).then_inc(s("lax_e"), 1)
            act.wait_ge(s("lad"), 1)
            act.activation(e_out, e_out, ACT.Exp, scale=1.0 / 16).then_inc(s("lax_e"), 1)

            def head_squares(i, name):
                if i >= 2:
                    job_wait(act, f"nr{i - 2}")
                job_wait(act, name)
                act.activation(sq[:, 512 * (i % 2):512 * (i % 2) + 512], ps(name)[:, :], ACT.Square).then_inc(s("nsq"), 1)

            head_squares(0, "fq0")
            head_squares(1, "fq1")
            job_wait(act, "kot")
            act.activation(ko_nat, ps("kot")[:, :], ACT.Copy).then_inc(s("koc"), 1)
            root("nr0", 512)
            root("nr1", 512)
            head_squares(2, "fk0")
            head_squares(3, "fk1")
            for j in range(2):
                job_wait(act, f"go{j}")
                act.activation(go_sq[:, 512 * j:512 * j + 512], ps(f"go{j}")[:, :], ACT.Square).then_inc(s("gosq"), 1)
                root(f"gor{j}", 512)
                if j == 0:
                    root("nr2", 512)
                    root("nr3", 512)
            for j in range(2):
                job_wait(act, f"fv{j}")
                act.activation(fv_nat[:, j, :], ps(f"fv{j}")[:, :], ACT.Copy).then_inc(s("fvc"), 1)
            head_squares(4, "mq0")
            head_squares(5, "mq1")

            def gate(j):
                job_wait(act, f"bg{j}")
                for i in range(2):
                    m = 2 * j + i
                    act.activation(gates[:, m, :], ps2(f"bg{j}")[:, i, :], ACT.Sigmoid, bias=col("b_gate", m)).then_inc(s("gate"), 1)

            for u in range(10):
                if u < 8:
                    for i in range(2):
                        act.wait_ge(s("unm"), u + 1)
                        if u >= 2:
                            job_wait(act, f"ut{u - 2}")
                        act.activation(probs[u % 2][:, i, :], logits[:, i, :], ACT.Exp, bias=small[:, 2 + i:3 + i],
                                       accum_out=small[:, 4 + i:5 + i]).then_inc(s("ue"), 1)
                gate(u)
                if u == 0:
                    root("nr4", 512)
                    root("nr5", 512)
                if 1 <= u <= 8:
                    job_wait(act, f"ut{u - 1}")
                    if u >= 3:
                        job_wait(act, f"uo{(u - 3) // 2}")
                    act.activation(tabw[:, 1536 + 512 * ((u - 1) % 2):2048 + 512 * ((u - 1) % 2)], ps(f"ut{u - 1}")[:, :], ACT.Copy).then_inc(s("upt"), 1)
                if u >= 3 and u % 2 == 1:
                    j = (u - 3) // 2
                    job_wait(act, f"uo{j}")
                    act.activation(ys[1 + j // 2][:, 2 * (j % 2):2 * (j % 2) + 2, :], ps2(f"uo{j}"), ACT.Copy).then_inc(s("uoc"), 1)
            gate(10)
            gate(11)
            squares(6)
            for p in range(6):
                for i in range(2 * p, min(2 * p + 2, 11)):
                    job_wait(act, f"fg{i}")
                    if i >= 4:
                        act.wait_ge(s("fact"), i - 3)
                    act.activation(tmp[:, 512 * (i % 4):512 * (i % 4) + 512], ps(f"fg{i}")[:, :], ACT.Silu).then_inc(s("fsil"), 1)

        @block.vector
        def _(dve):
            count = [0]

            def link(ins):
                count[0] += 1
                ins.then_inc(s("s5d"), 1)
                dve.wait_ge(s("s5d"), count[0])

            tt, ts, stt = dve.tensor_tensor, dve.tensor_scalar, dve.scalar_tensor_tensor
            li, dt = sc[1], sc[3]
            dve.wait_ge(s("s5_in"), 16)
            link(ts(sc[4], sc[0], -1e-4, None, ALU.min))
            dve.wait_ge(s("s5a"), 1)
            link(tt(sc[5], sc[4], dt, ALU.mult))
            link(tt(sc[6], li, dt, ALU.mult))
            link(ts(sc[7], sc[6], 1.0 / (2 * np.pi), ROUND, ALU.mult, ALU.add))
            link(ts(sc[9], sc[7], ROUND, None, ALU.subtract))
            link(stt(sc[6], sc[9], -TWO_PI_A, sc[6], ALU.mult, ALU.add))
            link(stt(sc[6], sc[9], -TWO_PI_B, sc[6], ALU.mult, ALU.add))
            link(stt(sc[6], sc[9], -TWO_PI_C, sc[6], ALU.mult, ALU.add))
            link(ts(sc[7], sc[6], PI_SAFE, -PI_SAFE, ALU.min, ALU.max))
            dve.wait_ge(s("s5a"), 4)
            c1, s1 = rotp[:, 0, 0, :], rotp[:, 0, 1, :]
            link(tt(sc[9], sc[8], sc[8], ALU.mult))
            link(ts(c1, sc[9], -2.0, 1.0, ALU.mult, ALU.add))
            abr, abi, nr, den, t0, t1 = sc[10], sc[11], sc[12], sc[13], sc[14], sc[15]
            link(tt(abr, mag, c1, ALU.mult))
            link(tt(abi, mag, s1, ALU.mult))
            link(ts(nr, abr, -1.0, None, ALU.add))
            link(tt(t0, sc[4], sc[4], ALU.mult))
            link(tt(t1, li, li, ALU.mult))
            link(tt(den, t0, t1, ALU.add))
            link(dve.reciprocal(den, den))
            link(tt(t0, nr, sc[4], ALU.mult))
            link(tt(t1, abi, li, ALU.mult))
            link(tt(t0, t0, t1, ALU.add))
            link(tt(f_re, t0, den, ALU.mult))
            link(tt(t0, abi, sc[4], ALU.mult))
            link(tt(t1, nr, li, ALU.mult))
            link(tt(t0, t0, t1, ALU.subtract))
            link(tt(f_im, t0, den, ALU.mult))
            link(ts(nf_re, f_re, -1.0, None, ALU.mult))
            link(ts(nf_im, f_im, -1.0, None, ALU.mult))
            for j in range(7):
                cj, sj = rotp[:, j, 0, :], rotp[:, j, 1, :]
                link(tt(t0, cj, cj, ALU.mult))
                link(tt(t1, sj, sj, ALU.mult))
                link(tt(rotp[:, j + 1, 0, :], t0, t1, ALU.subtract))
                link(tt(t0, cj, sj, ALU.mult))
                if j < 6:
                    link(ts(rotp[:, j + 1, 1, :], t0, 2.0, None, ALU.mult))
                else:
                    ts(rotp[:, j + 1, 1, :], t0, 2.0, None, ALU.mult).then_inc(s("s5_scal"), 1)

            def ada_acc(k):
                dve.wait_ge(*ada_in(k))
                if k >= 2:
                    job_wait(dve, f"ada{k - 2}")
                w = adas[k % 2][:, :].rearrange("p (k c) -> p k c", k=KT)
                acc = accb[:, 512 * (k % 2):512 * (k % 2) + 512]
                if k == 0:
                    dve.wait_ge(s("cact"), 1)
                for i in range(KT):
                    if i == 0:
                        ts(acc, w[:, 0, :], cact[:, 0:1], None, ALU.mult).then_inc(s("ada_part"), 1)
                    else:
                        dve.wait_ge(s("ada_part"), 7 * k + i)
                        stt(acc, w[:, i, :], cact[:, i:i + 1], acc, ALU.mult, ALU.add)\
                            .then_inc(s("ada_part") if i < KT - 1 else s("ada_acc"), 1)

            def ada_mod(k):
                job_wait(dve, f"ada{k}")
                tt(mod[:, 4 * k:4 * k + 4], ps(f"ada{k}")[:, 0:4], col("ada_b", 4 * k, 4), ALU.add).then_inc(s("mod"), 1)

            def rms(job, width=T, sem="rstd"):
                dve.wait_ge(s("root"), ROOTS.index(job) + 1)
                return dve.reciprocal(rs[:, 0:width], ps(job)[:, 0:width]).then_inc(s(sem), 1)

            def norm(n):
                name, g0 = NORM_G[n]
                gain = col(name, g0, 8)
                if n < 4:
                    l, f = divmod(n, 2)
                    dve.wait_ge(s("mod"), ADA * l + 6 * f + 4)
                    i = 48 * l + 24 * f + 8
                    stt(gs[:, :], mod[:, i:i + 8], 1.0, gain, ALU.add, ALU.mult).then_inc(s("gs"), 1)
                    dve.wait_ge(s("gs"), n + 1)
                    gain = gs[:, :]
                rms(f"ms{n}")
                dve.wait_ge(s("rstd"), n + 1)
                dst = x if n == 4 else h
                for k in range(KT):
                    stt(dst[:, k, :], x[:, k, :], gain[:, k:k + 1], rs[:, 0:T], ALU.mult, ALU.mult).then_inc(s("hn"), 1)

            def residual(r, name, gate):
                for p in range(4):
                    job_wait(dve, f"{name}.{p}")
                    for i in range(2):
                        m = 2 * p + i
                        xs = x[:, m, :]
                        if gate is None:
                            o = yt3[:, m, :] if r == 5 else xs
                            tt(o, ps2(f"{name}.{p}")[:, i, :], xs, ALU.add).then_inc(s("xres"), 1)
                        else:
                            stt(xs, ps2(f"{name}.{p}")[:, i, :], mod[:, gate + m:gate + m + 1], xs, ALU.mult, ALU.add)\
                                .then_inc(s("xres"), 1)

            for k in range(4):
                ada_acc(k)
                if k:
                    ada_mod(k - 1)
            ada_mod(3)
            dve.wait_ge(s("cols_in"), 16)
            norm(0)
            for k in range(4, 9):
                ada_acc(k)
                if k > 4:
                    ada_mod(k - 1)
            ada_mod(8)
            dve.wait_ge(s("pool_const"), 6)
            for j in range(2):
                dve.wait_ge(s("agsig"), j + 1)
                tt(a_pad[:, 2 * j:2 * j + 2, 15:15 + T], ps2(f"av{j}"), a_sig[:, 2 * j:2 * j + 2, :], ALU.mult).then_inc(s("amul"), 1)
            for tap in range(TAPS):
                for i in range(4):
                    n = 4 * tap + i
                    w = col("conv_w", TAPS * i + tap)
                    src = a_pad[:, i, tap:tap + T]
                    if tap == 0:
                        dve.wait_ge(s("amul"), i // 2 + 1)
                        ts(conv[:, i, :], src, w, col("conv_b", i), ALU.mult, ALU.add).then_inc(s("conv"), 1)
                    else:
                        dve.wait_ge(s("conv"), n - 3)
                        stt(conv[:, i, :], src, w, conv[:, i, :], ALU.mult, ALU.add).then_inc(s("conv"), 1)
            job_wait(dve, "mu")
            for j in range(2):
                dve.wait_ge(s("conv"), 4 * TAPS)
                c2 = conv[:, 2 * j:2 * j + 2, :]
                tt(c2, c2, ps("mu")[:, 0:T].unsqueeze(1).broadcast_to([P, 2, T]), ALU.subtract).then_inc(s("lnxc"), 1)
            dve.wait_ge(s("const_in"), 64)
            for j in range(4):
                qq = qk[:, 2 * j:2 * j + 2, :]
                ta, tbb = tmp3[:, 0:2, :], tmp3[:, 2:4, :]
                job_wait(dve, f"rot{j}")
                if j:
                    dve.wait_ge(s("rope"), 3 * j)
                tt(ta, qq, cos_t.unsqueeze(1).broadcast_to([P, 2, T]), ALU.mult).then_inc(s("rope"), 1)
                tt(tbb, ps2(f"rot{j}"), sin_t.unsqueeze(1).broadcast_to([P, 2, T]), ALU.mult).then_inc(s("rope"), 1)
                dve.wait_ge(s("rope"), 3 * j + 2)
                tt(qq, ta, tbb, ALU.add).then_inc(s("rope"), 1)
            rms("var", sem="lnrs")
            dve.wait_ge(s("lnrs"), 1)
            dve.wait_ge(s("lnxc"), 2)
            for i in range(4):
                stt(conv[:, i, :], conv[:, i, :], col("cln_g", i), rs[:, 0:T], ALU.mult, ALU.mult).then_inc(s("lny"), 1)
            ada_acc(9)
            for hd in range(4):
                job_wait(dve, f"sc{hd}")
                tt(sd[:, hd], ps2(f"sc{hd}"), dtab[:, hd], ALU.mult).then_inc(s("sd"), 1)
            ada_mod(9)
            for j in range(2):
                rms(f"rr{j}", 512, "rrs")
                dve.wait_ge(s("rrs"), j + 1)
                dst = qk[:, 2 * j:2 * j + 2, :]
                tt(dst, ps2(f"ro{j}"), rs[:, :].rearrange("p (k t) -> p k t", k=2), ALU.mult).then_inc(s("rn"), 1)
                dve.wait_ge(s("rn"), j + 1)
                dve.wait_ge(s("gsilu"), j + 1)
                tt(yt3[:, 4 + 2 * j:6 + 2 * j, :], dst, g_silu[:, 2 * j:2 * j + 2, :], ALU.mult).then_inc(s("ry"), 1)
            dve.wait_ge(s("mod"), 6)
            residual(0, "wo0", 16)
            norm(1)

            def ffn(l, after):
                for j in range(16):
                    dve.wait_ge(s("relu"), 16 * l + j + 1)
                    hh = big3[:, 2 * j:2 * j + 2, :]
                    tt(hh, hh, hh, ALU.mult).then_inc(s("fsq"), 1)
                    after(j)
                dve.wait_ge(s("mod"), ADA * (l + 1))
                residual(1 + 2 * l, f"f2.{l}", 48 * l + 40)

            def more_ada(j):
                if j < 14:
                    ada_acc(10 + j)
                if j >= 1 and j < 15:
                    ada_mod(9 + j)

            ffn(0, more_ada)
            norm(2)
            for n in range(66):
                k, q, d = n // 8, n // 2 % 4, n % 2
                if n < 64:
                    tab = tabs[n % 4]
                    job_wait(dve, f"bu{n}")
                    dve.wait_ge(s(f"tab{n % 4}"), 16 * (n // 4 + 1))
                    if n >= 2:
                        dve.wait_ge(s("s5w"), 2 * n - 2)
                    for f in range(2):
                        tt(pbuf[n % 2][:, f], ps2(f"bu{n}"), tab[:, f, :].unsqueeze(1).broadcast_to([P, 2, T]), ALU.mult).then_inc(s("s5p"), 1)
                if 1 <= n <= 64:
                    m = n - 1
                    mk, mq_, md = m // 8, m // 2 % 4, m % 2
                    tab = tabs[m % 4]
                    at = 32 * md + 4 * mk + mq_
                    dve.wait_ge(s("s5w"), 2 * m + 2)
                    for r in range(2):
                        dve.tensor_tensor_scan(gbuf[m % 2][:, r, :], mag[:, at:at + 1].broadcast_to([P, T]), wbuf[m % 2][:, r, :],
                                               0.0, ALU.mult, ALU.add).then_inc(s("s5g"), 1)
                    dve.wait_ge(s("s5g"), 2 * m + 2)
                    if m >= 2:
                        dve.wait_ge(s("s5h"), 2 * m - 2)
                    for f in range(2):
                        tt(qbuf[m % 2][:, f], gbuf[m % 2], tab[:, f, :].unsqueeze(1).broadcast_to([P, 2, T]), ALU.mult).then_inc(s("s5q"), 1)
                if n >= 9 and (n - 9) % 8 == 0:
                    kk = (n - 9) // 8
                    dve.wait_ge(s("s5y"), 8 * kk + 8)
                    stt(yt3[:, kk, :], h[:, kk, :], col("s5_d", kk), bank[6 + kk % 2][:, 0:T], ALU.mult, ALU.add).then_inc(s("s5z"), 1)
                if n == 11:
                    rms("mms", sem="mrs")
                    dve.wait_ge(s("mrs"), 1)
                    for kk in range(KT):
                        stt(mem_x[:, kk, :], mem_x[:, kk, :], col("g_mem", kk), rs[:, 0:T], ALU.mult, ALU.mult).then_inc(s("memn"), 1)
                if n in (20, 28):
                    j = (n - 20) // 8
                    rms(f"mkr{j}", 512, "mkrs")
                    dve.wait_ge(s("mkrs"), j + 1)
                    stt(mk_n[:, 2 * j:2 * j + 2, :].rearrange("p k t -> p (k t)"), ps(f"mk{j}")[:, :], col("g_mk"), rs[:, :],
                        ALU.mult, ALU.mult).then_inc(s("mkn"), 1)
            dve.wait_ge(s("mod"), ADA + 6)
            for p in range(4):
                dve.wait_ge(s("glus"), p + 1)
                g2 = tmp3[:, 2 * p:2 * p + 2, :]
                tt(g2, ps2(f"ga{p}"), g2, ALU.mult).then_inc(s("glut"), 1)
                dve.wait_ge(s("glut"), p + 1)
                for i in range(2):
                    m = 2 * p + i
                    stt(x[:, m, :], tmp3[:, m, :], mod[:, 48 + 16 + m:48 + 17 + m], x[:, m, :], ALU.mult, ALU.add).then_inc(s("xres"), 1)
            norm(3)
            ffn(1, lambda j: None)
            norm(4)
            norm(5)
            dve.memset(tmp[:, 0:1024], 0.0).then_inc(s("atz"), 1)
            ts(gsc[:, 0:1], col("g_fq"), float(128 ** -0.5), None, ALU.mult).then_inc(s("gqs"), 1)
            ts(gsc[:, 1:2], col("g_mq"), float(128 ** -0.5), None, ALU.mult).then_inc(s("gqs"), 1)
            dve.memset(fb, 1.0).then_inc(s("fb"), 1)
            job_wait(dve, "ff")
            ts(ff_x, ps("ff")[0:64, 0:T], cols[0:64, COLS["b_fox"]:COLS["b_fox"] + 1], None, ALU.add).then_inc(s("ffx"), 1)
            dve.wait_ge(s("ffx"), 1)
            stt(ff_c, ff_x, -1.0, ff_x, ALU.mult, ALU.max).then_inc(s("ffa"), 1)
            job_wait(dve, "la")
            for i in range(2):
                ts(la_x[:, T * i:T * i + T], ps2("la")[:, i, :], col("b_gla", i), None, ALU.add).then_inc(s("lax"), 1)
            dve.wait_ge(s("lax"), 2)
            stt(la_c, la_x, -1.0, la_x, ALU.mult, ALU.max).then_inc(s("lab"), 1)
            dve.wait_ge(s("ffe"), 2)
            stt(ff_x, ff_x, 0.0, ff_c, ALU.min, ALU.subtract).then_inc(s("ffl"), 1)
            dve.wait_ge(s("ffl"), 1)
            dve.wait_ge(s("fb"), 1)
            dve.tensor_tensor_scan(ff_c, fb, ff_x, 0.0, ALU.mult, ALU.add).then_inc(s("ffs"), 1)
            dve.wait_ge(s("ffs"), 1)
            ts(early[32:64, 896:1152], tmp[32:64, 1792:2048], -1.0, None, ALU.mult).then_inc(s("fb"), 1)
            dve.wait_ge(s("lae"), 2)
            stt(la_x, la_x, 0.0, la_c, ALU.min, ALU.subtract).then_inc(s("las"), 1)
            dve.wait_ge(s("las"), 1)
            for i in range(2):
                dve.tensor_tensor_scan(la_c[:, T * i:T * i + T], scanmask[:, :], la_x[:, T * i:T * i + T], 0.0,
                                       ALU.mult, ALU.add).then_inc(s("lac"), 1)
            dve.wait_ge(s("lac"), 2)
            c8 = la_c.rearrange("p (c t) -> p c t", t=CHUNK)
            tt(e_out.rearrange("p (c t) -> p c t", t=CHUNK), c8[:, :, CHUNK - 1:CHUNK].broadcast_to([P, 8, CHUNK]), c8,
               ALU.subtract).then_inc(s("lad"), 1)
            dve.wait_ge(s("gqk"), 2)
            dve.wait_ge(s("lax_e"), 2)
            stt(gq_s, gq_s, float(DK ** -0.5), e_pos, ALU.mult, ALU.mult).then_inc(s("gin"), 1)
            tt(k_in, gk_s, e_neg, ALU.mult).then_inc(s("gin"), 1)
            dve.wait_ge(s("lax_e"), 3)
            tt(gk_s, gk_s, e_out, ALU.mult).then_inc(s("gin"), 1)

            def head_norm(i, name, gain, dst):
                if i:
                    dve.wait_ge(s("nq"), i)
                rms(f"nr{i}", 512, "nrs")
                dve.wait_ge(s("nrs"), i + 1)
                stt(dst.rearrange("p k t -> p (k t)"), ps(name)[:, :], gain, rs[:, :], ALU.mult, ALU.mult).then_inc(s("nq"), 1)

            job_wait(dve, "cs1")
            cs0 = ps("cs0")[:, :].rearrange("p (c m v) -> p c m v", c=2, m=2)
            cs1 = ps("cs1")[:, 0:256].rearrange("p (m v) -> p m v", m=2)
            dve.tensor_copy(state[:, 0], cs0[:, 0]).then_inc(s("gst"), 1)
            for c in (1, 2):
                dve.wait_ge(s("gst"), 2 * c - 1)
                for m in range(2):
                    at = T * m + CHUNK * c + CHUNK - 1
                    stt(state[:, c, m], state[:, c - 1, m], e_pos[:, at:at + 1], cs1[:, m] if c == 1 else cs0[:, 1, m],
                        ALU.mult, ALU.add).then_inc(s("gst"), 1)
            dve.wait_ge(s("gqs"), 2)
            for j in range(2):
                head_norm(j, f"fq{j}", gsc[:, 0:1], fq_n[:, 2 * j:2 * j + 2, :])
            dve.wait_ge(s("late"), 80)
            dve.wait_ge(s("atz"), 1)
            for i in range(2):
                job_wait(dve, f"at{i}")
                dve.copy_predicated(att[:, 4 * i:4 * i + 4, :], glamask.unsqueeze(1).broadcast_to([P, 4, P]),
                                    ps(f"at{i}")[:, :].rearrange("p (k t) -> p k t", k=4)).then_inc(s("atc"), 1)

            def gla_out(j):
                rms(f"gor{j}", 512, "gors")
                dve.wait_ge(s("gors"), j + 1)
                for i in range(2):
                    hd = j + 2 * i
                    stt(go_n[:, hd, :], ps2(f"go{j}")[:, i, :], col("g_gla", hd), rs[:, T * i:T * i + T], ALU.mult, ALU.mult).then_inc(s("gon"), 1)
                dve.wait_ge(s("gon"), 2 * j + 2)
                dve.wait_ge(s("ggs"), 2)
                tt(ys[0][:, j::2, :], go_n[:, j::2, :], gg_s[:, j::2, :], ALU.mult).then_inc(s("ygla"), 1)

            gla_out(0)
            for j in range(2):
                head_norm(2 + j, f"fk{j}", col("g_fk"), fk_n[:, 2 * j:2 * j + 2, :])
            gla_out(1)

            def fox_rows(hd):
                if hd >= 2:
                    job_wait(dve, f"us{hd - 2}")
                ts(fa[hd % 2][0:32, :], tmp[0:32, 1792:2048], ident[0:32, hd:hd + 1], None, ALU.mult).then_inc(s("fa"), 1)
                ts(fa[hd % 2][32:64, :], scan_ones, ident[32:64, 32 + hd:33 + hd], None, ALU.mult).then_inc(s("fa"), 1)

            scan_ones = tmp[32:64, 1536:1792]
            dve.memset(scan_ones, 1.0).then_inc(s("pick1"), 1)
            dve.wait_ge(s("pick1"), 1)
            fox_rows(0)
            for u in range(9):
                if u < 8:
                    if u + 1 < 4:
                        fox_rows(u + 1)
                    job_wait(dve, f"us{u}")
                    if u >= 1:
                        dve.wait_ge(s("ue"), 2 * u)
                    if u < 4:
                        tt(logits, ps2(f"us{u}"), foxmask, ALU.add).then_inc(s("ul"), 1)
                    else:
                        dve.tensor_copy(logits, ps2(f"us{u}")).then_inc(s("ul"), 1)
                    dve.wait_ge(s("ul"), u + 1)
                    dve.tensor_reduce(small[:, 0:2], logits, AX_X, ALU.max).then_inc(s("umx"), 1)
                    dve.wait_ge(s("umx"), u + 1)
                    ts(small[:, 2:4], small[:, 0:2], -1.0, None, ALU.mult).then_inc(s("unm"), 1)
                    dve.wait_ge(s("ue"), 2 * u + 2)
                    dve.reciprocal(small[:, 6:8], small[:, 4:6]).then_inc(s("urc"), 1)
                    dve.wait_ge(s("urc"), u + 1)
                    for i in range(2):
                        ts(probs[u % 2][:, i, :], probs[u % 2][:, i, :], small[:, 6 + i:7 + i], None, ALU.mult).then_inc(s("up"), 1)
                if u == 0:
                    for j in range(2):
                        head_norm(4 + j, f"mq{j}", gsc[:, 1:2], mq_n[:, 2 * j:2 * j + 2, :])
            for n in range(12):
                i, p = divmod(n, 4)
                job_wait(dve, f"br{i}.{p}")
                m = KT * i + 2 * p
                dve.wait_ge(s("gate"), m + 2)
                if i == 2:
                    dve.wait_ge(s("mga"), p + 1)
                dst = (yt3 if i == 0 else tmp3)[:, 2 * p:2 * p + 2, :]
                tt(dst, ps2(f"br{i}.{p}"), gates[:, m:m + 2, :], ALU.mult).then_inc(s("mgm"), 1)
            residual(4, "w2o", None)
            norm(6)
            for p in range(6):
                for i in range(2 * p, min(2 * p + 2, 11)):
                    dve.wait_ge(s("fsil"), i + 1)
                    job_wait(dve, f"fu{i}")
                    tt(big[:, 512 * i:512 * i + 512], ps(f"fu{i}")[:, :], tmp[:, 512 * (i % 4):512 * (i % 4) + 512], ALU.mult).then_inc(s("fact"), 1)
            residual(5, "fd", None)

        @block.tensor
        def _(pe):
            at = [0]

            def begin(name):
                i = INDEX[name]
                assert at[0] == i, (name, JOBS[at[0]])
                at[0] += 1
                if name not in TURN:
                    if int(name[3:]) >= 2:
                        pe.wait_ge(s("mod"), int(name[3:]) - 1)
                elif TURN[name] >= BANKS:
                    sem, n = freed[ROTATING[TURN[name] - BANKS]]
                    pe.wait_ge(s(sem), n)

            def end(mm):
                mm.then_inc(s("job"), 1)

            def panel(name):
                i = place[name]
                pe.wait_ge(s(f"panel{i % RING}"), 16 * (i // RING + 1))
                return panel_view(name)

            def mm(*args, **kw):
                return pe.matmul(*args, skip_group_check=True, **kw)

            def project(name, w, m0, src, ready, tiles=2):
                begin(name)
                for i in range(tiles):
                    c = (m0 + i) * P
                    for k in range(KT):
                        ready(k)
                        last = mm(ps2(name)[:, i, :], w[:, k, c:c + P], src[:, k, :], start=(k == 0), stop=(k == KT - 1))
                end(last)

            def project_nat(name, w, i, src):
                begin(name)
                for k in range(KT):
                    last = mm(ps(name)[:, :], src[:, k, P * i:P * i + P], w[:, k, :], start=(k == 0), stop=(k == KT - 1))
                end(last)

            def rows_job(names, panel_name, blocks, src, ready):
                for name in names:
                    begin(name)
                kt = 0
                for b in range(blocks):
                    w = panel(f"{panel_name}{b}")
                    nk = w.shape[1]
                    for m in range(KT):
                        for k in range(nk):
                            ready(kt + k)
                            last = mm(ps2(names[m // 2])[:, m % 2, :], w[:, k, P * m:P * m + P], src[:, kt + k, :],
                                      start=(kt + k == 0 and m % 2 == 0), stop=(b == blocks - 1 and k == nk - 1))
                        if b == blocks - 1 and m % 2 == 1:
                            end(last)
                    if b < blocks - 1:
                        last.then_inc(s("row_panel"), 1)
                    kt += nk

            def ada(k):
                begin(f"ada{k}")
                pe.wait_ge(s("ada_acc"), k + 1)
                for i in range(4):
                    last = mm(ps(f"ada{k}")[:, i:i + 1], accb[:, 512 * (k % 2) + P * i:512 * (k % 2) + P * i + P], one[:, :], start=(i == 0), stop=(i == 3))
                end(last)

            def mean_squares(n):
                begin(f"ms{n}")
                for k in range(KT):
                    pe.wait_ge(s("sq"), 4 * n + k // 2 + 1)
                    last = mm(ps(f"ms{n}")[:, 0:T], inv1024, sq3[:, k, :], start=(k == 0), stop=(k == KT - 1))
                end(last)

            def mean(name, m, src, width=512):
                begin(name)
                end(mm(ps(name)[:, 0:width], m, src, start=True, stop=True))

            def h_ready(n):
                if n < 4:
                    return lambda k: pe.wait_ge(s("h"), 8 * n + k + 1)
                return lambda k: pe.wait_ge(s("hn"), 8 * n + k + 1)

            def no_wait(k):
                return None

            pe.wait_ge(s("pool_const"), 6)
            for k in range(4):
                ada(k)
            mean_squares(0)
            w = panel("av")
            project("av0", w, 0, h, h_ready(0))
            ada(4)
            project("av1", w, 2, h, no_wait)
            ada(5)
            w = panel("ag")
            project("ag0", w, 0, h, no_wait)
            ada(6)
            project("ag1", w, 2, h, no_wait)
            ada(7)
            w = panel("q")
            project("q0", w, 0, h, no_wait)
            ada(8)
            project("q1", w, 2, h, no_wait)
            w = panel("k")
            project("k0", w, 0, h, no_wait)
            project("k1", w, 2, h, no_wait)
            w = panel("v")
            project_nat("v0", w, 0, h)
            project_nat("v1", w, 1, h)
            begin("mu")
            for i in range(4):
                pe.wait_ge(s("conv"), 4 * (TAPS - 1) + i + 1)
                last = mm(ps("mu")[:, 0:T], inv512, conv[:, i, :], start=(i == 0), stop=(i == 3))
            end(last)
            pe.wait_ge(s("const_in"), 64)
            for j in range(4):
                pe.wait_ge(s("qkc"), j + 1)
                mean(f"rot{j}", perm, qk[:, 2 * j:2 * j + 2, :].rearrange("p k t -> p (k t)"))
            w = panel("g")
            project("g0", w, 0, h, no_wait)
            begin("var")
            for i in range(4):
                pe.wait_ge(s("lnsq"), i // 2 + 1)
                last = mm(ps("var")[:, 0:T], inv512, sq3[:, i, :], start=(i == 0), stop=(i == 3))
            end(last)
            project("g1", w, 2, h, no_wait)
            for hd in range(4):
                begin(f"sc{hd}")
                pe.wait_ge(s("rope"), 12)
                for i in range(2):
                    last = mm(ps2(f"sc{hd}")[:, i, :], qk[:, 4 + hd, P * i:P * i + P], qk[:, hd, :], start=True, stop=True)
                end(last)
            ada(9)
            pe.wait_ge(s("vc"), 2)
            for j in range(2):
                begin(f"ro{j}")
                for i in range(2):
                    hd = 2 * j + i
                    pe.wait_ge(s("sd"), hd + 1)
                    for t in range(2):
                        last = mm(ps2(f"ro{j}")[:, i, :], v_nat[:, t, P * hd:P * hd + P], sd[:, hd, t, :], start=(t == 0), stop=(t == 1))
                end(last)
                pe.wait_ge(s("rsq"), j + 1)
                mean(f"rr{j}", inv128, sq[:, 1024 + 512 * j:1536 + 512 * j])

            def cat_ready(k):
                pe.wait_ge(s("yconv") if k < 4 else s("ry"), k + 1 if k < 4 else (k - 4) // 2 + 1)

            for i in range(2):
                w = panel(f"wo{i}")
                for j in range(2):
                    project(f"wo0.{2 * i + j}", w, 2 * j, yt3, cat_ready)
            mean_squares(1)

            def ffn(l, after):
                for i in range(8):
                    w = panel(f"f1.{l}.{i}")
                    for j in range(2):
                        project(f"f1.{l}.{2 * i + j}", w, 2 * j, h, h_ready(1 + 2 * l) if i == 0 and j == 0 else no_wait)
                        after(2 * i + j)
                rows_job([f"f2.{l}.{p}" for p in range(4)], f"f2.{l}.", 8, big3, lambda k: pe.wait_ge(s("fsq"), 16 * l + k // 2 + 1))

            ffn(0, lambda j: ada(8 + j) if j >= 2 else None)
            mean_squares(2)
            def memory(n):
                if n == 8:
                    begin("mms")
                    for k in range(KT):
                        pe.wait_ge(s("msq"), k // 2 + 1)
                        last = mm(ps("mms")[:, 0:T], inv1024, mem_sq[:, T * k:T * k + T], start=(k == 0), stop=(k == KT - 1))
                    end(last)
                if n in (16, 24):
                    project(f"mk{(n - 16) // 8}", panel("mk"), (n - 16) // 4, mem_x, lambda k: pe.wait_ge(s("memn"), k + 1))
                if n in (18, 26):
                    j = (n - 18) // 8
                    pe.wait_ge(s("mksq"), j + 1)
                    mean(f"mkr{j}", inv128, mem_sq[:, 512 * j:512 * j + 512])
                if n in (32, 40):
                    project_nat(f"mv{(n - 32) // 8}", panel("mv"), (n - 32) // 8, mem_x)

            pe.wait_ge(s("bc_in"), 48)
            for n in range(67):
                if n < 64:
                    k, q, d = n // 8, n // 2 % 4, n % 2
                    begin(f"bu{n}")
                    pe.wait_ge(s("ur") if d else s("h"), k + 1 if d else 16 + k + 1)
                    u = (u_rev if d else h)[32 * q:32 * q + 32, k, :]
                    for r in range(2):
                        last = mm(ps2(f"bu{n}")[:, r, :], b_w[32 * q:32 * q + 32, k, d, r, :], u, start=True, stop=True)
                    end(last)
                    memory(n)
                if n >= 3:
                    m = n - 3
                    k, q, d = m // 8, m // 2 % 4, m % 2
                    if m == 0:
                        pe.wait_ge(s("cw"), 12)
                    if k >= 2 and m % 8 == 0:
                        pe.wait_ge(s("s5z"), k - 1)
                    pe.wait_ge(s("s5h"), 2 * m + 2)
                    for r in range(2):
                        last = mm(bank[6 + k % 2][32 * q:32 * q + 32, 0:T], c_w[:, 32 * d + 4 * k + q, r, :], hbuf[m % 2][:, r, :],
                                  start=(d == 0 and r == 0), stop=(d == 1 and r == 1))
                    last.then_inc(s("s5y"), 1)
            for i in range(2):
                for t in "ab":
                    w = panel(f"g{t}{i}")
                    for j in range(2):
                        project(f"g{t}{2 * i + j}", w, 2 * j, yt3, (lambda k: pe.wait_ge(s("z"), k + 1)) if i == 0 else no_wait)
            mean_squares(3)
            ffn(1, lambda j: None)
            mean_squares(4)
            mean_squares(5)
            w = panel("gqk")
            project("gq0", w, 0, h, h_ready(5))
            project("gk0", w, 2, h, no_wait)
            pe.wait_ge(s("late"), 80)
            for name, c0, m in (("ga1r", 64, 16), ("ff", 0, 64)):
                begin(name)
                for k in range(KT):
                    last = mm(ps(name)[0:m, 0:T], wsm[:, k, c0:c0 + m], h[:, k, :], start=(k == 0), stop=(k == KT - 1))
                end(last)
            w = panel("gv")
            project_nat("gv0", w, 0, h)
            project_nat("gv1", w, 1, h)
            begin("la")
            pe.wait_ge(s("ga1c"), 1)
            for i in range(2):
                last = mm(ps2("la")[:, i, :], wa2[:, P * i:P * i + P], ga1_s, start=True, stop=True)
            end(last)
            for name, w_name in (("gg", "gg"), ("fq", "fq")):
                w = panel(w_name)
                for j in range(2):
                    project(f"{name}{j}", w, 2 * j, h, no_wait)
            begin("kot")
            pe.wait_ge(s("gin"), 3)
            for t in range(2):
                for m in range(2):
                    last = pe.transpose(ps("kot")[:, 256 * t + P * m:256 * t + P * m + P], gk_s[:, T * m + P * t:T * m + P * t + P], ident[:, :])
            end(last)
            pe.wait_ge(s("koc"), 1)
            pe.wait_ge(s("gvc"), 2)
            for name, chunks in (("cs0", (0, 2)), ("cs1", (1,))):
                begin(name)
                for c in chunks:
                    r0 = CHUNK * (c % 2)
                    for hd in range(4):
                        m, p0 = hd // 2, DK * (hd % 2)
                        o = 256 * (c // 2) + P * m
                        last = mm(ps(name)[p0:p0 + DK, o:o + P], ko_nat[r0:r0 + CHUNK, 256 * (c // 2) + DK * hd:256 * (c // 2) + DK * hd + DK],
                                  gv_nat[r0:r0 + CHUNK, c // 2, P * hd:P * hd + P], start=True, stop=True)
                end(last)

            def head_mean(i):
                pe.wait_ge(s("nsq"), i + 1)
                mean(f"nr{i}", inv128, sq[:, 512 * (i % 2):512 * (i % 2) + 512])

            head_mean(0)
            head_mean(1)
            for odd in range(2):
                begin(f"at{odd}")
                for t in range(2):
                    for m in range(2):
                        c = slice(T * m + P * t, T * m + P * t + P)
                        last = mm(ps(f"at{odd}")[:, 256 * t + P * m:256 * t + P * m + P], k_in[DK * odd:DK * odd + DK, c],
                                  gq_s[DK * odd:DK * odd + DK, c], start=True, stop=True)
                end(last)
            w = panel("fk")
            for j in range(2):
                project(f"fk{j}", w, 2 * j, h, no_wait)

            def gla_out(j):
                begin(f"go{j}")
                pe.wait_ge(s("atc"), 2)
                pe.wait_ge(s("gst"), 5)
                for i in range(2):
                    hd = j + 2 * i
                    m, p0 = i, DK * j
                    for t in range(2):
                        mm(ps2(f"go{j}")[:, i, P * t:P * t + P], gv_nat[:, t, P * hd:P * hd + P], att[:, 4 * j + 2 * t + i, :],
                           start=(i == 0 and t == 0), stop=False)
                    for c in range(1, 4):
                        last = mm(ps2(f"go{j}")[:, i, CHUNK * c:CHUNK * c + CHUNK], state[p0:p0 + DK, c - 1, m, :],
                                  gq_s[p0:p0 + DK, T * m + CHUNK * c:T * m + CHUNK * c + CHUNK], start=False, stop=(c == 3))
                end(last)
                pe.wait_ge(s("gosq"), j + 1)
                mean(f"gor{j}", inv128, go_sq[:, 512 * j:512 * j + 512])

            gla_out(0)
            head_mean(2)
            head_mean(3)
            gla_out(1)
            w = panel("fv")
            project_nat("fv0", w, 0, h)
            project_nat("fv1", w, 1, h)
            w = panel("mq")
            for j in range(2):
                project(f"mq{j}", w, 2 * j, h, no_wait)

            def gate(j):
                project(f"bg{j}", panel(f"bg{j // 2}"), 2 * (j % 2), h, no_wait)

            for u in range(10):
                if u < 8:
                    begin(f"us{u}")
                    if u < 4:
                        pe.wait_ge(s("nq"), 4)
                        pe.wait_ge(s("fa"), 2 * u + 2)
                        pe.wait_ge(s("fb"), 2)
                    else:
                        pe.wait_ge(s("nq"), 6)
                        pe.wait_ge(s("mkn"), 2)
                    for t in range(2):
                        o = ps2(f"us{u}")[:, t, :]
                        if u < 4:
                            mm(o, fq_n[:, u, P * t:P * t + P], fk_n[:, u, :], start=True, stop=False)
                            last = mm(o, fa[u % 2][:, P * t:P * t + P], fb, start=False, stop=True)
                        else:
                            last = mm(o, mq_n[:, u - 4, P * t:P * t + P], mk_n[:, u - 4, :], start=True, stop=True)
                    end(last)
                gate(u)
                if u == 0:
                    head_mean(4)
                    head_mean(5)
                if 1 <= u <= 8:
                    m = u - 1
                    begin(f"ut{m}")
                    pe.wait_ge(s("up"), 2 * m + 2)
                    for ks in range(2):
                        for t in range(2):
                            last = pe.transpose(ps(f"ut{m}")[:, 256 * ks + P * t:256 * ks + P * t + P], probs[m % 2][:, t, P * ks:P * ks + P], ident[:, :])
                    end(last)
                if u >= 3 and u % 2 == 1:
                    j = (u - 3) // 2
                    begin(f"uo{j}")
                    v = fv_nat if j < 2 else mv_nat
                    pe.wait_ge(s("fvc") if j < 2 else s("mvc"), 2)
                    for i in range(2):
                        m = 2 * j + i
                        hd = m % 4
                        pe.wait_ge(s("upt"), m + 1)
                        for ks in range(2):
                            last = mm(ps2(f"uo{j}")[:, i, :], v[:, ks, P * hd:P * hd + P], prob_t[m % 2][:, ks, :], start=(ks == 0), stop=(ks == 1))
                    end(last)
            gate(10)
            gate(11)
            for i in range(3):
                pe.wait_ge(s("ygla") if i == 0 else s("uoc"), (2, 2, 4)[i])
                w = panel(f"br{i}.0")
                for p in range(4):
                    begin(f"br{i}.{p}")
                    for j in range(2):
                        m = 2 * p + j
                        for k in range(4):
                            last = mm(ps2(f"br{i}.{p}")[:, j, :], w[:, k, P * m:P * m + P], ys[i][:, k, :], start=(k == 0), stop=(k == 3))
                    end(last)
            for i in range(2):
                w = panel(f"w2o{i}")
                for j in range(2):
                    project(f"w2o.{2 * i + j}", w, 2 * j, yt3, lambda k: pe.wait_ge(s("mga"), 4 + k // 2 + 1))
            mean_squares(6)
            for p in range(6):
                n = 2 if p < 5 else 1
                for t in "gu":
                    w = panel(f"f{t}{p}")
                    for i in range(n):
                        project(f"f{t}{2 * p + i}", w, 2 * i, h, h_ready(6) if p == 0 and t == "g" and i == 0 else no_wait)
            rows_job([f"fd.{p}" for p in range(4)], "fd", 6, big3, lambda k: pe.wait_ge(s("fact"), k // 2 + 1))
            assert at[0] == len(JOBS)


def shape_constants():
    f = np.float32
    inv = (np.float64(10000.0) ** (-np.arange(0, P, 2) / P)).astype(f)
    ang = (np.arange(T, dtype=f)[:, None] * inv[None, :]).astype(f)
    cos, sin = np.cos(ang).astype(f).T, np.sin(ang).astype(f).T
    perm = np.zeros((P, P), f)
    half = P // 2
    perm[np.arange(half) + half, np.arange(half)] = -1.0
    perm[np.arange(half), np.arange(half) + half] = 1.0
    rope = np.concatenate([np.concatenate([cos, cos]), np.concatenate([sin, sin]), perm], 1)
    log_g = np.log1p(-np.exp2(-5.0 - np.arange(HEADS)))
    m = np.arange(T).reshape(2, P)
    dist = np.abs(m[:, :, None] - np.arange(T)[None, None, :])
    decay = np.exp(log_g[:, None, None, None] * dist[None]) * P ** -0.5
    decay = decay.transpose(2, 0, 1, 3).reshape(P, -1)
    q = np.arange(T).reshape(2, P)
    fox = np.where(np.arange(T)[None, None, :] <= q[:, :, None], 0.0, NEG).transpose(1, 0, 2).reshape(P, -1)
    i = np.arange(P)
    gla = (i[:, None] <= i[None, :]) & (i[:, None] // CHUNK == i[None, :] // CHUNK)
    scan = np.broadcast_to((np.arange(T) % CHUNK != 0), (P, T))
    return {"rope": rope.astype(f), "decay": decay.astype(f), "foxmask": fox.astype(f), "glamask": gla.astype(np.int32),
            "scanmask": scan.astype(f), "ident": np.eye(P, dtype=f)}


def kernel(**inp):
    import concourse.bacc as bacc
    from concourse.bass_utils import run_bass_kernel_spmd as run

    inp = {k: np.asarray(v) for k, v in inp.items()}

    def cols_of(v):
        return np.reshape(v, (-1, P)).T

    b_fox = np.zeros((P, 1), np.float32)
    b_fox[0:HEADS, 0] = inp["b_fox_f_2"][0]
    b_fox[32:32 + HEADS, 0] = inp["b_fox_f_2"][0]
    pack = {
        "c": cols_of(inp["c"]), "norm_g": cols_of(inp["norm_g"]), "ada_b": cols_of(inp["ada_b"]),
        "conv_w": inp["conv_w"][0].reshape(TAPS, 4, P).transpose(2, 1, 0).reshape(P, -1), "conv_b": cols_of(inp["conv_b"]),
        "cln_g": cols_of(inp["cln_g"]), "cln_b": cols_of(inp["cln_b"]), "s5_d": cols_of(inp["s5_d"]),
        "norm_f": cols_of(inp["norm_f"]), "g_mix": cols_of(inp["g_mix_2"]), "b_gla": cols_of(inp["b_gla_a_2"]),
        "g_gla": cols_of(inp["g_gla_out_2"]), "g_fq": cols_of(inp["g_fox_q_2"]), "g_fk": cols_of(inp["g_fox_k_2"]),
        "g_mem": cols_of(inp["g_mem_2"]), "g_mq": cols_of(inp["g_mem_q_2"]), "g_mk": cols_of(inp["g_mem_k_2"]),
        "b_gate": cols_of(inp["b_gate_2"]), "g_ffn": cols_of(inp["g_ffn_2"]), "b_fox": b_fox,
    }
    cols = np.concatenate([pack[name] for name in COLS], 1)

    def states(v):
        return v.reshape(2, 32, 2, 64).transpose(2, 3, 0, 1).reshape(P, 64)

    step = np.repeat(inp["s5_log_step"][0][:, :, None], 64, 2)
    scal = np.concatenate([states(inp["s5_lam_re"][0]), states(inp["s5_lam_im"][0]), states(step)], 1)
    bw = np.zeros((4, 2, 16, 8, 2, 2, 2, 64), np.float32)
    cw = np.zeros((2, 64, 2, 2, 32, 2, 16), np.float32)
    for r, (bn, cn) in enumerate((("s5_b_re", "s5_c_re"), ("s5_b_im", "s5_c_im"))):
        b = inp[bn][0].reshape(2, 8, 4, 2, 64, 16)
        c = inp[cn][0].reshape(2, 32, 2, 16, 64)
        for g in range(2):
            bw[:, g, :, :, :, r, g, :] = b[:, :, :, g].transpose(2, 4, 1, 0, 3)
            cw[g, :, r, :, :, g, :] = c[:, :, g].transpose(3, 0, 1, 2)
    w_fox = np.zeros((D, 64), np.float32)
    w_fox[:, 0:HEADS] = inp["w_in_2"][0][:, FFG:FFG + HEADS]
    w_fox[:, 32:32 + HEADS] = inp["w_in_2"][0][:, FFG:FFG + HEADS]
    arrays = {
        "x": inp["x"][0].T, "mem": inp["mem_2"][0].T, "cols": cols, "s5_scal": scal,
        "s5_b": bw.reshape(P, 4096), "s5_c": cw.reshape(P, 2, 2048), "w_fox_f": w_fox,
        "ada_w": inp["ada_w"], "w_in": inp["w_in"][0], "w_out": inp["w_out"][0], "w_fc1": inp["w_fc1"], "w_fc2": inp["w_fc2"],
        "w_glu_a": inp["w_glu_a"][0], "w_glu_b": inp["w_glu_b"][0], "w_in_2": inp["w_in_2"][0], "w_mem_kv": inp["w_mem_kv_2"][0],
        "w_gla_a2": inp["w_gla_a2_2"][0], "w_branch": inp["w_branch_2"][0], "w_out_2": inp["w_out_2"][0],
        "w_ffn_gate": inp["w_ffn_gate_2"][0], "w_ffn_up": inp["w_ffn_up_2"][0], "w_ffn_down": inp["w_ffn_down_2"][0],
    }
    arrays.update(shape_constants())
    arrays = {k: np.ascontiguousarray(v) for k, v in arrays.items()}
    nc = bacc.Bacc("TRN2", target_bir_lowering=False, num_devices=1)
    aps = {k: nc.dram_tensor(f"in_{k}", v.shape, mybir.dt.from_np(v.dtype), kind="ExternalInput").ap() for k, v in arrays.items()}
    out = nc.dram_tensor("out_t", (D, T), F32, kind="ExternalOutput").ap()
    build(nc, aps, out)
    r = run(nc, [{f"in_{k}": v for k, v in arrays.items()}], core_ids=[0])
    return np.ascontiguousarray(np.asarray(r.results[0]["out_t"]).T)[None]
```

```python
from contextlib import ExitStack

import numpy as np

import concourse.bass as bass
from concourse import mybir

F32 = mybir.dt.float32
I32 = mybir.dt.int32
F32R = mybir.dt.float32r
ALU = mybir.AluOpType
ACT = mybir.ActivationFunctionType
AX_X = mybir.AxisListType.X

P = 128
T = 256
D = 1024
KT = D // P
EPS = 1e-6
RING = 4
SLOT = 4096
FF1 = 4096
FF2 = 2816
TAPS = 31
HEADS = 4
DK = 64
CHUNK = 64
NEG = -3.0e38
TWO_PI_A = 6.28125
TWO_PI_B = float(np.float32(np.round((2 * np.pi - 6.28125) * 2.0 ** 21) / 2.0 ** 21))
TWO_PI_C = 2 * np.pi - TWO_PI_A - TWO_PI_B
ROUND = 12582912.0
ADA = 12
PI_SAFE = 3.1415925
SW_ADA = 10

COLS = {}
_at = 0
for _name, _n in (("c", 8), ("norm_g", 32), ("ada_b", 96), ("conv_w", 4 * TAPS), ("conv_b", 4), ("cln_g", 4),
                  ("cln_b", 4), ("s5_d", 8), ("norm_f", 8), ("g_mix", 8), ("b_gla", 2), ("g_gla", 4),
                  ("g_fq", 1), ("g_fk", 1), ("g_mem", 8), ("g_mq", 1), ("g_mk", 1), ("b_gate", 24),
                  ("g_ffn", 8), ("b_fox", 1)):
    COLS[_name] = _at
    _at += _n
NCOLS = _at
GQ, GV, GG, GA, FQ, FK, FV, FFG, MQ, BG = 0, 512, 1024, 1536, 1552, 2064, 2576, 3088, 3092, 3604


def job_order():
    jobs = [f"ada{k}" for k in range(4)] + ["ms0"]
    jobs += ["av0", "ada4", "av1", "ada5", "ag0", "ada6", "ag1", "ada7", "q0", "ada8", "q1", "k0", "k1",
             "v0", "v1", "g0", "g1", "mu", "rot0", "rot1", "rot2", "rot3", "var"]
    jobs += ["sc0", "sc1", "sc2", "sc3", "ada9", "ro0", "rr0", "ro1", "rr1"] + [f"wo0.{p}" for p in range(4)] + ["ms1"]
    for j in range(16):
        jobs.append(f"f1.0.{j}")
        if 2 <= j < 16:
            jobs.append(f"ada{8 + j}")
    jobs += [f"f2.0.{p}" for p in range(4)] + ["ms2"]
    fill = {8: "mms", 16: "mk0", 18: "mkr0", 24: "mk1", 26: "mkr1", 32: "mv0", 40: "mv1"}
    for n in range(64):
        jobs.append(f"bu{n}")
        if n in fill:
            jobs.append(fill[n])
    jobs += ["ga0", "ga1", "gb0", "gb1", "ga2", "ga3", "gb2", "gb3", "ms3"]
    jobs += [f"f1.1.{j}" for j in range(16)] + [f"f2.1.{p}" for p in range(4)] + ["ms4", "ms5"]
    jobs += ["gq0", "gk0", "ga1r", "ff", "gv0", "gv1", "la", "gg0", "gg1", "fq0", "fq1", "kot", "cs0", "cs1",
             "nr0", "nr1", "at0", "at1", "fk0", "fk1", "go0", "gor0", "nr2", "nr3", "go1", "gor1",
             "fv0", "fv1", "mq0", "mq1"]
    bg = 0
    for u in range(10):
        if u < 8:
            jobs.append(f"us{u}")
        jobs.append(f"bg{bg}")
        bg += 1
        if u == 0:
            jobs += ["nr4", "nr5"]
        if 1 <= u <= 8:
            jobs.append(f"ut{u - 1}")
        if u >= 3 and u % 2 == 1:
            jobs.append(f"uo{(u - 3) // 2}")
    jobs += ["bg10", "bg11"]
    jobs += [f"br{i}.{p}" for i in range(3) for p in range(4)] + [f"w2o.{p}" for p in range(4)] + ["ms6"]
    for p in range(6):
        n = 2 if p < 5 else 1
        jobs += [f"fg{2 * p + i}" for i in range(n)] + [f"fu{2 * p + i}" for i in range(n)]
    jobs += [f"fd.{p}" for p in range(4)]
    return jobs


JOBS = job_order()
INDEX = {name: i for i, name in enumerate(JOBS)}
ROOTS = ["ms0", "var", "rr0", "rr1", "ms1", "ms2", "mms", "mkr0", "mkr1", "ms3", "ms4", "ms5", "nr0", "nr1", "gor0",
         "nr2", "nr3", "gor1", "nr4", "nr5", "ms6"]
BANKS = 6
ROTATING = [name for name in JOBS if not name.startswith("ada")]
TURN = {name: i for i, name in enumerate(ROTATING)}


def build(nc, a, out):
    ctx = ExitStack()
    with ctx:
        def sb(name, free, dt=F32, parts=P):
            return ctx.enter_context(nc.sbuf_tensor(name, [parts, free], dt))

        sems = {}

        def s(name):
            if name not in sems:
                sems[name] = ctx.enter_context(nc.semaphore("s_" + name))
            return sems[name]

        shared = [(f"ring{i}", SLOT) for i in range(RING)] + [(f"ada_slot{i}", SLOT) for i in range(2)]
        shared += [("h_in", KT * T), ("squares", KT * T), ("tmp", KT * T), ("y_cat", KT * T), ("big", 32 * T),
                   ("decay_or_mem", 2048), ("tabw", 3072)]
        with ExitStack() as first:
            plain = {name: first.enter_context(nc.sbuf_tensor(name, [P, free], F32)) for name, free in shared}
        split = {name: sb(name + "_split", free, F32R) for name, free in shared}
        ring = [plain[f"ring{i}"] for i in range(RING)]
        adas = [plain[f"ada_slot{i}"] for i in range(2)]
        x = sb("x_res", KT * T)[:, :].rearrange("p (k t) -> p k t", k=KT)
        h = plain["h_in"][:, :].rearrange("p (k t) -> p k t", k=KT)
        sq, tmp, yt, big = plain["squares"], plain["tmp"], plain["y_cat"], plain["big"]
        dreg, tabw = plain["decay_or_mem"], plain["tabw"]
        accb = sb("ada_acc", 1024)
        rs = sb("rstd", 512)
        early = sb("early", 1984)
        scanmask = sb("scanmask", T)
        ident = sb("ident", P)
        inv = sb("inv", 3 * P)
        one = sb("one", 1)
        eps = sb("eps", 1)
        cols = sb("cols", NCOLS)
        mod = sb("mod", 96)
        gs = sb("gs", 8)
        cact = sb("cact", 8)
        gsc = sb("gsc", 2)
        small = sb("small", 8)
        bank = [ctx.enter_context(nc.psum_tensor(f"bank{i}", [P, 512], F32)) for i in range(8)]

        def col(name, i=0, n=1):
            return cols[:, COLS[name] + i:COLS[name] + i + n]

        inv1024, inv512, inv128 = (inv[:, i * P:(i + 1) * P] for i in range(3))
        sq3 = sq[:, :].rearrange("p (k t) -> p k t", k=KT)
        yt3 = yt[:, :].rearrange("p (k t) -> p k t", k=KT)
        big3 = big[:, :].rearrange("p (k t) -> p k t", k=32)
        tmp3 = tmp[:, :].rearrange("p (k t) -> p k t", k=KT)

        def ps(name):
            return bank[TURN[name] % BANKS] if name in TURN else bank[BANKS + int(name[3:]) % 2]

        def ps2(name):
            return ps(name)[:, :].rearrange("p (k t) -> p k t", k=2)

        APW = T + TAPS - 1
        a_pad = big[:, 0:4 * APW].rearrange("p (k t) -> p k t", k=4)
        conv = big[:, 1152:2176].rearrange("p (k t) -> p k t", k=4)
        a_sig = big[:, 2176:3200].rearrange("p (k t) -> p k t", k=4)
        qk = big[:, 3200:5248].rearrange("p (k t) -> p k t", k=8)
        v_nat = big[:, 5248:6272].rearrange("p (k t) -> p k t", k=2)
        g_silu = big[:, 6272:7296].rearrange("p (k t) -> p k t", k=4)
        cos_t, sin_t = early[:, 1344:1600], early[:, 1600:1856]
        perm = early[:, 1856:1984]
        dtab = dreg[:, :].rearrange("p (h k t) -> p h k t", h=4, k=2)
        sd = tmp[:, :].rearrange("p (h k t) -> p h k t", h=4, k=2)
        mag, f_re, f_im, nf_re, nf_im = (early[:, 64 * i:64 * i + 64] for i in range(5))
        rotp = early[:, 320:1344].rearrange("p (j c s) -> p j c s", j=8, c=2)
        sc = [tabw[:, 64 * i:64 * i + 64] for i in range(20)]
        tm = tabw[:, 2048:3072].rearrange("p (f s c t) -> p f s c t", f=2, s=4, c=2)
        b_w = adas[0][:, :].rearrange("p (k d c m) -> p k d c m", k=8, d=2, c=2)
        c_w = adas[1][:, :].rearrange("p (s c m) -> p s c m", s=64, c=2)
        tabs = [tabw[:, 768 * i:768 * i + 768].rearrange("p (c t) -> p c t", c=3) for i in range(4)]
        pbuf = [big[:, 2048 + 1024 * i:3072 + 1024 * i].rearrange("p (f c t) -> p f c t", f=2, c=2) for i in range(2)]
        qbuf = [big[:, 4096 + 1024 * i:5120 + 1024 * i].rearrange("p (f c t) -> p f c t", f=2, c=2) for i in range(2)]
        wbuf = [big[:, 6144 + 512 * i:6656 + 512 * i].rearrange("p (c t) -> p c t", c=2) for i in range(2)]
        gbuf = [big[:, 7168 + 512 * i:7680 + 512 * i].rearrange("p (c t) -> p c t", c=2) for i in range(2)]
        qbuf += [tmp[:, 1024 * i:1024 * i + 1024].rearrange("p (f c t) -> p f c t", f=2, c=2) for i in range(2)]

        def rotated(m):
            return qbuf[m % 4][:, :, :, ::-1] if m % 2 else qbuf[m % 4]
        u_rev = sq3
        mk_n = dreg[:, 0:1024].rearrange("p (k t) -> p k t", k=4)
        mv_nat = dreg[:, 1024:2048].rearrange("p (k t) -> p k t", k=2)
        A0, A1 = adas
        gq_s, gk_s = A0[:, 0:512], A0[:, 512:1024]
        la_x, la_c = A0[:, 1024:1536], A0[:, 1536:2048]
        e_pos, e_neg, e_out, k_in = (A0[:, 2048 + 512 * i:2560 + 512 * i] for i in range(4))
        go_n = A0[:, 1024:2048].rearrange("p (k t) -> p k t", k=4)
        go_sq = A0[:, 2560:3584]
        mq_n = accb[:, :].rearrange("p (k t) -> p k t", k=4)
        ys = [A1[:, 1024 * i:1024 * i + 1024].rearrange("p (k t) -> p k t", k=4) for i in range(3)]
        state = A1[:, 3072:3840].rearrange("p (c m v) -> p c m v", c=3, m=2)
        ga1_s = A1[0:16, 3840:4096]
        gv_nat = big[:, 6144:7168].rearrange("p (k t) -> p k t", k=2)
        gg_s = big[:, 7168:8192].rearrange("p (k t) -> p k t", k=4)
        gates = big3
        att = tmp[:, 0:1024].rearrange("p (k t) -> p k t", k=8)
        ko_nat = tmp[:, 1024:1536]
        ff_x, ff_c = tmp[0:64, 1536:1792], tmp[0:64, 1792:2048]
        fq_n = yt[:, 0:1024].rearrange("p (k t) -> p k t", k=4)
        fk_n = yt[:, 1024:2048].rearrange("p (k t) -> p k t", k=4)
        fv_nat = sq[:, 1024:2048].rearrange("p (k t) -> p k t", k=2)
        wsm = early[:, 0:640].rearrange("p (k c) -> p k c", k=8)
        wa2 = early[0:16, 640:896]
        fb = early[0:64, 896:1152]
        foxmask = early[:, 1152:1664].rearrange("p (k t) -> p k t", k=2)
        glamask = early[:, 1664:1792].bitcast(I32)
        logits = tabw[:, 0:512].rearrange("p (k t) -> p k t", k=2)
        probs = [tabw[:, 512 + 512 * i:1024 + 512 * i].rearrange("p (k t) -> p k t", k=2) for i in range(2)]
        prob_t = [tabw[:, 1536 + 512 * i:2048 + 512 * i].rearrange("p (k t) -> p k t", k=2) for i in range(2)]
        fa = [tabw[0:64, 2560 + 256 * i:2816 + 256 * i] for i in range(2)]

        tab_d = nc.dram_tensor("s5_tables", (64, P, 512), F32, kind="Internal").ap()

        panels = []

        def cols_panel(name, w, c0, n, last_job):
            panels.append((name, w[:, c0:c0 + n].rearrange("(k p) c -> p k c", p=P), KT, n, ("job", last_job)))

        def rows_panels(name, w, rows, last_job):
            k0, i = 0, 0
            while k0 < rows // P:
                nk = min(4, rows // P - k0)
                done = k0 + nk >= rows // P
                panels.append((f"{name}{i}", w[k0 * P:(k0 + nk) * P, :].rearrange("(k p) c -> p k c", p=P), nk, D,
                               ("job", last_job) if done else ("row", None)))
                k0 += nk
                i += 1

        for i, (name, job) in enumerate((("av", "av1"), ("ag", "ag1"), ("q", "q1"), ("k", "k1"), ("v", "v1"), ("g", "g1"))):
            cols_panel(name, a["w_in"], 512 * i, 512, job)
        for i in range(2):
            cols_panel(f"wo{i}", a["w_out"], 512 * i, 512, f"wo0.{2 * i + 1}")

        def ffn_panels(l):
            for i in range(8):
                cols_panel(f"f1.{l}.{i}", a["w_fc1"][l], 512 * i, 512, f"f1.{l}.{2 * i + 1}")
            rows_panels(f"f2.{l}.", a["w_fc2"][l], FF1, f"f2.{l}.3")

        ffn_panels(0)
        panels.append(("mem", a["mem"].rearrange("(k p) t -> p k t", p=P), KT, T, ("job", "mv1")))
        cols_panel("mk", a["w_mem_kv"], 0, 512, "mk1")
        cols_panel("mv", a["w_mem_kv"], 512, 512, "mv1")
        for i in range(2):
            cols_panel(f"ga{i}", a["w_glu_a"], 512 * i, 512, f"ga{2 * i + 1}")
            cols_panel(f"gb{i}", a["w_glu_b"], 512 * i, 512, f"gb{2 * i + 1}")
        ffn_panels(1)
        w2 = a["w_in_2"]
        cols_panel("gqk", w2, GQ, 512, "gk0")
        cols_panel("gv", w2, GV, 512, "gv1")
        cols_panel("gg", w2, GG, 512, "gg1")
        cols_panel("fq", w2, FQ, 512, "fq1")
        cols_panel("fk", w2, FK, 512, "fk1")
        cols_panel("fv", w2, FV, 512, "fv1")
        cols_panel("mq", w2, MQ, 512, "mq1")
        for i in range(6):
            cols_panel(f"bg{i}", w2, BG + 512 * i, 512, f"bg{2 * i + 1}")
        for i in range(3):
            rows_panels(f"br{i}.", a["w_branch"][i], 512, f"br{i}.3")
        for i in range(2):
            cols_panel(f"w2o{i}", a["w_out_2"], 512 * i, 512, f"w2o.{2 * i + 1}")
        for i in range(6):
            n = 512 if i < 5 else 256
            last = 2 * i + 1 if i < 5 else 10
            cols_panel(f"fg{i}", a["w_ffn_gate"], 512 * i, n, f"fg{last}")
            cols_panel(f"fu{i}", a["w_ffn_up"], 512 * i, n, f"fu{last}")
        rows_panels("fd", a["w_ffn_down"], FF2, "fd.3")
        place = {pn[0]: i for i, pn in enumerate(panels)}
        rows_before = []
        count = 0
        for pn in panels:
            count += pn[4][0] == "row"
            rows_before.append(count)

        def panel_view(name):
            i = place[name]
            _, _, k, n, _ = panels[i]
            return ring[i % RING][:, 0:k * n].rearrange("p (k c) -> p k c", k=k)

        units = []

        def add_units(names, width, buffers):
            for name in names:
                n = panels[place[name]][3]
                for c0 in range(0, n, width):
                    units.append((name, c0, width, buffers[(len(units) - base) % 3]))

        base = 0
        high_bufs = [split[name][:, 0:2048] for name in ("tabw", "y_cat", "tmp")]
        add_units([f"f1.1.{i}" for i in range(8)], 256, high_bufs)
        add_units([f"f2.1.{i}" for i in range(8)], 512, high_bufs)
        base = LAST = len(units)
        high_bufs = [split["decay_or_mem"][:, :], split["tabw"][:, 0:2048], split["ada_slot1"][:, 2048:4096]]
        add_units([f"f{t}{i}" for i in range(6) for t in "gu"], 256, high_bufs)
        DOWN = len(units)
        add_units([f"fd{i}" for i in range(6)], 512, high_bufs)

        def unit_parts(u):
            name, c0, n, buf = units[u]
            i = place[name]
            _, _, k, width, _ = panels[i]
            low = split[f"ring{i % RING}"][:, 0:k * width].rearrange("p (k c) -> p k c", k=k)
            return panel_view(name)[:, :, c0:c0 + n], low[:, :, c0:c0 + n], buf[:, 0:k * n].rearrange("p (k c) -> p k c", k=k)

        h_hi = split["squares"][:, :].rearrange("p (k t) -> p k t", k=KT)
        h_lo = split["h_in"][:, :].rearrange("p (k t) -> p k t", k=KT)
        big_lo = split["big"][:, :].rearrange("p (k t) -> p k t", k=32)

        def big_hi(m, n=1):
            return split[f"ada_slot{m // 16}"][:, T * (m % 16):T * (m % 16 + n)].rearrange("p (k t) -> p k t", k=n)

        mem_x = panel_view("mem")
        mem_sq = ring[place["mem"] % RING][:, 2048:4096]

        freed = {f"ms{n}": ("rstd", n + 1) for n in range(7)}
        for j in range(2):
            freed.update({f"av{j}": ("amul", j + 1), f"ag{j}": ("agsig", j + 1), f"q{j}": ("qkc", j + 1),
                          f"k{j}": ("qkc", j + 3), f"v{j}": ("vc", j + 1), f"g{j}": ("gsilu", j + 1),
                          f"ro{j}": ("rn", j + 1), f"rr{j}": ("rrs", j + 1)})
            freed.update({f"mk{j}": ("mkn", j + 1), f"mkr{j}": ("mkrs", j + 1), f"mv{j}": ("mvc", j + 1)})
            freed.update({f"gv{j}": ("gvc", j + 1), f"gg{j}": ("ggs", j + 1), f"at{j}": ("atc", j + 1),
                          f"go{j}": ("gon", 2 * j + 2), f"gor{j}": ("gors", j + 1), f"fv{j}": ("fvc", j + 1)})
            freed.update({f"fq{j}": ("nq", j + 1), f"fk{j}": ("nq", j + 3), f"mq{j}": ("nq", j + 5)})
        freed.update({"mu": ("lnxc", 2), "var": ("lnrs", 1), "mms": ("mrs", 1)})
        freed.update({f"rot{j}": ("rope", 3 * j + 2) for j in range(4)})
        freed.update({f"sc{j}": ("sd", j + 1) for j in range(4)})
        for r, name in ((0, "wo0"), (1, "f2.0"), (3, "f2.1"), (4, "w2o"), (5, "fd")):
            freed.update({f"{name}.{p}": ("xres", 8 * r + 2 * p + 2) for p in range(4)})
        freed.update({f"f1.{l}.{j}": ("relu", 16 * l + j + 1) for l in range(2) for j in range(16)})
        freed.update({f"bu{n}": ("s5p", 2 * n + 2) for n in range(64)})
        freed.update({f"ga{p}": ("glut", p + 1) for p in range(4)})
        freed.update({f"gb{p}": ("glus", p + 1) for p in range(4)})
        freed.update({"gq0": ("gqk", 1), "gk0": ("gqk", 2), "ga1r": ("ga1c", 1), "ff": ("ffx", 1), "la": ("lax", 2),
                      "kot": ("koc", 1), "cs0": ("gst", 5), "cs1": ("gst", 3)})
        freed.update({f"nr{i}": ("nrs", i + 1) for i in range(6)})
        freed.update({f"us{u}": ("ul", u + 1) for u in range(8)})
        freed.update({f"ut{u}": ("upt", u + 1) for u in range(8)})
        freed.update({f"uo{j}": ("uoc", j + 1) for j in range(4)})
        freed.update({f"bg{j}": ("gate", 2 * j + 2) for j in range(12)})
        freed.update({f"br{i}.{p}": ("mgm", 4 * i + p + 1) for i in range(3) for p in range(4)})
        freed.update({f"fg{i}": ("fsil", i + 1) for i in range(11)})
        freed.update({f"fu{i}": ("fact", i + 1) for i in range(11)})

        def job_wait(eng, name):
            eng.wait_ge(s("job"), INDEX[name] + 1)

        def unit_wait(eng, u):
            name = units[u][0]
            if u < 16:
                job_wait(eng, f"f1.1.{u}")
            elif LAST <= u < DOWN:
                job_wait(eng, last_jobs[u - LAST])
            else:
                i = u - 16 if u < LAST else u - DOWN
                if i % 2 == 0:
                    eng.wait_ge(s("row_half"), i // 2 + 1 + (7 if u >= LAST else 0))
                else:
                    eng.wait_ge(s("row_panel"), rows_before[place[name]])

        last_jobs = [name for name in JOBS if name[:2] in ("fg", "fu")]
        NORM_G = (("norm_g", 0), ("norm_g", 8), ("norm_g", 16), ("norm_g", 24), ("norm_f", 0), ("g_mix", 0), ("g_ffn", 0))
        NCONST = 6
        NLATE = 8

        block = ctx.enter_context(nc.Block())

        @block.sync
        def _(sp):
            sp.dma_start(cols[:, :], a["cols"]).then_inc(s("cols_in"), 16)
            sp.dma_start(x, a["x"].rearrange("(k p) t -> p k t", p=P)).then_inc(s("x_in"), 16)
            for i, (name, src, k, n, _) in enumerate(panels):
                if i >= RING:
                    kind, job = panels[i - RING][4]
                    if kind == "job":
                        job_wait(sp, job)
                    else:
                        sp.wait_ge(s("row_panel"), rows_before[i - RING])
                else:
                    sp.wait_ge(s("ada_acc"), i + 1)
                sp.dma_start(panel_view(name), src).then_inc(s(f"panel{i % RING}"), 16)
            for p in range(4):
                sp.wait_ge(s("xres"), 8 * 5 + 2 * p + 2)
                sp.dma_start(out[2 * p * P:(2 * p + 2) * P, :].rearrange("(k p) t -> p k t", p=P),
                             yt3[:, 2 * p:2 * p + 2, :]).then_inc(s("out"), 16)
            sp.wait_ge(s("out"), 64)

        def ada_in(k):
            return s(f"ada_{'sw' if k < SW_ADA else 'hw'}{k % 2}"), 16 * ((k - SW_ADA if k >= SW_ADA else k) // 2 + 1)

        def ada_load(eng, k):
            if k >= 2:
                eng.wait_ge(s("ada_acc"), k - 1)
            l, c = divmod(k, ADA)
            eng.dma_start(adas[k % 2][:, :].rearrange("p (k c) -> p k c", k=KT),
                          a["ada_w"][l][:, 512 * c:512 * c + 512].rearrange("(k p) c -> p k c", p=P)).then_inc(ada_in(k)[0], 16)

        @block.gpsimd
        def _(pool):
            pool.dma_start(tabw[:, 0:192], a["s5_scal"]).then_inc(s("s5_in"), 16)
            ada_load(pool, 0)
            ada_load(pool, 1)
            pool.dma_start(early[:, 1344:1984], a["rope"]).then_inc(s("const_in"), 16)
            pool.dma_start(ident[:, :], a["ident"]).then_inc(s("const_in"), 16)
            pool.dma_start(scanmask[:, :], a["scanmask"]).then_inc(s("const_in"), 16)
            for i, n in enumerate((1024, 512, 128)):
                pool.memset(inv[:, i * P:(i + 1) * P], 1.0 / n).then_inc(s("pool_const"), 1)
            pool.memset(one[:, :], 1.0).then_inc(s("pool_const"), 1)
            pool.memset(eps[:, :], EPS).then_inc(s("pool_const"), 1)
            pool.memset(big[:, 0:4 * APW], 0.0).then_inc(s("pool_const"), 1)
            for k in range(2, 9):
                ada_load(pool, k)
                if k == 3:
                    pool.dma_start(dreg[:, :], a["decay"]).then_inc(s("const_in"), 16)
            pool.wait_ge(s("s5_scal"), 1)
            done = 0

            def step(ins):
                ins.then_inc(s("tab_step"), 1)

            tables_out = [0, 0]
            for b in range(16):
                second = int(b >= 5 and b % 2 == 1)
                buffer = dreg if second else tabw
                tb = buffer[:, 0:2048].rearrange("p (s c t) -> p s c t", s=4, c=2)
                if tables_out[second]:
                    pool.wait_ge(s(f"tab_out{second}"), 16 * tables_out[second])
                if b == 5:
                    pool.wait_ge(s("sd"), 4)
                if b == 1:
                    ada_load(pool, 9)
                step(pool.memset(tb[:, :, 0, 0:1], 1.0))
                step(pool.memset(tb[:, :, 1, 0:1], 0.0))
                done += 2
                for j in range(8):
                    n = 1 << j
                    for t0 in range(0, n, 64):
                        w = min(64, n)
                        src = tb[:, :, :, t0:t0 + w]
                        pool.wait_ge(s("tab_step"), done)
                        for r in range(2):
                            rot = rotp[:, j, r, 4 * b:4 * b + 4].unsqueeze(2).unsqueeze(3)
                            step(pool.tensor_tensor(tm[:, r, :, :, 0:w], src, rot.broadcast_to([P, 4, 2, w]), ALU.mult))
                        done += 2
                        pool.wait_ge(s("tab_step"), done)
                        step(pool.tensor_tensor(tb[:, :, 0, n + t0:n + t0 + w], tm[:, 0, :, 0, 0:w], tm[:, 1, :, 1, 0:w], ALU.subtract))
                        step(pool.tensor_tensor(tb[:, :, 1, n + t0:n + t0 + w], tm[:, 1, :, 0, 0:w], tm[:, 0, :, 1, 0:w], ALU.add))
                        done += 2
                pool.wait_ge(s("tab_step"), done)
                pool.dma_start(tab_d[4 * b:4 * b + 4].rearrange("s p f -> p s f"),
                               buffer[:, 0:2048].rearrange("p (s f) -> p s f", s=4)).then_inc(s(f"tab_out{second}"), 16)
                tables_out[second] += 1
            for n in range(65):
                if n < 64:
                    pool.wait_ge(s("s5p"), 2 * n + 2)
                    if n >= 2:
                        pool.wait_ge(s("s5g"), 2 * n - 2)
                    pb = pbuf[n % 2]
                    pool.tensor_tensor(wbuf[n % 2], pb[:, 0], pb[:, 1], ALU.add).then_inc(s("s5w"), 1)
                if n >= 1:
                    m = n - 1
                    pool.wait_ge(s("s5g"), 2 * m + 2)
                    if m >= 4:
                        pool.wait_ge(s("s5y"), m - 3)
                    pool.tensor_tensor(rotated(m)[:, 1], gbuf[m % 2][:, ::-1, :], tabs[m % 4][:, 2:0:-1, :], ALU.mult).then_inc(s("s5r"), 1)
            for n in range(4, 12):
                p = n % 4
                pool.wait_ge(s("mgm"), n + 1)
                merged = yt3[:, 2 * p:2 * p + 2, :]
                pool.tensor_tensor(merged, merged, tmp3[:, 2 * p:2 * p + 2, :], ALU.add).then_inc(s("mga"), 1)

        @block.scalar
        def _(act):
            act.wait_ge(s("cols_in"), 16)
            act.activation(cact[:, :], col("c", 0, 8), ACT.Silu).then_inc(s("cact"), 1)
            act.wait_ge(s("s5_in"), 16)
            act.activation(sc[3], sc[2], ACT.Exp).then_inc(s("s5a"), 1)
            act.wait_ge(s("s5d"), 2)
            act.activation(mag, sc[5], ACT.Exp).then_inc(s("s5a"), 1)
            act.wait_ge(s("s5d"), 9)
            act.activation(rotp[:, 0, 1, :], sc[7], ACT.Sin).then_inc(s("s5a"), 1)
            act.activation(sc[8], sc[7], ACT.Sin, scale=0.5).then_inc(s("s5a"), 1)

            def root(job, width=T):
                job_wait(act, job)
                act.activation(ps(job)[:, 0:width], ps(job)[:, 0:width], ACT.Sqrt, bias=eps[:, :]).then_inc(s("root"), 1)

            def squares(n):
                for c in range(4):
                    if n == 0:
                        act.wait_ge(s("x_in"), 16)
                    elif n == 5:
                        act.wait_ge(s("hn"), 8 * 4 + 2 * c + 2)
                    else:
                        act.wait_ge(s("xres"), 8 * {1: 0, 2: 1, 3: 2, 4: 3, 6: 4}[n] + 2 * c + 2)
                    act.activation(sq3[:, 2 * c:2 * c + 2, :], x[:, 2 * c:2 * c + 2, :], ACT.Square).then_inc(s("sq"), 1)
                root(f"ms{n}")

            def shift(n):
                act.wait_ge(s("mod"), ADA * (n // 2) + (2 if n % 2 == 0 else 8))
                for k in range(KT):
                    act.wait_ge(s("hn"), 8 * n + k + 1)
                    i = 48 * (n // 2) + 24 * (n % 2) + k
                    act.activation(h[:, k, :], h[:, k, :], ACT.Identity, bias=mod[:, i:i + 1]).then_inc(s("h"), 1)
                    if n == 3 and k:
                        input_high(k - 1, s("h"), 24)
                if n == 3:
                    input_high(KT - 1, s("h"), 24)

            def input_high(k, ready, base):
                act.wait_ge(ready, base + k + 1)
                act.activation(h_hi[:, k, :], h[:, k, :], ACT.Copy).then_inc(s("h_high"), 1)

            def split_high(u):
                name = units[u][0]
                i = place[name]
                act.wait_ge(s(f"panel{i % RING}"), 16 * (i // RING + 1))
                if u == 1:
                    job_wait(act, "gb3")
                elif u == 2:
                    act.wait_ge(s("xres"), 24)
                elif u == LAST:
                    job_wait(act, "uo3")
                elif u == LAST + 2:
                    job_wait(act, "br2.3")
                elif u not in (0, LAST + 1):
                    unit_wait(act, u - 3)
                whole, _, high = unit_parts(u)
                act.activation(high, whole, ACT.Copy).then_inc(s("w_high"), 1)

            def act_high(n, m, ready, count):
                act.wait_ge(ready, count)
                act.activation(big_hi(m, 2), big3[:, m:m + 2, :], ACT.Copy).then_inc(s("a_high"), 1)

            act.wait_ge(s("pool_const"), 6)
            squares(0)
            shift(0)
            for j in range(2):
                job_wait(act, f"ag{j}")
                act.activation(a_sig[:, 2 * j:2 * j + 2, :], ps2(f"ag{j}"), ACT.Sigmoid).then_inc(s("agsig"), 1)
            for j, name in enumerate(("q0", "q1", "k0", "k1")):
                job_wait(act, name)
                act.activation(qk[:, 2 * j:2 * j + 2, :], ps2(name), ACT.Copy).then_inc(s("qkc"), 1)
            for j in range(2):
                job_wait(act, f"v{j}")
                act.activation(v_nat[:, j, :], ps(f"v{j}")[:, :], ACT.Copy).then_inc(s("vc"), 1)
            for j in range(2):
                job_wait(act, f"g{j}")
                act.activation(g_silu[:, 2 * j:2 * j + 2, :], ps2(f"g{j}"), ACT.Silu).then_inc(s("gsilu"), 1)
            for j in range(2):
                act.wait_ge(s("lnxc"), j + 1)
                act.activation(sq3[:, 2 * j:2 * j + 2, :], conv[:, 2 * j:2 * j + 2, :], ACT.Square).then_inc(s("lnsq"), 1)
            root("var")
            for i in range(4):
                act.wait_ge(s("lny"), i + 1)
                act.activation(yt3[:, i, :], conv[:, i, :], ACT.Silu, bias=col("cln_b", i)).then_inc(s("yconv"), 1)
            for j in range(2):
                job_wait(act, f"ro{j}")
                act.activation(sq[:, 1024 + 512 * j:1536 + 512 * j], ps(f"ro{j}")[:, :], ACT.Square).then_inc(s("rsq"), 1)
                root(f"rr{j}", 512)
            squares(1)
            shift(1)

            def relus(l, after):
                for j in range(16):
                    job_wait(act, f"f1.{l}.{j}")
                    act.activation(big3[:, 2 * j:2 * j + 2, :], ps2(f"f1.{l}.{j}"), ACT.Relu).then_inc(s("relu"), 1)
                    after(j)

            def next_ada(j):
                if 12 + j < 24:
                    ada_load(act, 12 + j)

            ada_load(act, 10)
            ada_load(act, 11)
            relus(0, next_ada)
            act.wait_ge(s("ada_acc"), 2 * ADA)
            act.dma_start(adas[0][:, :], a["s5_b"]).then_inc(s("bc_in"), 16)
            act.dma_start(tmp[:, :], a["s5_c"][:, 0, :]).then_inc(s("bc_in"), 16)
            act.dma_start(yt[:, :], a["s5_c"][:, 1, :]).then_inc(s("bc_in"), 16)
            squares(2)
            shift(2)
            for k in range(KT):
                act.wait_ge(s("h"), 16 + k + 1)
                act.activation(u_rev[:, k, :], h[:, k, ::-1], ACT.Copy).then_inc(s("ur"), 1)
            act.wait_ge(s("tab_out0"), 16 * 10)
            act.wait_ge(s("tab_out1"), 16 * 6)

            def table(n):
                if n < 64:
                    if n >= 4:
                        act.wait_ge(s("s5q"), n - 3)
                        act.wait_ge(s("s5r"), n - 3)
                    k, q, d = n // 8, n // 2 % 4, n % 2
                    act.dma_start(tabw[:, 768 * (n % 4):768 * (n % 4) + 512], tab_d[32 * d + 4 * k + q]).then_inc(s(f"tab{n % 4}"), 16)

            def negate(n):
                act.wait_ge(s(f"tab{n % 4}"), 16 * (n // 4 + 1))
                act.activation(tabs[n % 4][:, 2, :], tabs[n % 4][:, 1, :], ACT.Copy, scale=-1.0).then_inc(s("s5n"), 1)

            for n in range(4):
                table(n)
            for n in range(3):
                negate(n)
            i = place["mem"]
            act.wait_ge(s(f"panel{i % RING}"), 16 * (i // RING + 1))
            for c in range(4):
                act.activation(mem_sq[:, 512 * c:512 * c + 512].rearrange("p (k t) -> p k t", k=2), mem_x[:, 2 * c:2 * c + 2, :], ACT.Square).then_inc(s("msq"), 1)
            for n in range(4, 68):
                if n < 65:
                    negate(n - 1)
                table(n)
                m = n - 4
                if m == 9:
                    root("mms")
                if m in (16, 24):
                    j = (m - 16) // 8
                    job_wait(act, f"mk{j}")
                    act.activation(mem_sq[:, 512 * j:512 * j + 512], ps(f"mk{j}")[:, :], ACT.Square).then_inc(s("mksq"), 1)
                if m in (18, 26):
                    root(f"mkr{(m - 18) // 8}", 512)
                if m in (34, 42):
                    j = (m - 34) // 8
                    job_wait(act, f"mv{j}")
                    act.activation(mv_nat[:, j, :], ps(f"mv{j}")[:, :], ACT.Copy).then_inc(s("mvc"), 1)
                if m >= 11 and (m - 11) % 8 == 0:
                    k = (m - 11) // 8
                    act.wait_ge(s("s5z"), k + 1)
                    act.activation(yt3[:, k, :], yt3[:, k, :], ACT.Gelu_apprx_tanh).then_inc(s("z"), 1)
            act.wait_ge(s("s5z"), 8)
            act.activation(yt3[:, 7, :], yt3[:, 7, :], ACT.Gelu_apprx_tanh).then_inc(s("z"), 1)
            act.dma_start(wsm[:, :, 0:64], a["w_fox_f"].rearrange("(k p) c -> p k c", p=P)).then_inc(s("late"), 16)
            act.dma_start(wsm[:, :, 64:80], a["w_in_2"][:, GA:GA + 16].rearrange("(k p) c -> p k c", p=P)).then_inc(s("late"), 16)
            act.dma_start(wa2, a["w_gla_a2"]).then_inc(s("late"), 16)
            act.dma_start(early[:, 1152:1664], a["foxmask"]).then_inc(s("late"), 16)
            act.dma_start(glamask, a["glamask"]).then_inc(s("late"), 16)
            for p in range(4):
                job_wait(act, f"gb{p}")
                act.activation(tmp3[:, 2 * p:2 * p + 2, :], ps2(f"gb{p}"), ACT.Sigmoid).then_inc(s("glus"), 1)
            split_high(0)
            split_high(1)
            squares(3)
            shift(3)
            split_high(2)

            def after_relu(j):
                split_high(j + 3)
                act_high(j, 2 * j, s("fsq"), 16 + j + 1)

            relus(1, after_relu)
            for u in range(19, 32):
                split_high(u)
            squares(4)
            squares(5)
            for j, (name, o) in enumerate((("gq0", gq_s), ("gk0", gk_s))):
                job_wait(act, name)
                act.activation(o, ps(name)[:, :], ACT.Copy).then_inc(s("gqk"), 1)
            job_wait(act, "ga1r")
            act.activation(ga1_s, ps("ga1r")[0:16, 0:T], ACT.Copy).then_inc(s("ga1c"), 1)
            for j in range(2):
                job_wait(act, f"gv{j}")
                act.activation(gv_nat[:, j, :], ps(f"gv{j}")[:, :], ACT.Copy).then_inc(s("gvc"), 1)
            for j in range(2):
                job_wait(act, f"gg{j}")
                act.activation(gg_s[:, 2 * j:2 * j + 2, :], ps2(f"gg{j}"), ACT.Silu).then_inc(s("ggs"), 1)
            act.wait_ge(s("ffa"), 1)
            act.activation(ff_c, ff_c, ACT.Exp, scale=-1.0).then_inc(s("ffe"), 1)
            act.wait_ge(s("ffe"), 1)
            act.activation(ff_c, ff_c, ACT.Ln, bias=1.0).then_inc(s("ffe"), 1)
            act.wait_ge(s("lab"), 1)
            act.activation(la_c, la_c, ACT.Exp, scale=-1.0).then_inc(s("lae"), 1)
            act.wait_ge(s("lae"), 1)
            act.activation(la_c, la_c, ACT.Ln, bias=1.0).then_inc(s("lae"), 1)
            act.wait_ge(s("lac"), 2)
            act.activation(e_pos, la_c, ACT.Exp, scale=1.0 / 16).then_inc(s("lax_e"), 1)
            act.activation(e_neg, la_c, ACT.Exp, scale=-1.0 / 16).then_inc(s("lax_e"), 1)
            act.wait_ge(s("lad"), 1)
            act.activation(e_out, e_out, ACT.Exp, scale=1.0 / 16).then_inc(s("lax_e"), 1)

            def head_squares(i, name):
                if i >= 2:
                    job_wait(act, f"nr{i - 2}")
                job_wait(act, name)
                act.activation(sq[:, 512 * (i % 2):512 * (i % 2) + 512], ps(name)[:, :], ACT.Square).then_inc(s("nsq"), 1)

            head_squares(0, "fq0")
            head_squares(1, "fq1")
            job_wait(act, "kot")
            act.activation(ko_nat, ps("kot")[:, :], ACT.Copy).then_inc(s("koc"), 1)
            root("nr0", 512)
            root("nr1", 512)
            head_squares(2, "fk0")
            head_squares(3, "fk1")
            for j in range(2):
                job_wait(act, f"go{j}")
                act.activation(go_sq[:, 512 * j:512 * j + 512], ps(f"go{j}")[:, :], ACT.Square).then_inc(s("gosq"), 1)
                root(f"gor{j}", 512)
                if j == 0:
                    root("nr2", 512)
                    root("nr3", 512)
            for j in range(2):
                job_wait(act, f"fv{j}")
                act.activation(fv_nat[:, j, :], ps(f"fv{j}")[:, :], ACT.Copy).then_inc(s("fvc"), 1)
            head_squares(4, "mq0")
            head_squares(5, "mq1")

            def gate(j):
                job_wait(act, f"bg{j}")
                for i in range(2):
                    m = 2 * j + i
                    act.activation(gates[:, m, :], ps2(f"bg{j}")[:, i, :], ACT.Sigmoid, bias=col("b_gate", m)).then_inc(s("gate"), 1)

            for u in range(10):
                if u < 8:
                    for i in range(2):
                        act.wait_ge(s("unm"), u + 1)
                        if u >= 2:
                            job_wait(act, f"ut{u - 2}")
                        act.activation(probs[u % 2][:, i, :], logits[:, i, :], ACT.Exp, bias=small[:, 2 + i:3 + i],
                                       accum_out=small[:, 4 + i:5 + i]).then_inc(s("ue"), 1)
                gate(u)
                if u == 0:
                    root("nr4", 512)
                    root("nr5", 512)
                if 1 <= u <= 8:
                    job_wait(act, f"ut{u - 1}")
                    if u >= 3:
                        job_wait(act, f"uo{(u - 3) // 2}")
                    act.activation(tabw[:, 1536 + 512 * ((u - 1) % 2):2048 + 512 * ((u - 1) % 2)], ps(f"ut{u - 1}")[:, :], ACT.Copy).then_inc(s("upt"), 1)
                if u >= 3 and u % 2 == 1:
                    j = (u - 3) // 2
                    job_wait(act, f"uo{j}")
                    act.activation(ys[1 + j // 2][:, 2 * (j % 2):2 * (j % 2) + 2, :], ps2(f"uo{j}"), ACT.Copy).then_inc(s("uoc"), 1)
            gate(10)
            gate(11)
            for u in range(3):
                split_high(LAST + u)
            squares(6)
            for k in range(KT):
                input_high(k, s("hn"), 48)
            for u, name in enumerate(last_jobs):
                i = int(name[2:])
                if name[:2] == "fg":
                    job_wait(act, name)
                    if i >= 4:
                        act.wait_ge(s("fact"), i - 3)
                    act.activation(tmp[:, 512 * (i % 4):512 * (i % 4) + 512], ps(name)[:, :], ACT.Silu).then_inc(s("fsil"), 1)
                split_high(LAST + u + 3)
                if name[:2] == "fu":
                    act_high(16 + i, 2 * i, s("fact"), i + 1)
            for u in range(DOWN + 3, len(units)):
                split_high(u)

        @block.vector
        def _(dve):
            count = [0]

            def link(ins):
                count[0] += 1
                ins.then_inc(s("s5d"), 1)
                dve.wait_ge(s("s5d"), count[0])

            tt, ts, stt = dve.tensor_tensor, dve.tensor_scalar, dve.scalar_tensor_tensor
            li, dt = sc[1], sc[3]
            dve.wait_ge(s("s5_in"), 16)
            link(ts(sc[4], sc[0], -1e-4, None, ALU.min))
            dve.wait_ge(s("s5a"), 1)
            link(tt(sc[5], sc[4], dt, ALU.mult))
            link(tt(sc[6], li, dt, ALU.mult))
            link(ts(sc[7], sc[6], 1.0 / (2 * np.pi), ROUND, ALU.mult, ALU.add))
            link(ts(sc[9], sc[7], ROUND, None, ALU.subtract))
            link(stt(sc[6], sc[9], -TWO_PI_A, sc[6], ALU.mult, ALU.add))
            link(stt(sc[6], sc[9], -TWO_PI_B, sc[6], ALU.mult, ALU.add))
            link(stt(sc[6], sc[9], -TWO_PI_C, sc[6], ALU.mult, ALU.add))
            link(ts(sc[7], sc[6], PI_SAFE, -PI_SAFE, ALU.min, ALU.max))
            dve.wait_ge(s("s5a"), 4)
            c1, s1 = rotp[:, 0, 0, :], rotp[:, 0, 1, :]
            link(tt(sc[9], sc[8], sc[8], ALU.mult))
            link(ts(c1, sc[9], -2.0, 1.0, ALU.mult, ALU.add))
            abr, abi, nr, den, t0, t1 = sc[10], sc[11], sc[12], sc[13], sc[14], sc[15]
            link(tt(abr, mag, c1, ALU.mult))
            link(tt(abi, mag, s1, ALU.mult))
            link(ts(nr, abr, -1.0, None, ALU.add))
            link(tt(t0, sc[4], sc[4], ALU.mult))
            link(tt(t1, li, li, ALU.mult))
            link(tt(den, t0, t1, ALU.add))
            link(dve.reciprocal(den, den))
            link(tt(t0, nr, sc[4], ALU.mult))
            link(tt(t1, abi, li, ALU.mult))
            link(tt(t0, t0, t1, ALU.add))
            link(tt(f_re, t0, den, ALU.mult))
            link(tt(t0, abi, sc[4], ALU.mult))
            link(tt(t1, nr, li, ALU.mult))
            link(tt(t0, t0, t1, ALU.subtract))
            link(tt(f_im, t0, den, ALU.mult))
            link(ts(nf_re, f_re, -1.0, None, ALU.mult))
            link(ts(nf_im, f_im, -1.0, None, ALU.mult))
            for j in range(7):
                cj, sj = rotp[:, j, 0, :], rotp[:, j, 1, :]
                link(tt(t0, cj, cj, ALU.mult))
                link(tt(t1, sj, sj, ALU.mult))
                link(tt(rotp[:, j + 1, 0, :], t0, t1, ALU.subtract))
                link(tt(t0, cj, sj, ALU.mult))
                if j < 6:
                    link(ts(rotp[:, j + 1, 1, :], t0, 2.0, None, ALU.mult))
                else:
                    ts(rotp[:, j + 1, 1, :], t0, 2.0, None, ALU.mult).then_inc(s("s5_scal"), 1)

            def ada_acc(k):
                dve.wait_ge(*ada_in(k))
                if k >= 2:
                    job_wait(dve, f"ada{k - 2}")
                w = adas[k % 2][:, :].rearrange("p (k c) -> p k c", k=KT)
                acc = accb[:, 512 * (k % 2):512 * (k % 2) + 512]
                if k == 0:
                    dve.wait_ge(s("cact"), 1)
                for i in range(KT):
                    if i == 0:
                        ts(acc, w[:, 0, :], cact[:, 0:1], None, ALU.mult).then_inc(s("ada_part"), 1)
                    else:
                        dve.wait_ge(s("ada_part"), 7 * k + i)
                        stt(acc, w[:, i, :], cact[:, i:i + 1], acc, ALU.mult, ALU.add)\
                            .then_inc(s("ada_part") if i < KT - 1 else s("ada_acc"), 1)

            def ada_mod(k):
                job_wait(dve, f"ada{k}")
                tt(mod[:, 4 * k:4 * k + 4], ps(f"ada{k}")[:, 0:4], col("ada_b", 4 * k, 4), ALU.add).then_inc(s("mod"), 1)

            def rms(job, width=T, sem="rstd"):
                dve.wait_ge(s("root"), ROOTS.index(job) + 1)
                return dve.reciprocal(rs[:, 0:width], ps(job)[:, 0:width]).then_inc(s(sem), 1)

            def norm(n):
                name, g0 = NORM_G[n]
                gain = col(name, g0, 8)
                if n < 4:
                    l, f = divmod(n, 2)
                    dve.wait_ge(s("mod"), ADA * l + 6 * f + 4)
                    i = 48 * l + 24 * f + 8
                    stt(gs[:, :], mod[:, i:i + 8], 1.0, gain, ALU.add, ALU.mult).then_inc(s("gs"), 1)
                    dve.wait_ge(s("gs"), n + 1)
                    gain = gs[:, :]
                rms(f"ms{n}")
                dve.wait_ge(s("rstd"), n + 1)
                dst = x if n == 4 else h
                for k in range(KT):
                    stt(dst[:, k, :], x[:, k, :], gain[:, k:k + 1], rs[:, 0:T], ALU.mult, ALU.mult).then_inc(s("hn"), 1)
                    if n in (3, 6) and k >= 2:
                        input_low(n, k - 2)
                if n in (3, 6):
                    input_low(n, KT - 2)
                    input_low(n, KT - 1)

            def input_low(n, k):
                dve.wait_ge(s("h_high"), (0 if n == 3 else 8) + k + 1)
                tt(h_lo[:, k, :], h[:, k, :], h_hi[:, k, :].bitcast(F32), ALU.subtract).then_inc(s("h_low"), 1)

            def split_low(u):
                dve.wait_ge(s("w_high"), u + 1)
                whole, low, high = unit_parts(u)
                tt(low, whole, high.bitcast(F32), ALU.subtract).then_inc(s("w_low"), 1)

            def act_low(n):
                m = 2 * (n if n < 16 else n - 16)
                dve.wait_ge(s("a_high"), n + 1)
                tt(big_lo[:, m:m + 2, :], big3[:, m:m + 2, :], big_hi(m, 2).bitcast(F32), ALU.subtract).then_inc(s("a_low"), 1)

            def residual(r, name, gate):
                for p in range(4):
                    job_wait(dve, f"{name}.{p}")
                    for i in range(2):
                        m = 2 * p + i
                        xs = x[:, m, :]
                        if gate is None:
                            o = yt3[:, m, :] if r == 5 else xs
                            tt(o, ps2(f"{name}.{p}")[:, i, :], xs, ALU.add).then_inc(s("xres"), 1)
                        else:
                            stt(xs, ps2(f"{name}.{p}")[:, i, :], mod[:, gate + m:gate + m + 1], xs, ALU.mult, ALU.add)\
                                .then_inc(s("xres"), 1)

            for k in range(4):
                ada_acc(k)
                if k:
                    ada_mod(k - 1)
            ada_mod(3)
            dve.wait_ge(s("cols_in"), 16)
            norm(0)
            for k in range(4, 9):
                ada_acc(k)
                if k > 4:
                    ada_mod(k - 1)
            ada_mod(8)
            dve.wait_ge(s("pool_const"), 6)
            for j in range(2):
                dve.wait_ge(s("agsig"), j + 1)
                tt(a_pad[:, 2 * j:2 * j + 2, 15:15 + T], ps2(f"av{j}"), a_sig[:, 2 * j:2 * j + 2, :], ALU.mult).then_inc(s("amul"), 1)
            for tap in range(TAPS):
                for i in range(4):
                    n = 4 * tap + i
                    w = col("conv_w", TAPS * i + tap)
                    src = a_pad[:, i, tap:tap + T]
                    if tap == 0:
                        dve.wait_ge(s("amul"), i // 2 + 1)
                        ts(conv[:, i, :], src, w, col("conv_b", i), ALU.mult, ALU.add).then_inc(s("conv"), 1)
                    else:
                        dve.wait_ge(s("conv"), n - 3)
                        stt(conv[:, i, :], src, w, conv[:, i, :], ALU.mult, ALU.add).then_inc(s("conv"), 1)
            job_wait(dve, "mu")
            for j in range(2):
                dve.wait_ge(s("conv"), 4 * TAPS)
                c2 = conv[:, 2 * j:2 * j + 2, :]
                tt(c2, c2, ps("mu")[:, 0:T].unsqueeze(1).broadcast_to([P, 2, T]), ALU.subtract).then_inc(s("lnxc"), 1)
            dve.wait_ge(s("const_in"), 64)
            for j in range(4):
                qq = qk[:, 2 * j:2 * j + 2, :]
                ta, tbb = tmp3[:, 0:2, :], tmp3[:, 2:4, :]
                job_wait(dve, f"rot{j}")
                if j:
                    dve.wait_ge(s("rope"), 3 * j)
                tt(ta, qq, cos_t.unsqueeze(1).broadcast_to([P, 2, T]), ALU.mult).then_inc(s("rope"), 1)
                tt(tbb, ps2(f"rot{j}"), sin_t.unsqueeze(1).broadcast_to([P, 2, T]), ALU.mult).then_inc(s("rope"), 1)
                dve.wait_ge(s("rope"), 3 * j + 2)
                tt(qq, ta, tbb, ALU.add).then_inc(s("rope"), 1)
            rms("var", sem="lnrs")
            dve.wait_ge(s("lnrs"), 1)
            dve.wait_ge(s("lnxc"), 2)
            for i in range(4):
                stt(conv[:, i, :], conv[:, i, :], col("cln_g", i), rs[:, 0:T], ALU.mult, ALU.mult).then_inc(s("lny"), 1)
            ada_acc(9)
            for hd in range(4):
                job_wait(dve, f"sc{hd}")
                tt(sd[:, hd], ps2(f"sc{hd}"), dtab[:, hd], ALU.mult).then_inc(s("sd"), 1)
            ada_mod(9)
            for j in range(2):
                rms(f"rr{j}", 512, "rrs")
                dve.wait_ge(s("rrs"), j + 1)
                dst = qk[:, 2 * j:2 * j + 2, :]
                tt(dst, ps2(f"ro{j}"), rs[:, :].rearrange("p (k t) -> p k t", k=2), ALU.mult).then_inc(s("rn"), 1)
                dve.wait_ge(s("rn"), j + 1)
                dve.wait_ge(s("gsilu"), j + 1)
                tt(yt3[:, 4 + 2 * j:6 + 2 * j, :], dst, g_silu[:, 2 * j:2 * j + 2, :], ALU.mult).then_inc(s("ry"), 1)
            dve.wait_ge(s("mod"), 6)
            residual(0, "wo0", 16)
            norm(1)

            def ffn_square(l, j):
                dve.wait_ge(s("relu"), 16 * l + j + 1)
                hh = big3[:, 2 * j:2 * j + 2, :]
                tt(hh, hh, hh, ALU.mult).then_inc(s("fsq"), 1)

            def s5_output_weights():
                dve.wait_ge(s("bc_in"), 48)
                n = 0
                for d in range(2):
                    c_re = tmp[:, 1024 * d:1024 * d + 1024].rearrange("p (s m) -> p s m", s=32)
                    c_im = yt[:, 1024 * d:1024 * d + 1024].rearrange("p (s m) -> p s m", s=32)
                    part = sq[:, 0:1024].rearrange("p (s m) -> p s m", s=32)
                    o_re, o_im = c_w[:, 32 * d:32 * d + 32, 0, :], c_w[:, 32 * d:32 * d + 32, 1, :]

                    def f(v):
                        return v[:, 32 * d:32 * d + 32].unsqueeze(2).broadcast_to([P, 32, 32])

                    for o, p0, f0, p1, f1, op in ((o_re, c_re, f_re, c_im, f_im, ALU.subtract),
                                                  (o_im, c_re, nf_im, c_im, nf_re, ALU.add)):
                        tt(o, p0, f(f0), ALU.mult).then_inc(s("cw"), 1)
                        if n:
                            dve.wait_ge(s("cw"), n)
                        tt(part, p1, f(f1), ALU.mult).then_inc(s("cw"), 1)
                        dve.wait_ge(s("cw"), n + 2)
                        tt(o, o, part, op).then_inc(s("cw"), 1)
                        n += 3

            def more_ada(j):
                if j < 14:
                    ada_acc(10 + j)
                if j >= 1 and j < 15:
                    ada_mod(9 + j)

            for j in range(16):
                ffn_square(0, j)
                more_ada(j)
            s5_output_weights()
            dve.wait_ge(s("mod"), ADA)
            residual(1, "f2.0", 40)
            norm(2)
            for n in range(66):
                k, q, d = n // 8, n // 2 % 4, n % 2
                if n < 64:
                    tab = tabs[n % 4]
                    job_wait(dve, f"bu{n}")
                    dve.wait_ge(s("s5n"), n + 1)
                    if n >= 2:
                        dve.wait_ge(s("s5w"), n - 1)
                    tt(pbuf[n % 2][:, 0], ps2(f"bu{n}"), tab[:, 0:1, :].broadcast_to([P, 2, T]), ALU.mult).then_inc(s("s5p"), 1)
                    tt(pbuf[n % 2][:, 1], ps2(f"bu{n}")[:, ::-1, :], tab[:, 1:3, :], ALU.mult).then_inc(s("s5p"), 1)
                if 1 <= n <= 64:
                    m = n - 1
                    mk, mq_, md = m // 8, m // 2 % 4, m % 2
                    tab = tabs[m % 4]
                    at = 32 * md + 4 * mk + mq_
                    dve.wait_ge(s("s5w"), m + 1)
                    if m >= 2:
                        dve.wait_ge(s("s5r"), m - 1)
                    for r in range(2):
                        dve.tensor_tensor_scan(gbuf[m % 2][:, r, :], mag[:, at:at + 1].broadcast_to([P, T]), wbuf[m % 2][:, r, :],
                                               0.0, ALU.mult, ALU.add).then_inc(s("s5g"), 1)
                    dve.wait_ge(s("s5g"), 2 * m + 2)
                    if m >= 4:
                        dve.wait_ge(s("s5y"), m - 3)
                    tt(rotated(m)[:, 0], gbuf[m % 2], tab[:, 0:1, :].broadcast_to([P, 2, T]), ALU.mult).then_inc(s("s5q"), 1)
                if n >= 9 and (n - 9) % 8 == 0:
                    kk = (n - 9) // 8
                    dve.wait_ge(s("s5y"), 8 * kk + 8)
                    stt(yt3[:, kk, :], h[:, kk, :], col("s5_d", kk), bank[6 + kk % 2][:, 0:T], ALU.mult, ALU.add).then_inc(s("s5z"), 1)
                if n == 11:
                    rms("mms", sem="mrs")
                    dve.wait_ge(s("mrs"), 1)
                    for kk in range(KT):
                        stt(mem_x[:, kk, :], mem_x[:, kk, :], col("g_mem", kk), rs[:, 0:T], ALU.mult, ALU.mult).then_inc(s("memn"), 1)
                if n in (20, 28):
                    j = (n - 20) // 8
                    rms(f"mkr{j}", 512, "mkrs")
                    dve.wait_ge(s("mkrs"), j + 1)
                    stt(mk_n[:, 2 * j:2 * j + 2, :].rearrange("p k t -> p (k t)"), ps(f"mk{j}")[:, :], col("g_mk"), rs[:, :],
                        ALU.mult, ALU.mult).then_inc(s("mkn"), 1)
            dve.wait_ge(s("mod"), ADA + 6)
            for p in range(4):
                dve.wait_ge(s("glus"), p + 1)
                g2 = tmp3[:, 2 * p:2 * p + 2, :]
                tt(g2, ps2(f"ga{p}"), g2, ALU.mult).then_inc(s("glut"), 1)
                dve.wait_ge(s("glut"), p + 1)
                for i in range(2):
                    m = 2 * p + i
                    stt(x[:, m, :], tmp3[:, m, :], mod[:, 48 + 16 + m:48 + 17 + m], x[:, m, :], ALU.mult, ALU.add).then_inc(s("xres"), 1)
            split_low(0)
            norm(3)
            for u in (1, 2):
                split_low(u)
            for j in range(16):
                ffn_square(1, j)
                if j:
                    act_low(j - 1)
                split_low(j + 3)
            act_low(15)
            for u in range(19, 32):
                split_low(u)
            dve.wait_ge(s("mod"), 2 * ADA)
            residual(3, "f2.1", 48 + 40)
            norm(4)
            norm(5)
            dve.memset(tmp[:, 0:1024], 0.0).then_inc(s("atz"), 1)
            ts(gsc[:, 0:1], col("g_fq"), float(128 ** -0.5), None, ALU.mult).then_inc(s("gqs"), 1)
            ts(gsc[:, 1:2], col("g_mq"), float(128 ** -0.5), None, ALU.mult).then_inc(s("gqs"), 1)
            dve.memset(fb, 1.0).then_inc(s("fb"), 1)
            job_wait(dve, "ff")
            ts(ff_x, ps("ff")[0:64, 0:T], cols[0:64, COLS["b_fox"]:COLS["b_fox"] + 1], None, ALU.add).then_inc(s("ffx"), 1)
            dve.wait_ge(s("ffx"), 1)
            stt(ff_c, ff_x, -1.0, ff_x, ALU.mult, ALU.max).then_inc(s("ffa"), 1)
            job_wait(dve, "la")
            for i in range(2):
                ts(la_x[:, T * i:T * i + T], ps2("la")[:, i, :], col("b_gla", i), None, ALU.add).then_inc(s("lax"), 1)
            dve.wait_ge(s("lax"), 2)
            stt(la_c, la_x, -1.0, la_x, ALU.mult, ALU.max).then_inc(s("lab"), 1)
            dve.wait_ge(s("ffe"), 2)
            stt(ff_x, ff_x, 0.0, ff_c, ALU.min, ALU.subtract).then_inc(s("ffl"), 1)
            dve.wait_ge(s("ffl"), 1)
            dve.wait_ge(s("fb"), 1)
            dve.tensor_tensor_scan(ff_c, fb, ff_x, 0.0, ALU.mult, ALU.add).then_inc(s("ffs"), 1)
            dve.wait_ge(s("ffs"), 1)
            ts(early[32:64, 896:1152], tmp[32:64, 1792:2048], -1.0, None, ALU.mult).then_inc(s("fb"), 1)
            dve.wait_ge(s("lae"), 2)
            stt(la_x, la_x, 0.0, la_c, ALU.min, ALU.subtract).then_inc(s("las"), 1)
            dve.wait_ge(s("las"), 1)
            for i in range(2):
                dve.tensor_tensor_scan(la_c[:, T * i:T * i + T], scanmask[:, :], la_x[:, T * i:T * i + T], 0.0,
                                       ALU.mult, ALU.add).then_inc(s("lac"), 1)
            dve.wait_ge(s("lac"), 2)
            c8 = la_c.rearrange("p (c t) -> p c t", t=CHUNK)
            tt(e_out.rearrange("p (c t) -> p c t", t=CHUNK), c8[:, :, CHUNK - 1:CHUNK].broadcast_to([P, 8, CHUNK]), c8,
               ALU.subtract).then_inc(s("lad"), 1)
            dve.wait_ge(s("gqk"), 2)
            dve.wait_ge(s("lax_e"), 2)
            stt(gq_s, gq_s, float(DK ** -0.5), e_pos, ALU.mult, ALU.mult).then_inc(s("gin"), 1)
            tt(k_in, gk_s, e_neg, ALU.mult).then_inc(s("gin"), 1)
            dve.wait_ge(s("lax_e"), 3)
            tt(gk_s, gk_s, e_out, ALU.mult).then_inc(s("gin"), 1)

            def head_norm(i, name, gain, dst):
                if i:
                    dve.wait_ge(s("nq"), i)
                rms(f"nr{i}", 512, "nrs")
                dve.wait_ge(s("nrs"), i + 1)
                stt(dst.rearrange("p k t -> p (k t)"), ps(name)[:, :], gain, rs[:, :], ALU.mult, ALU.mult).then_inc(s("nq"), 1)

            job_wait(dve, "cs1")
            cs0 = ps("cs0")[:, :].rearrange("p (c m v) -> p c m v", c=2, m=2)
            cs1 = ps("cs1")[:, 0:256].rearrange("p (m v) -> p m v", m=2)
            dve.tensor_copy(state[:, 0], cs0[:, 0]).then_inc(s("gst"), 1)
            for c in (1, 2):
                dve.wait_ge(s("gst"), 2 * c - 1)
                for m in range(2):
                    at = T * m + CHUNK * c + CHUNK - 1
                    stt(state[:, c, m], state[:, c - 1, m], e_pos[:, at:at + 1], cs1[:, m] if c == 1 else cs0[:, 1, m],
                        ALU.mult, ALU.add).then_inc(s("gst"), 1)
            dve.wait_ge(s("gqs"), 2)
            for j in range(2):
                head_norm(j, f"fq{j}", gsc[:, 0:1], fq_n[:, 2 * j:2 * j + 2, :])
            dve.wait_ge(s("late"), 80)
            dve.wait_ge(s("atz"), 1)
            for i in range(2):
                job_wait(dve, f"at{i}")
                dve.copy_predicated(att[:, 4 * i:4 * i + 4, :], glamask.unsqueeze(1).broadcast_to([P, 4, P]),
                                    ps(f"at{i}")[:, :].rearrange("p (k t) -> p k t", k=4)).then_inc(s("atc"), 1)

            def gla_out(j):
                rms(f"gor{j}", 512, "gors")
                dve.wait_ge(s("gors"), j + 1)
                for i in range(2):
                    hd = j + 2 * i
                    stt(go_n[:, hd, :], ps2(f"go{j}")[:, i, :], col("g_gla", hd), rs[:, T * i:T * i + T], ALU.mult, ALU.mult).then_inc(s("gon"), 1)
                dve.wait_ge(s("gon"), 2 * j + 2)
                dve.wait_ge(s("ggs"), 2)
                tt(ys[0][:, j::2, :], go_n[:, j::2, :], gg_s[:, j::2, :], ALU.mult).then_inc(s("ygla"), 1)

            gla_out(0)
            for j in range(2):
                head_norm(2 + j, f"fk{j}", col("g_fk"), fk_n[:, 2 * j:2 * j + 2, :])
            gla_out(1)

            def fox_rows(hd):
                if hd >= 2:
                    job_wait(dve, f"us{hd - 2}")
                ts(fa[hd % 2][0:32, :], tmp[0:32, 1792:2048], ident[0:32, hd:hd + 1], None, ALU.mult).then_inc(s("fa"), 1)
                ts(fa[hd % 2][32:64, :], scan_ones, ident[32:64, 32 + hd:33 + hd], None, ALU.mult).then_inc(s("fa"), 1)

            scan_ones = tmp[32:64, 1536:1792]
            dve.memset(scan_ones, 1.0).then_inc(s("pick1"), 1)
            dve.wait_ge(s("pick1"), 1)
            fox_rows(0)
            for u in range(9):
                if u < 8:
                    if u + 1 < 4:
                        fox_rows(u + 1)
                    job_wait(dve, f"us{u}")
                    if u >= 1:
                        dve.wait_ge(s("ue"), 2 * u)
                    if u < 4:
                        tt(logits, ps2(f"us{u}"), foxmask, ALU.add).then_inc(s("ul"), 1)
                    else:
                        dve.tensor_copy(logits, ps2(f"us{u}")).then_inc(s("ul"), 1)
                    dve.wait_ge(s("ul"), u + 1)
                    dve.tensor_reduce(small[:, 0:2], logits, AX_X, ALU.max).then_inc(s("umx"), 1)
                    dve.wait_ge(s("umx"), u + 1)
                    ts(small[:, 2:4], small[:, 0:2], -1.0, None, ALU.mult).then_inc(s("unm"), 1)
                    dve.wait_ge(s("ue"), 2 * u + 2)
                    dve.reciprocal(small[:, 6:8], small[:, 4:6]).then_inc(s("urc"), 1)
                    dve.wait_ge(s("urc"), u + 1)
                    for i in range(2):
                        ts(probs[u % 2][:, i, :], probs[u % 2][:, i, :], small[:, 6 + i:7 + i], None, ALU.mult).then_inc(s("up"), 1)
                if u == 0:
                    for j in range(2):
                        head_norm(4 + j, f"mq{j}", gsc[:, 1:2], mq_n[:, 2 * j:2 * j + 2, :])
            for n in range(12):
                i, p = divmod(n, 4)
                job_wait(dve, f"br{i}.{p}")
                m = KT * i + 2 * p
                dve.wait_ge(s("gate"), m + 2)
                if i == 2:
                    dve.wait_ge(s("mga"), p + 1)
                dst = (yt3 if i == 0 else tmp3)[:, 2 * p:2 * p + 2, :]
                tt(dst, ps2(f"br{i}.{p}"), gates[:, m:m + 2, :], ALU.mult).then_inc(s("mgm"), 1)
            for u in range(3):
                split_low(LAST + u)
            residual(4, "w2o", None)
            norm(6)
            for u, name in enumerate(last_jobs):
                i = int(name[2:])
                if name[:2] == "fu":
                    dve.wait_ge(s("fsil"), i + 1)
                    job_wait(dve, name)
                    tt(big[:, 512 * i:512 * i + 512], ps(name)[:, :], tmp[:, 512 * (i % 4):512 * (i % 4) + 512], ALU.mult).then_inc(s("fact"), 1)
                split_low(LAST + u + 3)
                if name[:2] == "fu":
                    act_low(16 + i)
            for u in range(DOWN + 3, len(units)):
                split_low(u)
            residual(5, "fd", None)

        @block.tensor
        def _(pe):
            at = [0]

            def begin(name):
                i = INDEX[name]
                assert at[0] == i, (name, JOBS[at[0]])
                at[0] += 1
                if name not in TURN:
                    if int(name[3:]) >= 2:
                        pe.wait_ge(s("mod"), int(name[3:]) - 1)
                elif TURN[name] >= BANKS:
                    sem, n = freed[ROTATING[TURN[name] - BANKS]]
                    pe.wait_ge(s(sem), n)

            def end(mm):
                mm.then_inc(s("job"), 1)

            def panel(name):
                i = place[name]
                pe.wait_ge(s(f"panel{i % RING}"), 16 * (i // RING + 1))
                return panel_view(name)

            def mm(*args, **kw):
                return pe.matmul(*args, skip_group_check=True, **kw)

            def project(name, w, m0, src, ready, tiles=2):
                begin(name)
                for i in range(tiles):
                    c = (m0 + i) * P
                    for k in range(KT):
                        ready(k)
                        last = mm(ps2(name)[:, i, :], w[:, k, c:c + P], src[:, k, :], start=(k == 0), stop=(k == KT - 1))
                end(last)

            def project_nat(name, w, i, src):
                begin(name)
                for k in range(KT):
                    last = mm(ps(name)[:, :], src[:, k, P * i:P * i + P], w[:, k, :], start=(k == 0), stop=(k == KT - 1))
                end(last)

            def rows_job(names, panel_name, blocks, src, ready):
                for name in names:
                    begin(name)
                kt = 0
                for b in range(blocks):
                    w = panel(f"{panel_name}{b}")
                    nk = w.shape[1]
                    for m in range(KT):
                        for k in range(nk):
                            ready(kt + k)
                            last = mm(ps2(names[m // 2])[:, m % 2, :], w[:, k, P * m:P * m + P], src[:, kt + k, :],
                                      start=(kt + k == 0 and m % 2 == 0), stop=(b == blocks - 1 and k == nk - 1))
                        if b == blocks - 1 and m % 2 == 1:
                            end(last)
                    if b < blocks - 1:
                        last.then_inc(s("row_panel"), 1)
                    kt += nk

            def three(out_, high, low, x_high, x_low, start, stop):
                mm(out_, high, x_high, start=start, stop=False)
                mm(out_, high, x_low, start=False, stop=False)
                return mm(out_, low, x_high, start=False, stop=stop)

            def project_split(name, u, ready):
                begin(name)
                pe.wait_ge(s("w_low"), u + 1)
                _, low, high = unit_parts(u)
                for i in range(2):
                    for k in range(KT):
                        ready(k)
                        c = slice(P * i, P * i + P)
                        last = three(ps2(name)[:, i, :], high[:, k, c], low[:, k, c], h_hi[:, k, :], h_lo[:, k, :], k == 0, k == KT - 1)
                end(last)

            def rows_split(names, u0, blocks, ready):
                for name in names:
                    begin(name)
                kt = 0
                for b in range(blocks):
                    for half in range(2):
                        u = u0 + 2 * b + half
                        pe.wait_ge(s("w_low"), u + 1)
                        _, low, high = unit_parts(u)
                        nk = low.shape[1]
                        for i in range(4):
                            m = 4 * half + i
                            for k in range(nk):
                                ready(kt + k)
                                c = slice(P * i, P * i + P)
                                last = three(ps2(names[m // 2])[:, m % 2, :], high[:, k, c], low[:, k, c],
                                             big_hi(kt + k)[:, 0, :], big_lo[:, kt + k, :],
                                             kt + k == 0 and m % 2 == 0, b == blocks - 1 and k == nk - 1)
                            if b == blocks - 1 and m % 2 == 1:
                                end(last)
                        if b < blocks - 1:
                            last.then_inc(s("row_panel" if half else "row_half"), 1)
                    kt += nk

            def ada(k):
                begin(f"ada{k}")
                pe.wait_ge(s("ada_acc"), k + 1)
                for i in range(4):
                    last = mm(ps(f"ada{k}")[:, i:i + 1], accb[:, 512 * (k % 2) + P * i:512 * (k % 2) + P * i + P], one[:, :], start=(i == 0), stop=(i == 3))
                end(last)

            def mean_squares(n):
                begin(f"ms{n}")
                for k in range(KT):
                    pe.wait_ge(s("sq"), 4 * n + k // 2 + 1)
                    last = mm(ps(f"ms{n}")[:, 0:T], inv1024, sq3[:, k, :], start=(k == 0), stop=(k == KT - 1))
                end(last)

            def mean(name, m, src, width=512):
                begin(name)
                end(mm(ps(name)[:, 0:width], m, src, start=True, stop=True))

            def h_ready(n):
                if n < 4:
                    return lambda k: pe.wait_ge(s("h"), 8 * n + k + 1)
                return lambda k: pe.wait_ge(s("hn"), 8 * n + k + 1)

            def no_wait(k):
                return None

            pe.wait_ge(s("pool_const"), 6)
            for k in range(4):
                ada(k)
            mean_squares(0)
            w = panel("av")
            project("av0", w, 0, h, h_ready(0))
            ada(4)
            project("av1", w, 2, h, no_wait)
            ada(5)
            w = panel("ag")
            project("ag0", w, 0, h, no_wait)
            ada(6)
            project("ag1", w, 2, h, no_wait)
            ada(7)
            w = panel("q")
            project("q0", w, 0, h, no_wait)
            ada(8)
            project("q1", w, 2, h, no_wait)
            w = panel("k")
            project("k0", w, 0, h, no_wait)
            project("k1", w, 2, h, no_wait)
            w = panel("v")
            project_nat("v0", w, 0, h)
            project_nat("v1", w, 1, h)
            w = panel("g")
            project("g0", w, 0, h, no_wait)
            project("g1", w, 2, h, no_wait)
            begin("mu")
            for i in range(4):
                pe.wait_ge(s("conv"), 4 * (TAPS - 1) + i + 1)
                last = mm(ps("mu")[:, 0:T], inv512, conv[:, i, :], start=(i == 0), stop=(i == 3))
            end(last)
            pe.wait_ge(s("const_in"), 64)
            for j in range(4):
                pe.wait_ge(s("qkc"), j + 1)
                mean(f"rot{j}", perm, qk[:, 2 * j:2 * j + 2, :].rearrange("p k t -> p (k t)"))
            begin("var")
            for i in range(4):
                pe.wait_ge(s("lnsq"), i // 2 + 1)
                last = mm(ps("var")[:, 0:T], inv512, sq3[:, i, :], start=(i == 0), stop=(i == 3))
            end(last)
            for hd in range(4):
                begin(f"sc{hd}")
                pe.wait_ge(s("rope"), 12)
                for i in range(2):
                    last = mm(ps2(f"sc{hd}")[:, i, :], qk[:, 4 + hd, P * i:P * i + P], qk[:, hd, :], start=True, stop=True)
                end(last)
            ada(9)
            pe.wait_ge(s("vc"), 2)
            for j in range(2):
                begin(f"ro{j}")
                for i in range(2):
                    hd = 2 * j + i
                    pe.wait_ge(s("sd"), hd + 1)
                    for t in range(2):
                        last = mm(ps2(f"ro{j}")[:, i, :], v_nat[:, t, P * hd:P * hd + P], sd[:, hd, t, :], start=(t == 0), stop=(t == 1))
                end(last)
                pe.wait_ge(s("rsq"), j + 1)
                mean(f"rr{j}", inv128, sq[:, 1024 + 512 * j:1536 + 512 * j])

            def cat_ready(k):
                pe.wait_ge(s("yconv") if k < 4 else s("ry"), k + 1 if k < 4 else (k - 4) // 2 + 1)

            for i in range(2):
                w = panel(f"wo{i}")
                for j in range(2):
                    project(f"wo0.{2 * i + j}", w, 2 * j, yt3, cat_ready)
            mean_squares(1)

            for i in range(8):
                w = panel(f"f1.0.{i}")
                for j in range(2 * i, 2 * i + 2):
                    project(f"f1.0.{j}", w, 2 * (j % 2), h, h_ready(1) if j == 0 else no_wait)
                    if j >= 2:
                        ada(8 + j)
            rows_job([f"f2.0.{p}" for p in range(4)], "f2.0.", 8, big3, lambda k: pe.wait_ge(s("fsq"), k // 2 + 1))
            mean_squares(2)
            def memory(n):
                if n == 8:
                    begin("mms")
                    for k in range(KT):
                        pe.wait_ge(s("msq"), k // 2 + 1)
                        last = mm(ps("mms")[:, 0:T], inv1024, mem_sq[:, T * k:T * k + T], start=(k == 0), stop=(k == KT - 1))
                    end(last)
                if n in (16, 24):
                    project(f"mk{(n - 16) // 8}", panel("mk"), (n - 16) // 4, mem_x, lambda k: pe.wait_ge(s("memn"), k + 1))
                if n in (18, 26):
                    j = (n - 18) // 8
                    pe.wait_ge(s("mksq"), j + 1)
                    mean(f"mkr{j}", inv128, mem_sq[:, 512 * j:512 * j + 512])
                if n in (32, 40):
                    project_nat(f"mv{(n - 32) // 8}", panel("mv"), (n - 32) // 8, mem_x)

            pe.wait_ge(s("bc_in"), 48)
            for n in range(67):
                if n < 64:
                    k, q, d = n // 8, n // 2 % 4, n % 2
                    begin(f"bu{n}")
                    pe.wait_ge(s("ur") if d else s("h"), k + 1 if d else 16 + k + 1)
                    u = (u_rev if d else h)[32 * q:32 * q + 32, k, :]
                    for r in range(2):
                        last = mm(ps2(f"bu{n}")[:, r, :], b_w[32 * q:32 * q + 32, k, d, r, :], u, start=True, stop=True)
                    end(last)
                    memory(n)
                if n >= 3:
                    m = n - 3
                    k, q, d = m // 8, m // 2 % 4, m % 2
                    if m == 0:
                        pe.wait_ge(s("cw"), 12)
                    if k >= 2 and m % 8 == 0:
                        pe.wait_ge(s("s5z"), k - 1)
                    pe.wait_ge(s("s5q"), m + 1)
                    pe.wait_ge(s("s5r"), m + 1)
                    for f in range(2):
                        for r in range(2):
                            last = mm(bank[6 + k % 2][32 * q:32 * q + 32, 0:T], c_w[:, 32 * d + 4 * k + q, r, :],
                                      qbuf[m % 4][:, f, r, :], start=(d == 0 and f == 0 and r == 0),
                                      stop=(d == 1 and f == 1 and r == 1))
                    last.then_inc(s("s5y"), 1)
            for i in range(2):
                for t in "ab":
                    w = panel(f"g{t}{i}")
                    for j in range(2):
                        project(f"g{t}{2 * i + j}", w, 2 * j, yt3, (lambda k: pe.wait_ge(s("z"), k + 1)) if i == 0 else no_wait)
            mean_squares(3)
            for j in range(16):
                project_split(f"f1.1.{j}", j, (lambda k: pe.wait_ge(s("h_low"), k + 1)) if j == 0 else no_wait)
            rows_split([f"f2.1.{p}" for p in range(4)], 16, 8, lambda k: pe.wait_ge(s("a_low"), k // 2 + 1))
            mean_squares(4)
            mean_squares(5)
            w = panel("gqk")
            project("gq0", w, 0, h, h_ready(5))
            project("gk0", w, 2, h, no_wait)
            pe.wait_ge(s("late"), 80)
            for name, c0, m in (("ga1r", 64, 16), ("ff", 0, 64)):
                begin(name)
                for k in range(KT):
                    last = mm(ps(name)[0:m, 0:T], wsm[:, k, c0:c0 + m], h[:, k, :], start=(k == 0), stop=(k == KT - 1))
                end(last)
            w = panel("gv")
            project_nat("gv0", w, 0, h)
            project_nat("gv1", w, 1, h)
            begin("la")
            pe.wait_ge(s("ga1c"), 1)
            for i in range(2):
                last = mm(ps2("la")[:, i, :], wa2[:, P * i:P * i + P], ga1_s, start=True, stop=True)
            end(last)
            for name, w_name in (("gg", "gg"), ("fq", "fq")):
                w = panel(w_name)
                for j in range(2):
                    project(f"{name}{j}", w, 2 * j, h, no_wait)
            begin("kot")
            pe.wait_ge(s("gin"), 3)
            for t in range(2):
                for m in range(2):
                    last = pe.transpose(ps("kot")[:, 256 * t + P * m:256 * t + P * m + P], gk_s[:, T * m + P * t:T * m + P * t + P], ident[:, :])
            end(last)
            pe.wait_ge(s("koc"), 1)
            pe.wait_ge(s("gvc"), 2)
            for name, chunks in (("cs0", (0, 2)), ("cs1", (1,))):
                begin(name)
                for c in chunks:
                    r0 = CHUNK * (c % 2)
                    for hd in range(4):
                        m, p0 = hd // 2, DK * (hd % 2)
                        o = 256 * (c // 2) + P * m
                        last = mm(ps(name)[p0:p0 + DK, o:o + P], ko_nat[r0:r0 + CHUNK, 256 * (c // 2) + DK * hd:256 * (c // 2) + DK * hd + DK],
                                  gv_nat[r0:r0 + CHUNK, c // 2, P * hd:P * hd + P], start=True, stop=True)
                end(last)

            def head_mean(i):
                pe.wait_ge(s("nsq"), i + 1)
                mean(f"nr{i}", inv128, sq[:, 512 * (i % 2):512 * (i % 2) + 512])

            head_mean(0)
            head_mean(1)
            for odd in range(2):
                begin(f"at{odd}")
                for t in range(2):
                    for m in range(2):
                        c = slice(T * m + P * t, T * m + P * t + P)
                        last = mm(ps(f"at{odd}")[:, 256 * t + P * m:256 * t + P * m + P], k_in[DK * odd:DK * odd + DK, c],
                                  gq_s[DK * odd:DK * odd + DK, c], start=True, stop=True)
                end(last)
            w = panel("fk")
            for j in range(2):
                project(f"fk{j}", w, 2 * j, h, no_wait)

            def gla_out(j):
                begin(f"go{j}")
                pe.wait_ge(s("atc"), 2)
                pe.wait_ge(s("gst"), 5)
                for i in range(2):
                    hd = j + 2 * i
                    m, p0 = i, DK * j
                    for t in range(2):
                        mm(ps2(f"go{j}")[:, i, P * t:P * t + P], gv_nat[:, t, P * hd:P * hd + P], att[:, 4 * j + 2 * t + i, :],
                           start=(i == 0 and t == 0), stop=False)
                    for c in range(1, 4):
                        last = mm(ps2(f"go{j}")[:, i, CHUNK * c:CHUNK * c + CHUNK], state[p0:p0 + DK, c - 1, m, :],
                                  gq_s[p0:p0 + DK, T * m + CHUNK * c:T * m + CHUNK * c + CHUNK], start=False, stop=(c == 3))
                end(last)
                pe.wait_ge(s("gosq"), j + 1)
                mean(f"gor{j}", inv128, go_sq[:, 512 * j:512 * j + 512])

            gla_out(0)
            head_mean(2)
            head_mean(3)
            gla_out(1)
            w = panel("fv")
            project_nat("fv0", w, 0, h)
            project_nat("fv1", w, 1, h)
            w = panel("mq")
            for j in range(2):
                project(f"mq{j}", w, 2 * j, h, no_wait)

            def gate(j):
                project(f"bg{j}", panel(f"bg{j // 2}"), 2 * (j % 2), h, no_wait)

            for u in range(10):
                if u < 8:
                    begin(f"us{u}")
                    if u < 4:
                        pe.wait_ge(s("nq"), 4)
                        pe.wait_ge(s("fa"), 2 * u + 2)
                        pe.wait_ge(s("fb"), 2)
                    else:
                        pe.wait_ge(s("nq"), 6)
                        pe.wait_ge(s("mkn"), 2)
                    for t in range(2):
                        o = ps2(f"us{u}")[:, t, :]
                        if u < 4:
                            mm(o, fq_n[:, u, P * t:P * t + P], fk_n[:, u, :], start=True, stop=False)
                            last = mm(o, fa[u % 2][:, P * t:P * t + P], fb, start=False, stop=True)
                        else:
                            last = mm(o, mq_n[:, u - 4, P * t:P * t + P], mk_n[:, u - 4, :], start=True, stop=True)
                    end(last)
                gate(u)
                if u == 0:
                    head_mean(4)
                    head_mean(5)
                if 1 <= u <= 8:
                    m = u - 1
                    begin(f"ut{m}")
                    pe.wait_ge(s("up"), 2 * m + 2)
                    for ks in range(2):
                        for t in range(2):
                            last = pe.transpose(ps(f"ut{m}")[:, 256 * ks + P * t:256 * ks + P * t + P], probs[m % 2][:, t, P * ks:P * ks + P], ident[:, :])
                    end(last)
                if u >= 3 and u % 2 == 1:
                    j = (u - 3) // 2
                    begin(f"uo{j}")
                    v = fv_nat if j < 2 else mv_nat
                    pe.wait_ge(s("fvc") if j < 2 else s("mvc"), 2)
                    for i in range(2):
                        m = 2 * j + i
                        hd = m % 4
                        pe.wait_ge(s("upt"), m + 1)
                        for ks in range(2):
                            last = mm(ps2(f"uo{j}")[:, i, :], v[:, ks, P * hd:P * hd + P], prob_t[m % 2][:, ks, :], start=(ks == 0), stop=(ks == 1))
                    end(last)
            gate(10)
            gate(11)
            for i in range(3):
                pe.wait_ge(s("ygla") if i == 0 else s("uoc"), (2, 2, 4)[i])
                w = panel(f"br{i}.0")
                for p in range(4):
                    begin(f"br{i}.{p}")
                    for j in range(2):
                        m = 2 * p + j
                        for k in range(4):
                            last = mm(ps2(f"br{i}.{p}")[:, j, :], w[:, k, P * m:P * m + P], ys[i][:, k, :], start=(k == 0), stop=(k == 3))
                    end(last)
            for i in range(2):
                w = panel(f"w2o{i}")
                for j in range(2):
                    project(f"w2o.{2 * i + j}", w, 2 * j, yt3, lambda k: pe.wait_ge(s("mga"), 4 + k // 2 + 1))
            mean_squares(6)
            for u, name in enumerate(last_jobs):
                project_split(name, LAST + u, (lambda k: pe.wait_ge(s("h_low"), 8 + k + 1)) if u == 0 else no_wait)
            rows_split([f"fd.{p}" for p in range(4)], DOWN, 6, lambda k: pe.wait_ge(s("a_low"), 16 + k // 2 + 1))
            assert at[0] == len(JOBS)


def shape_constants():
    f = np.float32
    inv = (np.float64(10000.0) ** (-np.arange(0, P, 2) / P)).astype(f)
    ang = (np.arange(T, dtype=f)[:, None] * inv[None, :]).astype(f)
    cos, sin = np.cos(ang).astype(f).T, np.sin(ang).astype(f).T
    perm = np.zeros((P, P), f)
    half = P // 2
    perm[np.arange(half) + half, np.arange(half)] = -1.0
    perm[np.arange(half), np.arange(half) + half] = 1.0
    rope = np.concatenate([np.concatenate([cos, cos]), np.concatenate([sin, sin]), perm], 1)
    log_g = np.log1p(-np.exp2(-5.0 - np.arange(HEADS)))
    m = np.arange(T).reshape(2, P)
    dist = np.abs(m[:, :, None] - np.arange(T)[None, None, :])
    decay = np.exp(log_g[:, None, None, None] * dist[None]) * P ** -0.5
    decay = decay.transpose(2, 0, 1, 3).reshape(P, -1)
    q = np.arange(T).reshape(2, P)
    fox = np.where(np.arange(T)[None, None, :] <= q[:, :, None], 0.0, NEG).transpose(1, 0, 2).reshape(P, -1)
    i = np.arange(P)
    gla = (i[:, None] <= i[None, :]) & (i[:, None] // CHUNK == i[None, :] // CHUNK)
    scan = np.broadcast_to((np.arange(T) % CHUNK != 0), (P, T))
    return {"rope": rope.astype(f), "decay": decay.astype(f), "foxmask": fox.astype(f), "glamask": gla.astype(np.int32),
            "scanmask": scan.astype(f), "ident": np.eye(P, dtype=f)}


def kernel(**inp):
    import concourse.bacc as bacc
    from concourse.bass_utils import run_bass_kernel_spmd as run

    inp = {k: np.asarray(v) for k, v in inp.items()}

    def cols_of(v):
        return np.reshape(v, (-1, P)).T

    b_fox = np.zeros((P, 1), np.float32)
    b_fox[0:HEADS, 0] = inp["b_fox_f_2"][0]
    b_fox[32:32 + HEADS, 0] = inp["b_fox_f_2"][0]
    pack = {
        "c": cols_of(inp["c"]), "norm_g": cols_of(inp["norm_g"]), "ada_b": cols_of(inp["ada_b"]),
        "conv_w": inp["conv_w"][0].reshape(TAPS, 4, P).transpose(2, 1, 0).reshape(P, -1), "conv_b": cols_of(inp["conv_b"]),
        "cln_g": cols_of(inp["cln_g"]), "cln_b": cols_of(inp["cln_b"]), "s5_d": cols_of(inp["s5_d"]),
        "norm_f": cols_of(inp["norm_f"]), "g_mix": cols_of(inp["g_mix_2"]), "b_gla": cols_of(inp["b_gla_a_2"]),
        "g_gla": cols_of(inp["g_gla_out_2"]), "g_fq": cols_of(inp["g_fox_q_2"]), "g_fk": cols_of(inp["g_fox_k_2"]),
        "g_mem": cols_of(inp["g_mem_2"]), "g_mq": cols_of(inp["g_mem_q_2"]), "g_mk": cols_of(inp["g_mem_k_2"]),
        "b_gate": cols_of(inp["b_gate_2"]), "g_ffn": cols_of(inp["g_ffn_2"]), "b_fox": b_fox,
    }
    cols = np.concatenate([pack[name] for name in COLS], 1)

    def states(v):
        return v.reshape(2, 32, 2, 64).transpose(2, 3, 0, 1).reshape(P, 64)

    step = np.repeat(inp["s5_log_step"][0][:, :, None], 64, 2)
    scal = np.concatenate([states(inp["s5_lam_re"][0]), states(inp["s5_lam_im"][0]), states(step)], 1)
    bw = np.zeros((4, 2, 16, 8, 2, 2, 2, 64), np.float32)
    cw = np.zeros((2, 64, 2, 2, 32, 2, 16), np.float32)
    for r, (bn, cn) in enumerate((("s5_b_re", "s5_c_re"), ("s5_b_im", "s5_c_im"))):
        b = inp[bn][0].reshape(2, 8, 4, 2, 64, 16)
        c = inp[cn][0].reshape(2, 32, 2, 16, 64)
        for g in range(2):
            bw[:, g, :, :, :, r, g, :] = b[:, :, :, g].transpose(2, 4, 1, 0, 3)
            cw[g, :, r, :, :, g, :] = c[:, :, g].transpose(3, 0, 1, 2)
    w_fox = np.zeros((D, 64), np.float32)
    w_fox[:, 0:HEADS] = inp["w_in_2"][0][:, FFG:FFG + HEADS]
    w_fox[:, 32:32 + HEADS] = inp["w_in_2"][0][:, FFG:FFG + HEADS]
    arrays = {
        "x": inp["x"][0].T, "mem": inp["mem_2"][0].T, "cols": cols, "s5_scal": scal,
        "s5_b": bw.reshape(P, 4096), "s5_c": cw.reshape(P, 2, 2048), "w_fox_f": w_fox,
        "ada_w": inp["ada_w"], "w_in": inp["w_in"][0], "w_out": inp["w_out"][0], "w_fc1": inp["w_fc1"], "w_fc2": inp["w_fc2"],
        "w_glu_a": inp["w_glu_a"][0], "w_glu_b": inp["w_glu_b"][0], "w_in_2": inp["w_in_2"][0], "w_mem_kv": inp["w_mem_kv_2"][0],
        "w_gla_a2": inp["w_gla_a2_2"][0], "w_branch": inp["w_branch_2"][0], "w_out_2": inp["w_out_2"][0],
        "w_ffn_gate": inp["w_ffn_gate_2"][0], "w_ffn_up": inp["w_ffn_up_2"][0], "w_ffn_down": inp["w_ffn_down_2"][0],
    }
    arrays.update(shape_constants())
    arrays = {k: np.ascontiguousarray(v) for k, v in arrays.items()}
    nc = bacc.Bacc("TRN2", target_bir_lowering=False, num_devices=1)
    aps = {k: nc.dram_tensor(f"in_{k}", v.shape, mybir.dt.from_np(v.dtype), kind="ExternalInput").ap() for k, v in arrays.items()}
    out = nc.dram_tensor("out_t", (D, T), F32, kind="ExternalOutput").ap()
    build(nc, aps, out)
    r = run(nc, [{f"in_{k}": v for k, v in arrays.items()}], core_ids=[0])
    return np.ascontiguousarray(np.asarray(r.results[0]["out_t"]).T)[None]
```

```python
from contextlib import ExitStack

import numpy as np

import concourse.bass as bass
from concourse import mybir

F32 = mybir.dt.float32
I32 = mybir.dt.int32
F32R = mybir.dt.float32r
ALU = mybir.AluOpType
ACT = mybir.ActivationFunctionType
AX_X = mybir.AxisListType.X

P = 128
T = 256
D = 1024
KT = D // P
EPS = 1e-6
RING = 4
SLOT = 4096
FF1 = 4096
FF2 = 2816
TAPS = 31
HEADS = 4
DK = 64
CHUNK = 64
NEG = -3.0e38
TWO_PI_A = 6.28125
TWO_PI_B = float(np.float32(np.round((2 * np.pi - 6.28125) * 2.0 ** 21) / 2.0 ** 21))
TWO_PI_C = 2 * np.pi - TWO_PI_A - TWO_PI_B
ROUND = 12582912.0
ADA = 12
PI_SAFE = 3.1415925
SW_ADA = 10

COLS = {}
_at = 0
for _name, _n in (("c", 8), ("norm_g", 32), ("ada_b", 96), ("conv_w", 4 * TAPS), ("conv_b", 4), ("cln_g", 4),
                  ("cln_b", 4), ("s5_d", 8), ("norm_f", 8), ("g_mix", 8), ("b_gla", 2), ("g_gla", 4),
                  ("g_fq", 1), ("g_fk", 1), ("g_mem", 8), ("g_mq", 1), ("g_mk", 1), ("b_gate", 24),
                  ("g_ffn", 8), ("b_fox", 1)):
    COLS[_name] = _at
    _at += _n
NCOLS = _at
GQ, GV, GG, GA, FQ, FK, FV, FFG, MQ, BG = 0, 512, 1024, 1536, 1552, 2064, 2576, 3088, 3092, 3604


def job_order():
    jobs = [f"ada{k}" for k in range(4)] + ["ms0"]
    jobs += ["av0", "av1", "ag0", "ada4", "ag1", "ada5", "q0", "ada6", "q1", "ada7", "k0", "k1",
             "v0", "v1", "g0", "g1", "mu", "rot0", "rot1", "rot2", "rot3", "var"]
    jobs += ["sc0", "sc1", "sc2", "sc3", "ro0", "rr0", "ro1", "rr1",
             "wo0.0", "ada8", "wo0.1", "ada9", "wo0.2", "wo0.3", "ms1"]
    for j in range(16):
        jobs.append(f"f1.0.{j}")
        if 2 <= j < 16:
            jobs.append(f"ada{8 + j}")
    jobs += [f"f2.0.{p}" for p in range(4)] + ["ms2"]
    fill = {7: "mms", 19: "mk0", 22: "mkr0", 29: "mk1", 32: "mkr1", 39: "mv0", 47: "mv1"}
    for n in range(64):
        jobs.append(f"bu{n}")
        if n in fill:
            jobs.append(fill[n])
    jobs += ["ga0", "ga1", "gb0", "gb1", "ga2", "ga3", "gb2", "gb3", "ms3"]
    jobs += [f"f1.1.{j}" for j in range(16)] + [f"f2.1.{p}" for p in range(4)] + ["ms4", "ms5"]
    jobs += ["gq0", "gk0", "ga1r", "ff", "gv0", "gv1", "la", "gg0", "gg1", "fq0", "fq1", "kot", "cs0", "cs1",
             "nr0", "nr1", "at0", "at1", "fk0", "fk1", "go0", "gor0", "nr2", "nr3", "go1", "gor1",
             "fv0", "fv1", "mq0", "mq1"]
    bg = 0
    for u in range(10):
        if u < 8:
            jobs.append(f"us{u}")
        jobs.append(f"bg{bg}")
        bg += 1
        if u == 0:
            jobs += ["nr4", "nr5"]
        if 1 <= u <= 8:
            jobs.append(f"ut{u - 1}")
        if u >= 3 and u % 2 == 1:
            jobs.append(f"uo{(u - 3) // 2}")
    jobs += ["bg10", "bg11"]
    jobs += [f"br{i}.{p}" for i in range(3) for p in range(4)] + [f"w2o.{p}" for p in range(4)] + ["ms6"]
    for p in range(6):
        n = 2 if p < 5 else 1
        jobs += [f"fg{2 * p + i}" for i in range(n)] + [f"fu{2 * p + i}" for i in range(n)]
    jobs += [f"fd.{p}" for p in range(4)]
    return jobs


JOBS = job_order()
INDEX = {name: i for i, name in enumerate(JOBS)}
ROOTS = ["ms0", "var", "rr0", "rr1", "ms1", "ms2", "mms", "mkr0", "mkr1", "ms3", "ms4", "ms5", "nr0", "nr1", "gor0",
         "nr2", "nr3", "gor1", "nr4", "nr5", "ms6"]
BANKS = 6
ROTATING = [name for name in JOBS if not name.startswith("ada")]
TURN = {name: i for i, name in enumerate(ROTATING)}


def build(nc, a, out):
    ctx = ExitStack()
    with ctx:
        def sb(name, free, dt=F32, parts=P):
            return ctx.enter_context(nc.sbuf_tensor(name, [parts, free], dt))

        sems = {}

        def s(name):
            if name not in sems:
                sems[name] = ctx.enter_context(nc.semaphore("s_" + name))
            return sems[name]

        shared = [(f"ring{i}", SLOT) for i in range(RING)] + [(f"ada_slot{i}", SLOT) for i in range(2)]
        shared += [("h_in", KT * T), ("squares", KT * T), ("tmp", KT * T), ("y_cat", KT * T), ("big", 32 * T),
                   ("decay_or_mem", 2048), ("tabw", 3072), ("ada_acc", 1024)]
        with ExitStack() as first:
            plain = {name: first.enter_context(nc.sbuf_tensor(name, [P, free], F32)) for name, free in shared}
        split = {name: sb(name + "_split", free, F32R) for name, free in shared}
        ring = [plain[f"ring{i}"] for i in range(RING)]
        adas = [plain[f"ada_slot{i}"] for i in range(2)]
        x = sb("x_res", KT * T)[:, :].rearrange("p (k t) -> p k t", k=KT)
        h = plain["h_in"][:, :].rearrange("p (k t) -> p k t", k=KT)
        sq, tmp, yt, big = plain["squares"], plain["tmp"], plain["y_cat"], plain["big"]
        dreg, tabw = plain["decay_or_mem"], plain["tabw"]
        accb = plain["ada_acc"]
        rs = sb("rstd", 512)
        early = sb("early", 1984)
        scanmask = sb("scanmask", T)
        ident = sb("ident", P)
        inv = sb("inv", 3 * P)
        one = sb("one", 1)
        eps = sb("eps", 1)
        cols = sb("cols", NCOLS)
        mod = sb("mod", 96)
        gs = sb("gs", 8)
        cact = sb("cact", 8)
        gsc = sb("gsc", 2)
        small = sb("small", 8)
        bank = [ctx.enter_context(nc.psum_tensor(f"bank{i}", [P, 512], F32)) for i in range(8)]

        def col(name, i=0, n=1):
            return cols[:, COLS[name] + i:COLS[name] + i + n]

        inv1024, inv512, inv128 = (inv[:, i * P:(i + 1) * P] for i in range(3))
        sq3 = sq[:, :].rearrange("p (k t) -> p k t", k=KT)
        yt3 = yt[:, :].rearrange("p (k t) -> p k t", k=KT)
        big3 = big[:, :].rearrange("p (k t) -> p k t", k=32)
        tmp3 = tmp[:, :].rearrange("p (k t) -> p k t", k=KT)

        def ps(name):
            return bank[TURN[name] % BANKS] if name in TURN else bank[BANKS + int(name[3:]) % 2]

        def ps2(name):
            return ps(name)[:, :].rearrange("p (k t) -> p k t", k=2)

        APW = T + TAPS - 1
        a_pad = big[:, 0:4 * APW].rearrange("p (k t) -> p k t", k=4)
        conv = big[:, 1152:2176].rearrange("p (k t) -> p k t", k=4)
        a_sig = big[:, 2176:3200].rearrange("p (k t) -> p k t", k=4)
        qk = big[:, 3200:5248].rearrange("p (k t) -> p k t", k=8)
        v_nat = big[:, 5248:6272].rearrange("p (k t) -> p k t", k=2)
        g_silu = big[:, 6272:7296].rearrange("p (k t) -> p k t", k=4)
        cos_t, sin_t = early[:, 1344:1600], early[:, 1600:1856]
        perm = early[:, 1856:1984]
        dtab = dreg[:, :].rearrange("p (h k t) -> p h k t", h=4, k=2)
        sd = tmp[:, :].rearrange("p (h k t) -> p h k t", h=4, k=2)
        mag, f_re, f_im, nf_re, nf_im = (early[:, 64 * i:64 * i + 64] for i in range(5))
        rotp = early[:, 320:1344].rearrange("p (j c s) -> p j c s", j=8, c=2)
        sc = [tabw[:, 64 * i:64 * i + 64] for i in range(20)]
        tm = tabw[:, 2048:3072].rearrange("p (f s c t) -> p f s c t", f=2, s=4, c=2)
        b_w = adas[0][:, :].rearrange("p (k d c m) -> p k d c m", k=8, d=2, c=2)
        c_w = adas[1][:, :].rearrange("p (s c m) -> p s c m", s=64, c=2)
        TABS = 7
        tab_at = [(tabw, 0), (tabw, 768), (tabw, 1536), (tabw, 2304), (big, 0), (big, 768), (accb, 0)]
        tabs = [buffer[:, o:o + 768].rearrange("p (c t) -> p c t", c=3) for buffer, o in tab_at]
        pbuf = [big[:, 2048 + 1024 * i:3072 + 1024 * i].rearrange("p (f c t) -> p f c t", f=2, c=2) for i in range(2)]
        qbuf = [big[:, 4096 + 1024 * i:5120 + 1024 * i].rearrange("p (f c t) -> p f c t", f=2, c=2) for i in range(2)]
        wbuf = [big[:, 6144 + 512 * i:6656 + 512 * i].rearrange("p (c t) -> p c t", c=2) for i in range(2)]
        gbuf = [big[:, 7168 + 512 * i:7680 + 512 * i].rearrange("p (c t) -> p c t", c=2) for i in range(2)]
        qbuf += [tmp[:, 1024 * i:1024 * i + 1024].rearrange("p (f c t) -> p f c t", f=2, c=2) for i in range(2)]

        def rotated(m):
            return qbuf[m % 4][:, :, :, ::-1] if m % 2 else qbuf[m % 4]
        u_rev = sq3
        mk_n = dreg[:, 0:1024].rearrange("p (k t) -> p k t", k=4)
        mv_nat = dreg[:, 1024:2048].rearrange("p (k t) -> p k t", k=2)
        A0, A1 = adas
        gq_s, gk_s = A0[:, 0:512], A0[:, 512:1024]
        la_x, la_c = A0[:, 1024:1536], A0[:, 1536:2048]
        e_pos, e_neg, e_out, k_in = (A0[:, 2048 + 512 * i:2560 + 512 * i] for i in range(4))
        go_n = A0[:, 1024:2048].rearrange("p (k t) -> p k t", k=4)
        go_sq = A0[:, 2560:3584]
        mq_n = accb[:, :].rearrange("p (k t) -> p k t", k=4)
        ys = [A1[:, 1024 * i:1024 * i + 1024].rearrange("p (k t) -> p k t", k=4) for i in range(3)]
        state = A1[:, 3072:3840].rearrange("p (c m v) -> p c m v", c=3, m=2)
        ga1_s = A1[0:16, 3840:4096]
        gv_nat = big[:, 6144:7168].rearrange("p (k t) -> p k t", k=2)
        gg_s = big[:, 7168:8192].rearrange("p (k t) -> p k t", k=4)
        gates = big3
        att = tmp[:, 0:1024].rearrange("p (k t) -> p k t", k=8)
        ko_nat = tmp[:, 1024:1536]
        ff_x, ff_c = tmp[0:64, 1536:1792], tmp[0:64, 1792:2048]
        fq_n = yt[:, 0:1024].rearrange("p (k t) -> p k t", k=4)
        fk_n = yt[:, 1024:2048].rearrange("p (k t) -> p k t", k=4)
        fv_nat = sq[:, 1024:2048].rearrange("p (k t) -> p k t", k=2)
        wsm = early[:, 0:640].rearrange("p (k c) -> p k c", k=8)
        wa2 = early[0:16, 640:896]
        fb = early[0:64, 896:1152]
        foxmask = early[:, 1152:1664].rearrange("p (k t) -> p k t", k=2)
        glamask = early[:, 1664:1792].bitcast(I32)
        logits = tabw[:, 0:512].rearrange("p (k t) -> p k t", k=2)
        probs = [tabw[:, 512 + 512 * i:1024 + 512 * i].rearrange("p (k t) -> p k t", k=2) for i in range(2)]
        prob_t = [tabw[:, 1536 + 512 * i:2048 + 512 * i].rearrange("p (k t) -> p k t", k=2) for i in range(2)]
        fa = [tabw[0:64, 2560 + 256 * i:2816 + 256 * i] for i in range(2)]

        tab_d = nc.dram_tensor("s5_tables", (64, P, 512), F32, kind="Internal").ap()

        panels = []

        def cols_panel(name, w, c0, n, last_job):
            panels.append((name, w[:, c0:c0 + n].rearrange("(k p) c -> p k c", p=P), KT, n, ("job", last_job)))

        def rows_panels(name, w, rows, last_job):
            k0, i = 0, 0
            while k0 < rows // P:
                nk = min(4, rows // P - k0)
                done = k0 + nk >= rows // P
                panels.append((f"{name}{i}", w[k0 * P:(k0 + nk) * P, :].rearrange("(k p) c -> p k c", p=P), nk, D,
                               ("job", last_job) if done else ("row", None)))
                k0 += nk
                i += 1

        for i, (name, job) in enumerate((("av", "av1"), ("ag", "ag1"), ("q", "q1"), ("k", "k1"), ("v", "v1"), ("g", "g1"))):
            cols_panel(name, a["w_in"], 512 * i, 512, job)
        for i in range(2):
            cols_panel(f"wo{i}", a["w_out"], 512 * i, 512, f"wo0.{2 * i + 1}")

        def ffn_panels(l):
            for i in range(8):
                cols_panel(f"f1.{l}.{i}", a["w_fc1"][l], 512 * i, 512, f"f1.{l}.{2 * i + 1}")
            rows_panels(f"f2.{l}.", a["w_fc2"][l], FF1, f"f2.{l}.3")

        ffn_panels(0)
        panels.append(("mem", a["mem"].rearrange("(k p) t -> p k t", p=P), KT, T, ("job", "mv1")))
        cols_panel("mk", a["w_mem_kv"], 0, 512, "mk1")
        cols_panel("mv", a["w_mem_kv"], 512, 512, "mv1")
        for i in range(2):
            cols_panel(f"ga{i}", a["w_glu_a"], 512 * i, 512, f"ga{2 * i + 1}")
            cols_panel(f"gb{i}", a["w_glu_b"], 512 * i, 512, f"gb{2 * i + 1}")
        ffn_panels(1)
        w2 = a["w_in_2"]
        cols_panel("gqk", w2, GQ, 512, "gk0")
        cols_panel("gv", w2, GV, 512, "gv1")
        cols_panel("gg", w2, GG, 512, "gg1")
        cols_panel("fq", w2, FQ, 512, "fq1")
        cols_panel("fk", w2, FK, 512, "fk1")
        cols_panel("fv", w2, FV, 512, "fv1")
        cols_panel("mq", w2, MQ, 512, "mq1")
        for i in range(6):
            cols_panel(f"bg{i}", w2, BG + 512 * i, 512, f"bg{2 * i + 1}")
        for i in range(3):
            rows_panels(f"br{i}.", a["w_branch"][i], 512, f"br{i}.3")
        for i in range(2):
            cols_panel(f"w2o{i}", a["w_out_2"], 512 * i, 512, f"w2o.{2 * i + 1}")
        for i in range(6):
            n = 512 if i < 5 else 256
            last = 2 * i + 1 if i < 5 else 10
            cols_panel(f"fg{i}", a["w_ffn_gate"], 512 * i, n, f"fg{last}")
            cols_panel(f"fu{i}", a["w_ffn_up"], 512 * i, n, f"fu{last}")
        rows_panels("fd", a["w_ffn_down"], FF2, "fd.3")
        place = {pn[0]: i for i, pn in enumerate(panels)}
        rows_before = []
        count = 0
        for pn in panels:
            count += pn[4][0] == "row"
            rows_before.append(count)

        def panel_view(name):
            i = place[name]
            _, _, k, n, _ = panels[i]
            return ring[i % RING][:, 0:k * n].rearrange("p (k c) -> p k c", k=k)

        units = []

        def add_units(names, width, buffers):
            for name in names:
                n = panels[place[name]][3]
                for c0 in range(0, n, width):
                    units.append((name, c0, width, buffers[(len(units) - base) % 3]))

        base = 0
        FC2 = 2
        add_units([f"f2.0.{b}" for b in range(FC2, 8)], 512, [split[name][:, 0:2048] for name in ("h_in", "y_cat", "tmp")])
        base = GLU = len(units)
        add_units(["ga0", "gb0", "ga1", "gb1"], 256, [split["ada_slot0"][:, 0:2048], split["ada_slot0"][:, 2048:4096],
                                                      split["squares"][:, 0:2048]])
        base = SECOND = len(units)
        high_bufs = [split[name][:, 0:2048] for name in ("tabw", "y_cat", "tmp")]
        add_units([f"f1.1.{i}" for i in range(8)], 256, high_bufs)
        add_units([f"f2.1.{i}" for i in range(8)], 512, high_bufs)
        base = BRANCH = len(units)
        high_bufs = [split["ada_slot0"][:, 0:2048], split["ada_slot0"][:, 2048:4096], split["big"][:, 24 * T:32 * T]]
        add_units([f"br{i}.0" for i in range(3)], 512, high_bufs)
        add_units(["w2o0", "w2o1"], 256, high_bufs)
        branch_ends = [f"br{i}.{p}" for i in range(3) for p in (1, 3)] + [f"w2o.{p}" for p in range(4)]
        base = LAST = len(units)
        high_bufs = [split["decay_or_mem"][:, :], split["tabw"][:, 0:2048], split["ada_slot1"][:, 2048:4096]]
        add_units([f"f{t}{i}" for i in range(6) for t in "gu"], 256, high_bufs)
        DOWN = len(units)
        add_units([f"fd{i}" for i in range(6)], 512, high_bufs)

        def unit_parts(u):
            name, c0, n, buf = units[u]
            i = place[name]
            _, _, k, width, _ = panels[i]
            low = split[f"ring{i % RING}"][:, 0:k * width].rearrange("p (k c) -> p k c", k=k)
            return panel_view(name)[:, :, c0:c0 + n], low[:, :, c0:c0 + n], buf[:, 0:k * n].rearrange("p (k c) -> p k c", k=k)

        ys_hi = [split[name][:, o:o + 1024].rearrange("p (k t) -> p k t", k=4) for name, o in
                 (("squares", 0), ("squares", 1024), ("ada_acc", 0))]
        ys_lo = [split["ada_slot1"][:, 1024 * i:1024 * i + 1024].rearrange("p (k t) -> p k t", k=4) for i in range(3)]
        merged_hi = split["h_in"][:, :].rearrange("p (k t) -> p k t", k=KT)
        merged_lo = split["y_cat"][:, :].rearrange("p (k t) -> p k t", k=KT)
        glu_jobs = ["ga0", "ga1", "gb0", "gb1", "ga2", "ga3", "gb2", "gb3"]
        glu_units = ((3, 4, 5), (6,), (7,), ())
        z_hi = split["h_in"][:, :].rearrange("p (k t) -> p k t", k=KT)
        z_lo = split["y_cat"][:, :].rearrange("p (k t) -> p k t", k=KT)
        h_hi = split["squares"][:, :].rearrange("p (k t) -> p k t", k=KT)
        h_lo = split["h_in"][:, :].rearrange("p (k t) -> p k t", k=KT)
        big_lo = split["big"][:, :].rearrange("p (k t) -> p k t", k=32)

        def fc2_high(b):
            name, o = (("squares", 0), ("squares", 1024), ("ada_acc", 0))[(b - FC2) % 3]
            return split[name][:, o:o + 1024].rearrange("p (k t) -> p k t", k=4)

        def big_hi(m, n=1):
            return split[f"ada_slot{m // 16}"][:, T * (m % 16):T * (m % 16 + n)].rearrange("p (k t) -> p k t", k=n)

        mem_x = panel_view("mem")
        mem_sq = ring[place["mem"] % RING][:, 2048:4096]

        freed = {f"ms{n}": ("rstd", n + 1) for n in range(7)}
        for j in range(2):
            freed.update({f"av{j}": ("amul", j + 1), f"ag{j}": ("agsig", j + 1), f"q{j}": ("qkc", j + 1),
                          f"k{j}": ("qkc", j + 3), f"v{j}": ("vc", j + 1), f"g{j}": ("gsilu", j + 1),
                          f"ro{j}": ("rn", j + 1), f"rr{j}": ("rrs", j + 1)})
            freed.update({f"mk{j}": ("mksq", j + 1), f"mkr{j}": ("mkrs", j + 1), f"mv{j}": ("mvc", j + 1)})
            freed.update({f"gv{j}": ("gvc", j + 1), f"gg{j}": ("ggs", j + 1), f"at{j}": ("atc", j + 1),
                          f"go{j}": ("gon", 2 * j + 2), f"gor{j}": ("gors", j + 1), f"fv{j}": ("fvc", j + 1)})
            freed.update({f"fq{j}": ("nsq", j + 1), f"fk{j}": ("nsq", j + 3), f"mq{j}": ("nsq", j + 5)})
        freed.update({"mu": ("lnxc", 2), "var": ("lnrs", 1), "mms": ("mrs", 1)})
        freed.update({f"rot{j}": ("rope", 3 * j + 2) for j in range(4)})
        freed.update({f"sc{j}": ("sd", j + 1) for j in range(4)})
        for r, name in ((0, "wo0"), (1, "f2.0"), (3, "f2.1"), (4, "w2o"), (5, "fd")):
            freed.update({f"{name}.{p}": ("xres", 8 * r + 2 * p + 2) for p in range(4)})
        freed.update({f"f1.{l}.{j}": ("relu", 16 * l + j + 1) for l in range(2) for j in range(16)})
        freed.update({f"bu{n}": ("s5p", 2 * n + 2) for n in range(64)})
        freed.update({f"ga{p}": ("glut", p + 1) for p in range(4)})
        freed.update({f"gb{p}": ("glus", p + 1) for p in range(4)})
        freed.update({"gq0": ("gqk", 1), "gk0": ("gqk", 2), "ga1r": ("ga1c", 1), "ff": ("ffx", 1), "la": ("lax", 2),
                      "kot": ("koc", 1), "cs0": ("gst", 5), "cs1": ("gst", 3)})
        freed.update({f"nr{i}": ("nrs", i + 1) for i in range(6)})
        freed.update({f"us{u}": ("ul", u + 1) for u in range(8)})
        freed.update({f"ut{u}": ("upt", u + 1) for u in range(8)})
        freed.update({f"uo{j}": ("uoc", j + 1) for j in range(4)})
        freed.update({f"bg{j}": ("gate", 2 * j + 2) for j in range(12)})
        freed.update({f"br{i}.{p}": ("mgm", 4 * i + p + 1) for i in range(3) for p in range(4)})
        freed.update({f"fg{i}": ("fsil", i + 1) for i in range(11)})
        freed.update({f"fu{i}": ("fact", i + 1) for i in range(11)})

        def job_wait(eng, name):
            eng.wait_ge(s("job"), INDEX[name] + 1)

        def unit_wait(eng, u):
            name = units[u][0]
            if SECOND <= u < SECOND + 16:
                job_wait(eng, f"f1.1.{u - SECOND}")
            elif LAST <= u < DOWN:
                job_wait(eng, last_jobs[u - LAST])
            elif GLU <= u < SECOND:
                job_wait(eng, glu_jobs[u - GLU])
            elif BRANCH <= u < LAST:
                job_wait(eng, branch_ends[u - BRANCH])
            else:
                first, before = (0, 0) if u < GLU else (SECOND + 16, 7 - FC2) if u < BRANCH else (DOWN, 14 - FC2)
                if (u - first) % 2 == 0:
                    eng.wait_ge(s("row_half"), before + (u - first) // 2 + 1)
                else:
                    eng.wait_ge(s("row_panel"), rows_before[place[name]])

        last_jobs = [name for name in JOBS if name[:2] in ("fg", "fu")]
        NORM_G = (("norm_g", 0), ("norm_g", 8), ("norm_g", 16), ("norm_g", 24), ("norm_f", 0), ("g_mix", 0), ("g_ffn", 0))

        block = ctx.enter_context(nc.Block())

        @block.sync
        def _(sp):
            sp.dma_start(cols[:, :], a["cols"]).then_inc(s("cols_in"), 16)
            sp.dma_start(x, a["x"].rearrange("(k p) t -> p k t", p=P)).then_inc(s("x_in"), 16)
            for i, (name, src, k, n, _) in enumerate(panels):
                if i >= RING:
                    kind, job = panels[i - RING][4]
                    if kind == "job":
                        job_wait(sp, job)
                    else:
                        sp.wait_ge(s("row_panel"), rows_before[i - RING])
                else:
                    sp.wait_ge(s("ada_acc"), min(i + 2, 4))
                sp.dma_start(panel_view(name), src).then_inc(s(f"panel{i % RING}"), 16)
            for p in range(4):
                sp.wait_ge(s("xres"), 8 * 5 + 2 * p + 2)
                sp.dma_start(out[2 * p * P:(2 * p + 2) * P, :].rearrange("(k p) t -> p k t", p=P),
                             yt3[:, 2 * p:2 * p + 2, :]).then_inc(s("out"), 16)
            sp.wait_ge(s("out"), 64)

        def ada_in(k):
            return s(f"ada_{'sw' if k < SW_ADA else 'hw'}{k % 2}"), 16 * ((k - SW_ADA if k >= SW_ADA else k) // 2 + 1)

        def ada_load(eng, k):
            if k >= 2:
                eng.wait_ge(s("ada_acc"), k - 1)
            l, c = divmod(k, ADA)
            eng.dma_start(adas[k % 2][:, :].rearrange("p (k c) -> p k c", k=KT),
                          a["ada_w"][l][:, 512 * c:512 * c + 512].rearrange("(k p) c -> p k c", p=P)).then_inc(ada_in(k)[0], 16)

        @block.gpsimd
        def _(pool):
            pool.dma_start(tabw[:, 0:192], a["s5_scal"]).then_inc(s("s5_in"), 16)
            ada_load(pool, 0)
            ada_load(pool, 1)
            pool.dma_start(early[:, 1344:1984], a["rope"]).then_inc(s("const_in"), 16)
            pool.dma_start(ident[:, :], a["ident"]).then_inc(s("const_in"), 16)
            pool.dma_start(scanmask[:, :], a["scanmask"]).then_inc(s("const_in"), 16)
            for i, n in enumerate((1024, 512, 128)):
                pool.memset(inv[:, i * P:(i + 1) * P], 1.0 / n).then_inc(s("pool_const"), 1)
            pool.memset(one[:, :], 1.0).then_inc(s("pool_const"), 1)
            pool.memset(eps[:, :], EPS).then_inc(s("pool_const"), 1)
            pool.memset(big[:, 0:4 * APW], 0.0).then_inc(s("pool_const"), 1)
            ada_load(pool, 2)
            ada_load(pool, 3)
            pool.dma_start(dreg[:, :], a["decay"]).then_inc(s("const_in"), 16)
            pool.wait_ge(s("s5a"), 4)
            pool.wait_ge(s("s5d"), 11)
            t0, t1 = sc[16], sc[17]
            turns = 0
            for j in range(7):
                cj, sj = rotp[:, j, 0, :], rotp[:, j, 1, :]
                if j:
                    pool.wait_ge(s("rotp"), turns)
                pool.tensor_tensor(t0, cj, cj, ALU.mult).then_inc(s("rotp"), 1)
                pool.tensor_tensor(t1, sj, sj, ALU.mult).then_inc(s("rotp"), 1)
                pool.wait_ge(s("rotp"), turns + 2)
                pool.tensor_tensor(rotp[:, j + 1, 0, :], t0, t1, ALU.subtract).then_inc(s("rotp"), 1)
                pool.wait_ge(s("rotp"), turns + 3)
                pool.tensor_tensor(t0, cj, sj, ALU.mult).then_inc(s("rotp"), 1)
                pool.wait_ge(s("rotp"), turns + 4)
                pool.tensor_tensor(rotp[:, j + 1, 1, :], t0, t0, ALU.add).then_inc(s("rotp"), 1)
                turns += 5
            for k in range(4, 8):
                ada_load(pool, k)
            pool.wait_ge(s("s5_scal"), 1)
            pool.wait_ge(s("rotp"), turns)
            done = 0

            def step(ins):
                ins.then_inc(s("tab_step"), 1)

            tables_out = [0, 0]
            for b in range(16):
                second = int(b >= 5 and b % 2 == 1)
                buffer = dreg if second else tabw
                tb = buffer[:, 0:2048].rearrange("p (s c t) -> p s c t", s=4, c=2)
                if tables_out[second]:
                    pool.wait_ge(s(f"tab_out{second}"), 16 * tables_out[second])
                if b == 5:
                    pool.wait_ge(s("sd"), 4)
                if b == 1:
                    ada_load(pool, 8)
                if b == 2:
                    ada_load(pool, 9)
                step(pool.memset(tb[:, :, 0, 0:1], 1.0))
                step(pool.memset(tb[:, :, 1, 0:1], 0.0))
                done += 2
                for j in range(8):
                    n = 1 << j
                    for t0 in range(0, n, 64):
                        w = min(64, n)
                        src = tb[:, :, :, t0:t0 + w]
                        pool.wait_ge(s("tab_step"), done)
                        for r in range(2):
                            rot = rotp[:, j, r, 4 * b:4 * b + 4].unsqueeze(2).unsqueeze(3)
                            step(pool.tensor_tensor(tm[:, r, :, :, 0:w], src, rot.broadcast_to([P, 4, 2, w]), ALU.mult))
                        done += 2
                        pool.wait_ge(s("tab_step"), done)
                        step(pool.tensor_tensor(tb[:, :, 0, n + t0:n + t0 + w], tm[:, 0, :, 0, 0:w], tm[:, 1, :, 1, 0:w], ALU.subtract))
                        step(pool.tensor_tensor(tb[:, :, 1, n + t0:n + t0 + w], tm[:, 1, :, 0, 0:w], tm[:, 0, :, 1, 0:w], ALU.add))
                        done += 2
                pool.wait_ge(s("tab_step"), done)
                pool.dma_start(tab_d[4 * b:4 * b + 4].rearrange("s p f -> p s f"),
                               buffer[:, 0:2048].rearrange("p (s f) -> p s f", s=4)).then_inc(s(f"tab_out{second}"), 16)
                tables_out[second] += 1
            for n in range(65):
                if n < 64:
                    pool.wait_ge(s("s5p"), 2 * n + 2)
                    if n >= 2:
                        pool.wait_ge(s("s5g"), 2 * n - 2)
                    pb = pbuf[n % 2]
                    pool.tensor_tensor(wbuf[n % 2], pb[:, 0], pb[:, 1], ALU.add).then_inc(s("s5w"), 1)
                if n >= 1:
                    m = n - 1
                    pool.wait_ge(s("s5g"), 2 * m + 2)
                    if m >= 4:
                        pool.wait_ge(s("s5y"), m - 3)
                    pool.tensor_tensor(rotated(m)[:, 1], gbuf[m % 2][:, ::-1, :], tabs[m % TABS][:, 2:0:-1, :], ALU.mult).then_inc(s("s5r"), 1)
            for n in range(4, 12):
                p = n % 4
                pool.wait_ge(s("mgm"), n + 1)
                merged = yt3[:, 2 * p:2 * p + 2, :]
                pool.tensor_tensor(merged, merged, tmp3[:, 2 * p:2 * p + 2, :], ALU.add).then_inc(s("mga"), 1)

        @block.scalar
        def _(act):
            act.wait_ge(s("cols_in"), 16)
            act.activation(cact[:, :], col("c", 0, 8), ACT.Silu).then_inc(s("cact"), 1)
            act.wait_ge(s("s5_in"), 16)
            act.activation(sc[3], sc[2], ACT.Exp).then_inc(s("s5a"), 1)
            act.wait_ge(s("s5d"), 2)
            act.activation(mag, sc[5], ACT.Exp).then_inc(s("s5a"), 1)
            act.wait_ge(s("s5d"), 9)
            act.activation(rotp[:, 0, 1, :], sc[7], ACT.Sin).then_inc(s("s5a"), 1)
            act.activation(sc[8], sc[7], ACT.Sin, scale=0.5).then_inc(s("s5a"), 1)

            def root(job, width=T):
                job_wait(act, job)
                act.activation(ps(job)[:, 0:width], ps(job)[:, 0:width], ACT.Sqrt, bias=eps[:, :]).then_inc(s("root"), 1)

            def squares(n):
                for c in range(4):
                    if n == 0:
                        act.wait_ge(s("x_in"), 16)
                    elif n == 5:
                        act.wait_ge(s("hn"), 8 * 4 + 2 * c + 2)
                    else:
                        act.wait_ge(s("xres"), 8 * {1: 0, 2: 1, 3: 2, 4: 3, 6: 4}[n] + 2 * c + 2)
                    act.activation(sq3[:, 2 * c:2 * c + 2, :], x[:, 2 * c:2 * c + 2, :], ACT.Square).then_inc(s("sq"), 1)
                root(f"ms{n}")

            def shift(n):
                act.wait_ge(s("mod"), ADA * (n // 2) + (2 if n % 2 == 0 else 8))
                for k in range(KT):
                    act.wait_ge(s("hn"), 8 * n + k + 1)
                    i = 48 * (n // 2) + 24 * (n % 2) + k
                    act.activation(h[:, k, :], h[:, k, :], ACT.Identity, bias=mod[:, i:i + 1]).then_inc(s("h"), 1)
                    if n == 3 and k:
                        input_high(k - 1, s("h"), 24)
                if n == 3:
                    input_high(KT - 1, s("h"), 24)

            def input_high(k, ready, base):
                act.wait_ge(ready, base + k + 1)
                act.activation(h_hi[:, k, :], h[:, k, :], ACT.Copy).then_inc(s("h_high"), 1)

            def split_high(u):
                name = units[u][0]
                i = place[name]
                act.wait_ge(s(f"panel{i % RING}"), 16 * (i // RING + 1))
                if u == 0:
                    job_wait(act, "f1.0.15")
                elif u in (1, 2):
                    act.wait_ge(s("cw"), 12)
                elif GLU <= u < GLU + 3:
                    job_wait(act, "bu63")
                elif u == SECOND + 1:
                    job_wait(act, "gb3")
                elif u == SECOND + 2:
                    act.wait_ge(s("xres"), 24)
                elif BRANCH <= u < BRANCH + 3:
                    act.wait_ge(s("ygla"), 2)
                elif u == LAST:
                    job_wait(act, "uo3")
                elif u == LAST + 2:
                    job_wait(act, "br2.3")
                elif u not in (SECOND, LAST + 1):
                    unit_wait(act, u - 3)
                whole, _, high = unit_parts(u)
                act.activation(high, whole, ACT.Copy).then_inc(s("w_high"), 1)

            def act_high(n, m, ready, count):
                act.wait_ge(ready, count)
                act.activation(big_hi(m, 2), big3[:, m:m + 2, :], ACT.Copy).then_inc(s("a_high"), 1)

            act.wait_ge(s("pool_const"), 6)
            squares(0)
            shift(0)
            for j in range(2):
                job_wait(act, f"ag{j}")
                act.activation(a_sig[:, 2 * j:2 * j + 2, :], ps2(f"ag{j}"), ACT.Sigmoid).then_inc(s("agsig"), 1)
            for j, name in enumerate(("q0", "q1", "k0", "k1")):
                job_wait(act, name)
                act.activation(qk[:, 2 * j:2 * j + 2, :], ps2(name), ACT.Copy).then_inc(s("qkc"), 1)
            for j in range(2):
                job_wait(act, f"v{j}")
                act.activation(v_nat[:, j, :], ps(f"v{j}")[:, :], ACT.Copy).then_inc(s("vc"), 1)
            for j in range(2):
                job_wait(act, f"g{j}")
                act.activation(g_silu[:, 2 * j:2 * j + 2, :], ps2(f"g{j}"), ACT.Silu).then_inc(s("gsilu"), 1)
            for j in range(2):
                act.wait_ge(s("lnxc"), j + 1)
                act.activation(sq3[:, 2 * j:2 * j + 2, :], conv[:, 2 * j:2 * j + 2, :], ACT.Square).then_inc(s("lnsq"), 1)
            root("var")
            for i in range(4):
                act.wait_ge(s("lny"), i + 1)
                act.activation(yt3[:, i, :], conv[:, i, :], ACT.Silu, bias=col("cln_b", i)).then_inc(s("yconv"), 1)
            for j in range(2):
                job_wait(act, f"ro{j}")
                act.activation(sq[:, 1024 + 512 * j:1536 + 512 * j], ps(f"ro{j}")[:, :], ACT.Square).then_inc(s("rsq"), 1)
                root(f"rr{j}", 512)
            squares(1)
            shift(1)

            def relus(l, after):
                for j in range(16):
                    job_wait(act, f"f1.{l}.{j}")
                    hh = big3[:, 2 * j:2 * j + 2, :]
                    act.activation(hh, ps2(f"f1.{l}.{j}"), ACT.Relu).then_inc(s("relu"), 1)
                    if l == 0:
                        act.wait_ge(s("relu"), j + 1)
                        act.activation(hh, hh, ACT.Square).then_inc(s("fsq_act"), 1)
                    after(j)

            def next_ada(j):
                if 12 + j < 24:
                    ada_load(act, 12 + j)

            ada_load(act, 10)
            ada_load(act, 11)
            job_wait(act, "wo0.3")
            act.dma_start(tmp[:, :], a["s5_c"][:, 0, :]).then_inc(s("c_in"), 16)
            act.dma_start(yt[:, :], a["s5_c"][:, 1, :]).then_inc(s("c_in"), 16)
            relus(0, next_ada)
            act.wait_ge(s("ada_acc"), 2 * ADA)
            act.dma_start(adas[0][:, :], a["s5_b"]).then_inc(s("b_in"), 16)
            for b in range(FC2, 8):
                split_high(2 * (b - FC2))
                split_high(2 * (b - FC2) + 1)
                if b >= FC2 + 3:
                    act.wait_ge(s("row_panel"), rows_before[place[f"f2.0.{b - 3}"]])
                act.wait_ge(s("fsq_act"), 2 * b + 2)
                act.activation(fc2_high(b), big3[:, 4 * b:4 * b + 4, :], ACT.Copy).then_inc(s("b_high"), 1)
            squares(2)
            shift(2)
            for k in range(KT):
                act.wait_ge(s("h"), 16 + k + 1)
                act.activation(u_rev[:, k, :], h[:, k, ::-1], ACT.Copy).then_inc(s("ur"), 1)
            act.wait_ge(s("tab_out0"), 16 * 10)
            act.wait_ge(s("tab_out1"), 16 * 6)

            def table(n):
                if n < 64:
                    if n >= TABS:
                        act.wait_ge(s("s5q"), n - TABS + 1)
                        act.wait_ge(s("s5r"), n - TABS + 1)
                    k, q, d = n // 8, n // 2 % 4, n % 2
                    act.dma_start(tabs[n % TABS][:, 0:2, :], tab_d[32 * d + 4 * k + q].rearrange("p (c t) -> p c t", c=2)).then_inc(s(f"tab{n % TABS}"), 16)

            def negate(n):
                act.wait_ge(s(f"tab{n % TABS}"), 16 * (n // TABS + 1))
                act.activation(tabs[n % TABS][:, 2, :], tabs[n % TABS][:, 1, :], ACT.Copy, scale=-1.0).then_inc(s("s5n"), 1)

            def z_tile(k):
                act.activation(yt3[:, k, :], yt3[:, k, :], ACT.Gelu_apprx_tanh).then_inc(s("z"), 1)
                act.wait_ge(s("z"), k + 1)
                act.activation(z_hi[:, k, :], yt3[:, k, :], ACT.Copy).then_inc(s("z_high"), 1)

            for n in range(TABS):
                table(n)
            for n in range(3):
                negate(n)
            i = place["mem"]
            act.wait_ge(s(f"panel{i % RING}"), 16 * (i // RING + 1))
            for c in range(4):
                act.activation(mem_sq[:, 512 * c:512 * c + 512].rearrange("p (k t) -> p k t", k=2), mem_x[:, 2 * c:2 * c + 2, :], ACT.Square).then_inc(s("msq"), 1)
            for n in range(4, 68):
                table(n + 3)
                if n < 65:
                    negate(n - 1)
                m = n - 4
                if m == 8:
                    root("mms")
                if m in (18, 28):
                    j = (m - 18) // 10
                    job_wait(act, f"mk{j}")
                    act.activation(mk_n[:, 2 * j:2 * j + 2, :], ps2(f"mk{j}"), ACT.Copy).then_inc(s("mkc"), 1)
                    act.activation(mem_sq[:, 512 * j:512 * j + 512], ps(f"mk{j}")[:, :], ACT.Square).then_inc(s("mksq"), 1)
                if m in (22, 32):
                    root(f"mkr{(m - 22) // 10}", 512)
                if m in (41, 49):
                    j = (m - 41) // 8
                    job_wait(act, f"mv{j}")
                    act.activation(mv_nat[:, j, :], ps(f"mv{j}")[:, :], ACT.Copy).then_inc(s("mvc"), 1)
                if m >= 11 and (m - 11) % 8 == 0:
                    k = (m - 11) // 8
                    act.wait_ge(s("s5z"), k + 1)
                    z_tile(k)
            for u in range(3):
                split_high(GLU + u)
            act.wait_ge(s("s5z"), 8)
            z_tile(7)
            act.dma_start(wsm[:, :, 0:64], a["w_fox_f"].rearrange("(k p) c -> p k c", p=P)).then_inc(s("late"), 16)
            act.dma_start(wsm[:, :, 64:80], a["w_in_2"][:, GA:GA + 16].rearrange("(k p) c -> p k c", p=P)).then_inc(s("late"), 16)
            act.dma_start(wa2, a["w_gla_a2"]).then_inc(s("late"), 16)
            act.dma_start(early[:, 1152:1664], a["foxmask"]).then_inc(s("late"), 16)
            act.dma_start(glamask, a["glamask"]).then_inc(s("late"), 16)
            for p in range(4):
                for u in glu_units[p]:
                    split_high(GLU + u)
                job_wait(act, f"gb{p}")
                act.activation(tmp3[:, 2 * p:2 * p + 2, :], ps2(f"gb{p}"), ACT.Sigmoid).then_inc(s("glus"), 1)
            split_high(SECOND)
            split_high(SECOND + 1)
            squares(3)
            shift(3)
            split_high(SECOND + 2)

            def after_relu(j):
                split_high(SECOND + j + 3)
                act_high(j, 2 * j, s("fsq"), j + 1)

            relus(1, after_relu)
            for u in range(SECOND + 19, BRANCH):
                split_high(u)
            squares(4)
            squares(5)
            for j, (name, o) in enumerate((("gq0", gq_s), ("gk0", gk_s))):
                job_wait(act, name)
                act.activation(o, ps(name)[:, :], ACT.Copy).then_inc(s("gqk"), 1)
            job_wait(act, "ga1r")
            act.activation(ga1_s, ps("ga1r")[0:16, 0:T], ACT.Copy).then_inc(s("ga1c"), 1)
            for j in range(2):
                job_wait(act, f"gv{j}")
                act.activation(gv_nat[:, j, :], ps(f"gv{j}")[:, :], ACT.Copy).then_inc(s("gvc"), 1)
            for j in range(2):
                job_wait(act, f"gg{j}")
                act.activation(gg_s[:, 2 * j:2 * j + 2, :], ps2(f"gg{j}"), ACT.Silu).then_inc(s("ggs"), 1)
            act.wait_ge(s("ffa"), 1)
            act.activation(ff_c, ff_c, ACT.Exp, scale=-1.0).then_inc(s("ffe"), 1)
            act.wait_ge(s("ffe"), 1)
            act.activation(ff_c, ff_c, ACT.Ln, bias=1.0).then_inc(s("ffe"), 1)
            act.wait_ge(s("lab"), 1)
            act.activation(la_c, la_c, ACT.Exp, scale=-1.0).then_inc(s("lae"), 1)
            act.wait_ge(s("lae"), 1)
            act.activation(la_c, la_c, ACT.Ln, bias=1.0).then_inc(s("lae"), 1)
            act.wait_ge(s("lac"), 2)
            act.activation(e_pos, la_c, ACT.Exp, scale=1.0 / 16).then_inc(s("lax_e"), 1)
            act.activation(e_neg, la_c, ACT.Exp, scale=-1.0 / 16).then_inc(s("lax_e"), 1)
            act.wait_ge(s("lad"), 1)
            act.activation(e_out, e_out, ACT.Exp, scale=1.0 / 16).then_inc(s("lax_e"), 1)

            def head_squares(i, name, dst):
                if i >= 2:
                    job_wait(act, f"nr{i - 2}")
                job_wait(act, name)
                act.activation(dst[:, 2 * (i % 2):2 * (i % 2) + 2, :], ps2(name), ACT.Copy).then_inc(s("nqc"), 1)
                act.activation(sq[:, 512 * (i % 2):512 * (i % 2) + 512], ps(name)[:, :], ACT.Square).then_inc(s("nsq"), 1)

            head_squares(0, "fq0", fq_n)
            head_squares(1, "fq1", fq_n)
            job_wait(act, "kot")
            act.activation(ko_nat, ps("kot")[:, :], ACT.Copy).then_inc(s("koc"), 1)
            root("nr0", 512)
            root("nr1", 512)
            head_squares(2, "fk0", fk_n)
            head_squares(3, "fk1", fk_n)
            for j in range(2):
                job_wait(act, f"go{j}")
                act.activation(go_sq[:, 512 * j:512 * j + 512], ps(f"go{j}")[:, :], ACT.Square).then_inc(s("gosq"), 1)
                root(f"gor{j}", 512)
                if j == 0:
                    root("nr2", 512)
                    root("nr3", 512)
            for j in range(2):
                job_wait(act, f"fv{j}")
                act.activation(fv_nat[:, j, :], ps(f"fv{j}")[:, :], ACT.Copy).then_inc(s("fvc"), 1)
            head_squares(4, "mq0", mq_n)
            head_squares(5, "mq1", mq_n)

            def gate(j):
                job_wait(act, f"bg{j}")
                for i in range(2):
                    m = 2 * j + i
                    act.activation(gates[:, m, :], ps2(f"bg{j}")[:, i, :], ACT.Sigmoid, bias=col("b_gate", m)).then_inc(s("gate"), 1)

            for u in range(10):
                if u < 8:
                    for i in range(2):
                        act.wait_ge(s("unm"), u + 1)
                        if u >= 2:
                            job_wait(act, f"ut{u - 2}")
                        act.activation(probs[u % 2][:, i, :], logits[:, i, :], ACT.Exp, bias=small[:, 2 + i:3 + i],
                                       accum_out=small[:, 4 + i:5 + i]).then_inc(s("ue"), 1)
                gate(u)
                if u == 0:
                    root("nr4", 512)
                    root("nr5", 512)
                if 1 <= u <= 8:
                    job_wait(act, f"ut{u - 1}")
                    if u >= 3:
                        job_wait(act, f"uo{(u - 3) // 2}")
                    act.activation(tabw[:, 1536 + 512 * ((u - 1) % 2):2048 + 512 * ((u - 1) % 2)], ps(f"ut{u - 1}")[:, :], ACT.Copy).then_inc(s("upt"), 1)
                if u >= 3 and u % 2 == 1:
                    j = (u - 3) // 2
                    job_wait(act, f"uo{j}")
                    act.activation(ys[1 + j // 2][:, 2 * (j % 2):2 * (j % 2) + 2, :], ps2(f"uo{j}"), ACT.Copy).then_inc(s("uoc"), 1)
            def branch_high(i):
                act.activation(ys_hi[i], ys[i], ACT.Copy).then_inc(s("ys_high"), 1)

            def merged_high(p):
                act.wait_ge(s("mga"), 4 + p + 1)
                act.activation(merged_hi[:, 2 * p:2 * p + 2, :], yt3[:, 2 * p:2 * p + 2, :], ACT.Copy).then_inc(s("merged_high"), 1)

            act.wait_ge(s("ygla"), 2)
            branch_high(0)
            split_high(BRANCH)
            gate(10)
            act.wait_ge(s("uoc"), 4)
            branch_high(1)
            split_high(BRANCH + 1)
            gate(11)
            branch_high(2)
            for u in range(2, 7):
                split_high(BRANCH + u)
            merged_high(0)
            merged_high(1)
            split_high(BRANCH + 7)
            merged_high(2)
            merged_high(3)
            for u in (8, 9):
                split_high(BRANCH + u)
            for u in range(3):
                split_high(LAST + u)
            squares(6)
            for k in range(KT):
                input_high(k, s("hn"), 48)
            for u, name in enumerate(last_jobs):
                i = int(name[2:])
                if name[:2] == "fg":
                    job_wait(act, name)
                    if i >= 4:
                        act.wait_ge(s("fact"), i - 3)
                    act.activation(tmp[:, 512 * (i % 4):512 * (i % 4) + 512], ps(name)[:, :], ACT.Silu).then_inc(s("fsil"), 1)
                split_high(LAST + u + 3)
                if name[:2] == "fu":
                    act_high(16 + i, 2 * i, s("fact"), i + 1)
            for u in range(DOWN + 3, len(units)):
                split_high(u)

        @block.vector
        def _(dve):
            count = [0]

            def link(ins):
                count[0] += 1
                ins.then_inc(s("s5d"), 1)
                dve.wait_ge(s("s5d"), count[0])

            tt, ts, stt = dve.tensor_tensor, dve.tensor_scalar, dve.scalar_tensor_tensor
            li, dt = sc[1], sc[3]
            dve.wait_ge(s("s5_in"), 16)
            link(ts(sc[4], sc[0], -1e-4, None, ALU.min))
            dve.wait_ge(s("s5a"), 1)
            link(tt(sc[5], sc[4], dt, ALU.mult))
            link(tt(sc[6], li, dt, ALU.mult))
            link(ts(sc[7], sc[6], 1.0 / (2 * np.pi), ROUND, ALU.mult, ALU.add))
            link(ts(sc[9], sc[7], ROUND, None, ALU.subtract))
            link(stt(sc[6], sc[9], -TWO_PI_A, sc[6], ALU.mult, ALU.add))
            link(stt(sc[6], sc[9], -TWO_PI_B, sc[6], ALU.mult, ALU.add))
            link(stt(sc[6], sc[9], -TWO_PI_C, sc[6], ALU.mult, ALU.add))
            link(ts(sc[7], sc[6], PI_SAFE, -PI_SAFE, ALU.min, ALU.max))
            dve.wait_ge(s("s5a"), 4)
            c1, s1 = rotp[:, 0, 0, :], rotp[:, 0, 1, :]
            link(tt(sc[9], sc[8], sc[8], ALU.mult))
            link(ts(c1, sc[9], -2.0, 1.0, ALU.mult, ALU.add))
            def s5_scalars():
                abr, abi, nr, den, t0, t1 = sc[10], sc[11], sc[12], sc[13], sc[14], sc[15]
                link(tt(abr, mag, c1, ALU.mult))
                link(tt(abi, mag, s1, ALU.mult))
                link(ts(nr, abr, -1.0, None, ALU.add))
                link(tt(t0, sc[4], sc[4], ALU.mult))
                link(tt(t1, li, li, ALU.mult))
                link(tt(den, t0, t1, ALU.add))
                link(dve.reciprocal(den, den))
                link(tt(t0, nr, sc[4], ALU.mult))
                link(tt(t1, abi, li, ALU.mult))
                link(tt(t0, t0, t1, ALU.add))
                link(tt(f_re, t0, den, ALU.mult))
                link(tt(t0, abi, sc[4], ALU.mult))
                link(tt(t1, nr, li, ALU.mult))
                link(tt(t0, t0, t1, ALU.subtract))
                link(tt(f_im, t0, den, ALU.mult))
                link(ts(nf_re, f_re, -1.0, None, ALU.mult))
                ts(nf_im, f_im, -1.0, None, ALU.mult).then_inc(s("s5_scal"), 1)

            def ada_acc(k):
                dve.wait_ge(*ada_in(k))
                if k >= 2:
                    job_wait(dve, f"ada{k - 2}")
                w = adas[k % 2][:, :].rearrange("p (k c) -> p k c", k=KT)
                acc = accb[:, 512 * (k % 2):512 * (k % 2) + 512]
                if k == 0:
                    dve.wait_ge(s("cact"), 1)
                for i in range(KT):
                    if i == 0:
                        ts(acc, w[:, 0, :], cact[:, 0:1], None, ALU.mult).then_inc(s("ada_part"), 1)
                    else:
                        dve.wait_ge(s("ada_part"), 7 * k + i)
                        stt(acc, w[:, i, :], cact[:, i:i + 1], acc, ALU.mult, ALU.add)\
                            .then_inc(s("ada_part") if i < KT - 1 else s("ada_acc"), 1)

            def ada_mod(k):
                job_wait(dve, f"ada{k}")
                tt(mod[:, 4 * k:4 * k + 4], ps(f"ada{k}")[:, 0:4], col("ada_b", 4 * k, 4), ALU.add).then_inc(s("mod"), 1)

            def rms(job, width=T, sem="rstd"):
                dve.wait_ge(s("root"), ROOTS.index(job) + 1)
                return dve.reciprocal(rs[:, 0:width], ps(job)[:, 0:width]).then_inc(s(sem), 1)

            def norm(n):
                name, g0 = NORM_G[n]
                gain = col(name, g0, 8)
                if n < 4:
                    l, f = divmod(n, 2)
                    dve.wait_ge(s("mod"), ADA * l + 6 * f + 4)
                    i = 48 * l + 24 * f + 8
                    stt(gs[:, :], mod[:, i:i + 8], 1.0, gain, ALU.add, ALU.mult).then_inc(s("gs"), 1)
                    dve.wait_ge(s("gs"), n + 1)
                    gain = gs[:, :]
                rms(f"ms{n}")
                dve.wait_ge(s("rstd"), n + 1)
                dst = x if n == 4 else h
                for k in range(KT):
                    stt(dst[:, k, :], x[:, k, :], gain[:, k:k + 1], rs[:, 0:T], ALU.mult, ALU.mult).then_inc(s("hn"), 1)
                    if n in (3, 6) and k >= 2:
                        input_low(n, k - 2)
                if n in (3, 6):
                    input_low(n, KT - 2)
                    input_low(n, KT - 1)

            def input_low(n, k):
                dve.wait_ge(s("h_high"), (0 if n == 3 else 8) + k + 1)
                tt(h_lo[:, k, :], h[:, k, :], h_hi[:, k, :].bitcast(F32), ALU.subtract).then_inc(s("h_low"), 1)

            def split_low(u):
                dve.wait_ge(s("w_high"), u + 1)
                whole, low, high = unit_parts(u)
                tt(low, whole, high.bitcast(F32), ALU.subtract).then_inc(s("w_low"), 1)

            def act_low(n):
                m = 2 * (n if n < 16 else n - 16)
                dve.wait_ge(s("a_high"), n + 1)
                tt(big_lo[:, m:m + 2, :], big3[:, m:m + 2, :], big_hi(m, 2).bitcast(F32), ALU.subtract).then_inc(s("a_low"), 1)

            def residual(r, name, gate):
                for p in range(4):
                    job_wait(dve, f"{name}.{p}")
                    for i in range(2):
                        m = 2 * p + i
                        xs = x[:, m, :]
                        if gate is None:
                            o = yt3[:, m, :] if r == 5 else xs
                            tt(o, ps2(f"{name}.{p}")[:, i, :], xs, ALU.add).then_inc(s("xres"), 1)
                        else:
                            stt(xs, ps2(f"{name}.{p}")[:, i, :], mod[:, gate + m:gate + m + 1], xs, ALU.mult, ALU.add)\
                                .then_inc(s("xres"), 1)

            for k in range(4):
                ada_acc(k)
                if k:
                    ada_mod(k - 1)
            ada_mod(3)
            dve.wait_ge(s("cols_in"), 16)
            norm(0)
            s5_scalars()
            for k in range(4, 8):
                ada_acc(k)
                if k > 4:
                    ada_mod(k - 1)
            ada_mod(7)
            dve.wait_ge(s("pool_const"), 6)
            for j in range(2):
                dve.wait_ge(s("agsig"), j + 1)
                tt(a_pad[:, 2 * j:2 * j + 2, 15:15 + T], ps2(f"av{j}"), a_sig[:, 2 * j:2 * j + 2, :], ALU.mult).then_inc(s("amul"), 1)
            for tap in range(TAPS):
                for i in range(4):
                    n = 4 * tap + i
                    w = col("conv_w", TAPS * i + tap)
                    src = a_pad[:, i, tap:tap + T]
                    if tap == 0:
                        dve.wait_ge(s("amul"), i // 2 + 1)
                        ts(conv[:, i, :], src, w, col("conv_b", i), ALU.mult, ALU.add).then_inc(s("conv"), 1)
                    else:
                        dve.wait_ge(s("conv"), n - 3)
                        stt(conv[:, i, :], src, w, conv[:, i, :], ALU.mult, ALU.add).then_inc(s("conv"), 1)
            job_wait(dve, "mu")
            for j in range(2):
                dve.wait_ge(s("conv"), 4 * TAPS)
                c2 = conv[:, 2 * j:2 * j + 2, :]
                tt(c2, c2, ps("mu")[:, 0:T].unsqueeze(1).broadcast_to([P, 2, T]), ALU.subtract).then_inc(s("lnxc"), 1)
            dve.wait_ge(s("const_in"), 64)
            for j in range(4):
                qq = qk[:, 2 * j:2 * j + 2, :]
                ta, tbb = tmp3[:, 0:2, :], tmp3[:, 2:4, :]
                job_wait(dve, f"rot{j}")
                if j:
                    dve.wait_ge(s("rope"), 3 * j)
                tt(ta, qq, cos_t.unsqueeze(1).broadcast_to([P, 2, T]), ALU.mult).then_inc(s("rope"), 1)
                tt(tbb, ps2(f"rot{j}"), sin_t.unsqueeze(1).broadcast_to([P, 2, T]), ALU.mult).then_inc(s("rope"), 1)
                dve.wait_ge(s("rope"), 3 * j + 2)
                tt(qq, ta, tbb, ALU.add).then_inc(s("rope"), 1)
            rms("var", sem="lnrs")
            dve.wait_ge(s("lnrs"), 1)
            dve.wait_ge(s("lnxc"), 2)
            for i in range(4):
                stt(conv[:, i, :], conv[:, i, :], col("cln_g", i), rs[:, 0:T], ALU.mult, ALU.mult).then_inc(s("lny"), 1)
            for hd in range(4):
                job_wait(dve, f"sc{hd}")
                tt(sd[:, hd], ps2(f"sc{hd}"), dtab[:, hd], ALU.mult).then_inc(s("sd"), 1)
            for j in range(2):
                rms(f"rr{j}", 512, "rrs")
                dve.wait_ge(s("rrs"), j + 1)
                dst = qk[:, 2 * j:2 * j + 2, :]
                tt(dst, ps2(f"ro{j}"), rs[:, :].rearrange("p (k t) -> p k t", k=2), ALU.mult).then_inc(s("rn"), 1)
                dve.wait_ge(s("rn"), j + 1)
                dve.wait_ge(s("gsilu"), j + 1)
                tt(yt3[:, 4 + 2 * j:6 + 2 * j, :], dst, g_silu[:, 2 * j:2 * j + 2, :], ALU.mult).then_inc(s("ry"), 1)
            ada_acc(8)
            ada_acc(9)
            ada_mod(8)
            ada_mod(9)
            dve.wait_ge(s("mod"), 6)
            residual(0, "wo0", 16)
            norm(1)

            def ffn_square(j):
                dve.wait_ge(s("relu"), 16 + j + 1)
                hh = big3[:, 2 * j:2 * j + 2, :]
                tt(hh, hh, hh, ALU.mult).then_inc(s("fsq"), 1)

            def s5_output_weights():
                dve.wait_ge(s("c_in"), 32)
                n = 0
                for d in range(2):
                    c_re = tmp[:, 1024 * d:1024 * d + 1024].rearrange("p (s m) -> p s m", s=32)
                    c_im = yt[:, 1024 * d:1024 * d + 1024].rearrange("p (s m) -> p s m", s=32)
                    part = sq[:, 0:1024].rearrange("p (s m) -> p s m", s=32)
                    o_re, o_im = c_w[:, 32 * d:32 * d + 32, 0, :], c_w[:, 32 * d:32 * d + 32, 1, :]

                    def f(v):
                        return v[:, 32 * d:32 * d + 32].unsqueeze(2).broadcast_to([P, 32, 32])

                    for o, p0, f0, p1, f1, op in ((o_re, c_re, f_re, c_im, f_im, ALU.subtract),
                                                  (o_im, c_re, nf_im, c_im, nf_re, ALU.add)):
                        tt(o, p0, f(f0), ALU.mult).then_inc(s("cw"), 1)
                        if n:
                            dve.wait_ge(s("cw"), n)
                        tt(part, p1, f(f1), ALU.mult).then_inc(s("cw"), 1)
                        dve.wait_ge(s("cw"), n + 2)
                        tt(o, o, part, op).then_inc(s("cw"), 1)
                        n += 3

            def more_ada(j):
                if j < 14:
                    ada_acc(10 + j)
                if j >= 1 and j < 15:
                    ada_mod(9 + j)

            for j in range(16):
                more_ada(j)
            s5_output_weights()
            for b in range(FC2, 8):
                split_low(2 * (b - FC2))
                split_low(2 * (b - FC2) + 1)
                dve.wait_ge(s("b_high"), b - FC2 + 1)
                tiles = slice(4 * b, 4 * b + 4)
                tt(big_lo[:, tiles, :], big3[:, tiles, :], fc2_high(b).bitcast(F32), ALU.subtract).then_inc(s("b_low"), 1)
            dve.wait_ge(s("mod"), ADA)
            residual(1, "f2.0", 40)
            norm(2)
            def z_low(k):
                dve.wait_ge(s("z_high"), k + 1)
                tt(z_lo[:, k, :], yt3[:, k, :], z_hi[:, k, :].bitcast(F32), ALU.subtract).then_inc(s("z_low"), 1)

            for n in range(66):
                k, q, d = n // 8, n // 2 % 4, n % 2
                if n < 64:
                    tab = tabs[n % TABS]
                    job_wait(dve, f"bu{n}")
                    dve.wait_ge(s("s5n"), n + 1)
                    if n >= 2:
                        dve.wait_ge(s("s5w"), n - 1)
                    tt(pbuf[n % 2][:, 0], ps2(f"bu{n}"), tab[:, 0:1, :].broadcast_to([P, 2, T]), ALU.mult).then_inc(s("s5p"), 1)
                    tt(pbuf[n % 2][:, 1], ps2(f"bu{n}")[:, ::-1, :], tab[:, 1:3, :], ALU.mult).then_inc(s("s5p"), 1)
                if 1 <= n <= 64:
                    m = n - 1
                    mk, mq_, md = m // 8, m // 2 % 4, m % 2
                    tab = tabs[m % TABS]
                    at = 32 * md + 4 * mk + mq_
                    dve.wait_ge(s("s5w"), m + 1)
                    if m >= 2:
                        dve.wait_ge(s("s5r"), m - 1)
                    for r in range(2):
                        dve.tensor_tensor_scan(gbuf[m % 2][:, r, :], mag[:, at:at + 1].broadcast_to([P, T]), wbuf[m % 2][:, r, :],
                                               0.0, ALU.mult, ALU.add).then_inc(s("s5g"), 1)
                    dve.wait_ge(s("s5g"), 2 * m + 2)
                    if m >= 4:
                        dve.wait_ge(s("s5y"), m - 3)
                    tt(rotated(m)[:, 0], gbuf[m % 2], tab[:, 0:1, :].broadcast_to([P, 2, T]), ALU.mult).then_inc(s("s5q"), 1)
                if n >= 9 and (n - 9) % 8 == 0:
                    kk = (n - 9) // 8
                    dve.wait_ge(s("s5y"), 8 * kk + 8)
                    stt(yt3[:, kk, :], h[:, kk, :], col("s5_d", kk), bank[6 + kk % 2][:, 0:T], ALU.mult, ALU.add).then_inc(s("s5z"), 1)
                if n >= 14 and (n - 14) % 8 == 0:
                    z_low((n - 14) // 8)
                if n == 10:
                    rms("mms", sem="mrs")
                if 10 <= n < 14:
                    dve.wait_ge(s("mrs"), 1)
                    for kk in (2 * n - 20, 2 * n - 19):
                        stt(mem_x[:, kk, :], mem_x[:, kk, :], col("g_mem", kk), rs[:, 0:T], ALU.mult, ALU.mult).then_inc(s("memn"), 1)
                if n in (24, 34):
                    j = (n - 24) // 10
                    rms(f"mkr{j}", 512, "mkrs")
                    dve.wait_ge(s("mkrs"), j + 1)
                    keys = mk_n[:, 2 * j:2 * j + 2, :].rearrange("p k t -> p (k t)")
                    dve.wait_ge(s("mkc"), j + 1)
                    stt(keys, keys, col("g_mk"), rs[:, :], ALU.mult, ALU.mult).then_inc(s("mkn"), 1)
            split_low(GLU)
            z_low(7)
            split_low(GLU + 1)
            split_low(GLU + 2)
            dve.wait_ge(s("mod"), ADA + 6)
            for p in range(4):
                for u in glu_units[p]:
                    split_low(GLU + u)
                dve.wait_ge(s("glus"), p + 1)
                g2 = tmp3[:, 2 * p:2 * p + 2, :]
                tt(g2, ps2(f"ga{p}"), g2, ALU.mult).then_inc(s("glut"), 1)
                dve.wait_ge(s("glut"), p + 1)
                for i in range(2):
                    m = 2 * p + i
                    stt(x[:, m, :], tmp3[:, m, :], mod[:, 48 + 16 + m:48 + 17 + m], x[:, m, :], ALU.mult, ALU.add).then_inc(s("xres"), 1)
            split_low(SECOND)
            norm(3)
            for u in (1, 2):
                split_low(SECOND + u)
            for j in range(16):
                ffn_square(j)
                if j:
                    act_low(j - 1)
                split_low(SECOND + j + 3)
            act_low(15)
            for u in range(SECOND + 19, BRANCH):
                split_low(u)
            dve.wait_ge(s("mod"), 2 * ADA)
            residual(3, "f2.1", 48 + 40)
            norm(4)
            norm(5)
            dve.memset(tmp[:, 0:1024], 0.0).then_inc(s("atz"), 1)
            ts(gsc[:, 0:1], col("g_fq"), float(128 ** -0.5), None, ALU.mult).then_inc(s("gqs"), 1)
            ts(gsc[:, 1:2], col("g_mq"), float(128 ** -0.5), None, ALU.mult).then_inc(s("gqs"), 1)
            dve.memset(fb, 1.0).then_inc(s("fb"), 1)
            job_wait(dve, "ff")
            ts(ff_x, ps("ff")[0:64, 0:T], cols[0:64, COLS["b_fox"]:COLS["b_fox"] + 1], None, ALU.add).then_inc(s("ffx"), 1)
            dve.wait_ge(s("ffx"), 1)
            stt(ff_c, ff_x, -1.0, ff_x, ALU.mult, ALU.max).then_inc(s("ffa"), 1)
            job_wait(dve, "la")
            for i in range(2):
                ts(la_x[:, T * i:T * i + T], ps2("la")[:, i, :], col("b_gla", i), None, ALU.add).then_inc(s("lax"), 1)
            dve.wait_ge(s("lax"), 2)
            stt(la_c, la_x, -1.0, la_x, ALU.mult, ALU.max).then_inc(s("lab"), 1)
            dve.wait_ge(s("ffe"), 2)
            stt(ff_x, ff_x, 0.0, ff_c, ALU.min, ALU.subtract).then_inc(s("ffl"), 1)
            dve.wait_ge(s("ffl"), 1)
            dve.wait_ge(s("fb"), 1)
            dve.tensor_tensor_scan(ff_c, fb, ff_x, 0.0, ALU.mult, ALU.add).then_inc(s("ffs"), 1)
            dve.wait_ge(s("ffs"), 1)
            ts(early[32:64, 896:1152], tmp[32:64, 1792:2048], -1.0, None, ALU.mult).then_inc(s("fb"), 1)
            dve.wait_ge(s("lae"), 2)
            stt(la_x, la_x, 0.0, la_c, ALU.min, ALU.subtract).then_inc(s("las"), 1)
            dve.wait_ge(s("las"), 1)
            for i in range(2):
                dve.tensor_tensor_scan(la_c[:, T * i:T * i + T], scanmask[:, :], la_x[:, T * i:T * i + T], 0.0,
                                       ALU.mult, ALU.add).then_inc(s("lac"), 1)
            dve.wait_ge(s("lac"), 2)
            c8 = la_c.rearrange("p (c t) -> p c t", t=CHUNK)
            tt(e_out.rearrange("p (c t) -> p c t", t=CHUNK), c8[:, :, CHUNK - 1:CHUNK].broadcast_to([P, 8, CHUNK]), c8,
               ALU.subtract).then_inc(s("lad"), 1)
            dve.wait_ge(s("gqk"), 2)
            dve.wait_ge(s("lax_e"), 2)
            stt(gq_s, gq_s, float(DK ** -0.5), e_pos, ALU.mult, ALU.mult).then_inc(s("gin"), 1)
            tt(k_in, gk_s, e_neg, ALU.mult).then_inc(s("gin"), 1)
            dve.wait_ge(s("lax_e"), 3)
            tt(gk_s, gk_s, e_out, ALU.mult).then_inc(s("gin"), 1)

            def head_norm(i, gain, dst):
                dve.wait_ge(s("nqc"), i + 1)
                if i:
                    dve.wait_ge(s("nq"), i)
                rms(f"nr{i}", 512, "nrs")
                dve.wait_ge(s("nrs"), i + 1)
                flat = dst.rearrange("p k t -> p (k t)")
                stt(flat, flat, gain, rs[:, :], ALU.mult, ALU.mult).then_inc(s("nq"), 1)

            job_wait(dve, "cs1")
            cs0 = ps("cs0")[:, :].rearrange("p (c m v) -> p c m v", c=2, m=2)
            cs1 = ps("cs1")[:, 0:256].rearrange("p (m v) -> p m v", m=2)
            dve.tensor_copy(state[:, 0], cs0[:, 0]).then_inc(s("gst"), 1)
            for c in (1, 2):
                dve.wait_ge(s("gst"), 2 * c - 1)
                for m in range(2):
                    at = T * m + CHUNK * c + CHUNK - 1
                    stt(state[:, c, m], state[:, c - 1, m], e_pos[:, at:at + 1], cs1[:, m] if c == 1 else cs0[:, 1, m],
                        ALU.mult, ALU.add).then_inc(s("gst"), 1)
            dve.wait_ge(s("gqs"), 2)
            for j in range(2):
                head_norm(j, gsc[:, 0:1], fq_n[:, 2 * j:2 * j + 2, :])
            dve.wait_ge(s("late"), 80)
            dve.wait_ge(s("atz"), 1)
            for i in range(2):
                job_wait(dve, f"at{i}")
                dve.copy_predicated(att[:, 4 * i:4 * i + 4, :], glamask.unsqueeze(1).broadcast_to([P, 4, P]),
                                    ps(f"at{i}")[:, :].rearrange("p (k t) -> p k t", k=4)).then_inc(s("atc"), 1)

            def gla_out(j):
                dve.wait_ge(s("nq"), 2 + 2 * j)
                rms(f"gor{j}", 512, "gors")
                dve.wait_ge(s("gors"), j + 1)
                for i in range(2):
                    hd = j + 2 * i
                    stt(go_n[:, hd, :], ps2(f"go{j}")[:, i, :], col("g_gla", hd), rs[:, T * i:T * i + T], ALU.mult, ALU.mult).then_inc(s("gon"), 1)
                dve.wait_ge(s("gon"), 2 * j + 2)
                dve.wait_ge(s("ggs"), 2)
                tt(ys[0][:, j::2, :], go_n[:, j::2, :], gg_s[:, j::2, :], ALU.mult).then_inc(s("ygla"), 1)

            gla_out(0)
            for j in range(2):
                head_norm(2 + j, col("g_fk"), fk_n[:, 2 * j:2 * j + 2, :])
            gla_out(1)

            def fox_rows(hd):
                if hd >= 2:
                    job_wait(dve, f"us{hd - 2}")
                ts(fa[hd % 2][0:32, :], tmp[0:32, 1792:2048], ident[0:32, hd:hd + 1], None, ALU.mult).then_inc(s("fa"), 1)
                ts(fa[hd % 2][32:64, :], scan_ones, ident[32:64, 32 + hd:33 + hd], None, ALU.mult).then_inc(s("fa"), 1)

            scan_ones = tmp[32:64, 1536:1792]
            dve.memset(scan_ones, 1.0).then_inc(s("pick1"), 1)
            dve.wait_ge(s("pick1"), 1)
            fox_rows(0)
            for u in range(9):
                if u < 8:
                    if u + 1 < 4:
                        fox_rows(u + 1)
                    job_wait(dve, f"us{u}")
                    if u >= 1:
                        dve.wait_ge(s("ue"), 2 * u)
                    if u < 4:
                        tt(logits, ps2(f"us{u}"), foxmask, ALU.add).then_inc(s("ul"), 1)
                    else:
                        dve.tensor_copy(logits, ps2(f"us{u}")).then_inc(s("ul"), 1)
                    dve.wait_ge(s("ul"), u + 1)
                    dve.tensor_reduce(small[:, 0:2], logits, AX_X, ALU.max).then_inc(s("umx"), 1)
                    dve.wait_ge(s("umx"), u + 1)
                    ts(small[:, 2:4], small[:, 0:2], -1.0, None, ALU.mult).then_inc(s("unm"), 1)
                    dve.wait_ge(s("ue"), 2 * u + 2)
                    dve.reciprocal(small[:, 6:8], small[:, 4:6]).then_inc(s("urc"), 1)
                    dve.wait_ge(s("urc"), u + 1)
                    for i in range(2):
                        ts(probs[u % 2][:, i, :], probs[u % 2][:, i, :], small[:, 6 + i:7 + i], None, ALU.mult).then_inc(s("up"), 1)
                if u == 0:
                    for j in range(2):
                        head_norm(4 + j, gsc[:, 1:2], mq_n[:, 2 * j:2 * j + 2, :])
            def branch_low(i):
                dve.wait_ge(s("ys_high"), i + 1)
                tt(ys_lo[i], ys[i], ys_hi[i].bitcast(F32), ALU.subtract).then_inc(s("ys_low"), 1)

            branch_low(0)
            split_low(BRANCH)
            branch_low(1)
            split_low(BRANCH + 1)
            branch_low(2)
            for n in range(12):
                i, p = divmod(n, 4)
                if n % 2 == 0:
                    split_low(BRANCH + 2 + n // 2)
                job_wait(dve, f"br{i}.{p}")
                m = KT * i + 2 * p
                dve.wait_ge(s("gate"), m + 2)
                if i == 2:
                    dve.wait_ge(s("mga"), p + 1)
                dst = (yt3 if i == 0 else tmp3)[:, 2 * p:2 * p + 2, :]
                tt(dst, ps2(f"br{i}.{p}"), gates[:, m:m + 2, :], ALU.mult).then_inc(s("mgm"), 1)
            for p in range(4):
                dve.wait_ge(s("merged_high"), p + 1)
                two = slice(2 * p, 2 * p + 2)
                tt(merged_lo[:, two, :], yt3[:, two, :], merged_hi[:, two, :].bitcast(F32), ALU.subtract).then_inc(s("merged_low"), 1)
            for u in (8, 9):
                split_low(BRANCH + u)
            for u in range(3):
                split_low(LAST + u)
            residual(4, "w2o", None)
            norm(6)
            for u, name in enumerate(last_jobs):
                i = int(name[2:])
                if name[:2] == "fu":
                    dve.wait_ge(s("fsil"), i + 1)
                    job_wait(dve, name)
                    tt(big[:, 512 * i:512 * i + 512], ps(name)[:, :], tmp[:, 512 * (i % 4):512 * (i % 4) + 512], ALU.mult).then_inc(s("fact"), 1)
                split_low(LAST + u + 3)
                if name[:2] == "fu":
                    act_low(16 + i)
            for u in range(DOWN + 3, len(units)):
                split_low(u)
            residual(5, "fd", None)

        @block.tensor
        def _(pe):
            at = [0]

            def begin(name):
                i = INDEX[name]
                assert at[0] == i, (name, JOBS[at[0]])
                at[0] += 1
                if name not in TURN:
                    if int(name[3:]) >= 2:
                        pe.wait_ge(s("mod"), int(name[3:]) - 1)
                elif TURN[name] >= BANKS:
                    sem, n = freed[ROTATING[TURN[name] - BANKS]]
                    pe.wait_ge(s(sem), n)

            def open_bank(name):
                sem, n = freed[ROTATING[TURN[name] - BANKS]]
                pe.wait_ge(s(sem), n)

            def close(name, last):
                assert at[0] == INDEX[name], name
                at[0] += 1
                end(last)

            def end(mm):
                mm.then_inc(s("job"), 1)

            def panel(name):
                i = place[name]
                pe.wait_ge(s(f"panel{i % RING}"), 16 * (i // RING + 1))
                return panel_view(name)

            def mm(*args, **kw):
                return pe.matmul(*args, skip_group_check=True, **kw)

            def project(name, w, m0, src, ready, tiles=2):
                begin(name)
                for i in range(tiles):
                    c = (m0 + i) * P
                    for k in range(KT):
                        ready(k)
                        last = mm(ps2(name)[:, i, :], w[:, k, c:c + P], src[:, k, :], start=(k == 0), stop=(k == KT - 1))
                end(last)

            def project_nat(name, w, i, src):
                begin(name)
                for k in range(KT):
                    last = mm(ps(name)[:, :], src[:, k, P * i:P * i + P], w[:, k, :], start=(k == 0), stop=(k == KT - 1))
                end(last)

            def rows_open(names, panel_name, blocks, src, ready):
                for name in names:
                    begin(name)
                for b in range(blocks):
                    w = panel(f"{panel_name}{b}")
                    for m in range(KT):
                        for k in range(4):
                            kt = 4 * b + k
                            ready(kt)
                            last = mm(ps2(names[m // 2])[:, m % 2, :], w[:, k, P * m:P * m + P], src[:, kt, :],
                                      start=(kt == 0 and m % 2 == 0), stop=False)
                    last.then_inc(s("row_panel"), 1)

            def three(out_, high, low, x_high, x_low, start, stop):
                mm(out_, high, x_high, start=start, stop=False)
                mm(out_, high, x_low, start=False, stop=False)
                return mm(out_, low, x_high, start=False, stop=stop)

            def project_split(name, u, x_high, x_low, ready):
                begin(name)
                pe.wait_ge(s("w_low"), u + 1)
                _, low, high = unit_parts(u)
                for i in range(2):
                    for k in range(KT):
                        ready(k)
                        c = slice(P * i, P * i + P)
                        last = three(ps2(name)[:, i, :], high[:, k, c], low[:, k, c], x_high[:, k, :], x_low[:, k, :], k == 0, k == KT - 1)
                end(last)

            def rows_split(names, u0, b0, blocks, x_high, ready):
                if b0 == 0:
                    for name in names:
                        begin(name)
                kt = 4 * b0
                for b in range(b0, blocks):
                    for half in range(2):
                        u = u0 + 2 * (b - b0) + half
                        pe.wait_ge(s("w_low"), u + 1)
                        _, low, high = unit_parts(u)
                        nk = low.shape[1]
                        for i in range(4):
                            m = 4 * half + i
                            for k in range(nk):
                                ready(kt + k)
                                c = slice(P * i, P * i + P)
                                last = three(ps2(names[m // 2])[:, m % 2, :], high[:, k, c], low[:, k, c],
                                             x_high(kt + k), big_lo[:, kt + k, :],
                                             kt + k == 0 and m % 2 == 0, b == blocks - 1 and k == nk - 1)
                            if b == blocks - 1 and m % 2 == 1:
                                end(last)
                        if b < blocks - 1:
                            last.then_inc(s("row_panel" if half else "row_half"), 1)
                    kt += nk

            def ada(k):
                begin(f"ada{k}")
                pe.wait_ge(s("ada_acc"), k + 1)
                for i in range(4):
                    last = mm(ps(f"ada{k}")[:, i:i + 1], accb[:, 512 * (k % 2) + P * i:512 * (k % 2) + P * i + P], one[:, :], start=(i == 0), stop=(i == 3))
                end(last)

            def mean_squares(n):
                begin(f"ms{n}")
                for k in range(KT):
                    pe.wait_ge(s("sq"), 4 * n + k // 2 + 1)
                    last = mm(ps(f"ms{n}")[:, 0:T], inv1024, sq3[:, k, :], start=(k == 0), stop=(k == KT - 1))
                end(last)

            def mean(name, m, src, width=512):
                begin(name)
                end(mm(ps(name)[:, 0:width], m, src, start=True, stop=True))

            def h_ready(n):
                if n < 4:
                    return lambda k: pe.wait_ge(s("h"), 8 * n + k + 1)
                return lambda k: pe.wait_ge(s("hn"), 8 * n + k + 1)

            def no_wait(k):
                return None

            pe.wait_ge(s("pool_const"), 6)
            for k in range(4):
                ada(k)
            mean_squares(0)
            w = panel("av")
            project("av0", w, 0, h, h_ready(0))
            project("av1", w, 2, h, no_wait)
            for name in ("ag", "q"):
                w = panel(name)
                for j in range(2):
                    project(f"{name}{j}", w, 2 * j, h, no_wait)
                    ada((4 if name == "ag" else 6) + j)
            w = panel("k")
            project("k0", w, 0, h, no_wait)
            project("k1", w, 2, h, no_wait)
            w = panel("v")
            project_nat("v0", w, 0, h)
            project_nat("v1", w, 1, h)
            w = panel("g")
            project("g0", w, 0, h, no_wait)
            project("g1", w, 2, h, no_wait)
            begin("mu")
            for i in range(4):
                pe.wait_ge(s("conv"), 4 * (TAPS - 1) + i + 1)
                last = mm(ps("mu")[:, 0:T], inv512, conv[:, i, :], start=(i == 0), stop=(i == 3))
            end(last)
            pe.wait_ge(s("const_in"), 64)
            for j in range(4):
                pe.wait_ge(s("qkc"), j + 1)
                mean(f"rot{j}", perm, qk[:, 2 * j:2 * j + 2, :].rearrange("p k t -> p (k t)"))
            begin("var")
            for i in range(4):
                pe.wait_ge(s("lnsq"), i // 2 + 1)
                last = mm(ps("var")[:, 0:T], inv512, sq3[:, i, :], start=(i == 0), stop=(i == 3))
            end(last)
            for hd in range(4):
                begin(f"sc{hd}")
                pe.wait_ge(s("rope"), 12)
                for i in range(2):
                    last = mm(ps2(f"sc{hd}")[:, i, :], qk[:, 4 + hd, P * i:P * i + P], qk[:, hd, :], start=True, stop=True)
                end(last)
            pe.wait_ge(s("vc"), 2)
            for j in range(2):
                begin(f"ro{j}")
                for i in range(2):
                    hd = 2 * j + i
                    pe.wait_ge(s("sd"), hd + 1)
                    for t in range(2):
                        last = mm(ps2(f"ro{j}")[:, i, :], v_nat[:, t, P * hd:P * hd + P], sd[:, hd, t, :], start=(t == 0), stop=(t == 1))
                end(last)
                pe.wait_ge(s("rsq"), j + 1)
                mean(f"rr{j}", inv128, sq[:, 1024 + 512 * j:1536 + 512 * j])

            def cat_ready(k):
                pe.wait_ge(s("yconv") if k < 4 else s("ry"), k + 1 if k < 4 else (k - 4) // 2 + 1)

            for i in range(2):
                w = panel(f"wo{i}")
                for j in range(2):
                    project(f"wo0.{2 * i + j}", w, 2 * j, yt3, cat_ready)
                    if i == 0:
                        ada(8 + j)
            mean_squares(1)

            for i in range(8):
                w = panel(f"f1.0.{i}")
                for j in range(2 * i, 2 * i + 2):
                    project(f"f1.0.{j}", w, 2 * (j % 2), h, h_ready(1) if j == 0 else no_wait)
                    if j >= 2:
                        ada(8 + j)
            sums = [f"f2.0.{p}" for p in range(4)]
            rows_open(sums, "f2.0.", FC2, big3, lambda k: pe.wait_ge(s("fsq_act"), k // 2 + 1))
            rows_split(sums, 0, FC2, 8, lambda k: fc2_high(k // 4)[:, k % 4, :], lambda k: pe.wait_ge(s("b_low"), k // 4 - FC2 + 1))
            mean_squares(2)
            def memory(n):
                if 4 <= n < 8:
                    if n == 4:
                        open_bank("mms")
                    for k in (2 * n - 8, 2 * n - 7):
                        pe.wait_ge(s("msq"), k // 2 + 1)
                        last = mm(ps("mms")[:, 0:T], inv1024, mem_sq[:, T * k:T * k + T], start=(k == 0), stop=(k == KT - 1))
                    if n == 7:
                        close("mms", last)
                if 16 <= n < 20 or 26 <= n < 30:
                    j, part = divmod(n - 16, 10)
                    name, w = f"mk{j}", panel("mk")
                    if part == 0:
                        open_bank(name)
                    i = part // 2
                    c = (2 * j + i) * P
                    for k in range(4 * (part % 2), 4 * (part % 2) + 4):
                        pe.wait_ge(s("memn"), k + 1)
                        last = mm(ps2(name)[:, i, :], w[:, k, c:c + P], mem_x[:, k, :], start=(k == 0), stop=(k == KT - 1))
                    if part == 3:
                        close(name, last)
                if n in (22, 32):
                    j = (n - 22) // 10
                    pe.wait_ge(s("mksq"), j + 1)
                    mean(f"mkr{j}", inv128, mem_sq[:, 512 * j:512 * j + 512])
                if 36 <= n < 40 or 44 <= n < 48:
                    j, part = divmod(n - 36, 8)
                    name, w = f"mv{j}", panel("mv")
                    if part == 0:
                        open_bank(name)
                    for k in (2 * part, 2 * part + 1):
                        last = mm(ps(name)[:, :], mem_x[:, k, P * j:P * j + P], w[:, k, :], start=(k == 0), stop=(k == KT - 1))
                    if part == 3:
                        close(name, last)

            pe.wait_ge(s("b_in"), 16)
            for n in range(67):
                if n < 64:
                    k, q, d = n // 8, n // 2 % 4, n % 2
                    begin(f"bu{n}")
                    pe.wait_ge(s("ur") if d else s("h"), k + 1 if d else 16 + k + 1)
                    u = (u_rev if d else h)[32 * q:32 * q + 32, k, :]
                    for r in range(2):
                        last = mm(ps2(f"bu{n}")[:, r, :], b_w[32 * q:32 * q + 32, k, d, r, :], u, start=True, stop=True)
                    end(last)
                    memory(n)
                if n >= 3:
                    m = n - 3
                    k, q, d = m // 8, m // 2 % 4, m % 2
                    if m == 0:
                        pe.wait_ge(s("cw"), 12)
                    if k >= 2 and m % 8 == 0:
                        pe.wait_ge(s("s5z"), k - 1)
                    pe.wait_ge(s("s5q"), m + 1)
                    pe.wait_ge(s("s5r"), m + 1)
                    for f in range(2):
                        for r in range(2):
                            last = mm(bank[6 + k % 2][32 * q:32 * q + 32, 0:T], c_w[:, 32 * d + 4 * k + q, r, :],
                                      qbuf[m % 4][:, f, r, :], start=(d == 0 and f == 0 and r == 0),
                                      stop=(d == 1 and f == 1 and r == 1))
                    last.then_inc(s("s5y"), 1)
            for u, name in enumerate(glu_jobs):
                project_split(name, GLU + u, z_hi, z_lo, (lambda k: pe.wait_ge(s("z_low"), k + 1)) if u == 0 else no_wait)
            mean_squares(3)
            for j in range(16):
                project_split(f"f1.1.{j}", SECOND + j, h_hi, h_lo, (lambda k: pe.wait_ge(s("h_low"), k + 1)) if j == 0 else no_wait)
            rows_split([f"f2.1.{p}" for p in range(4)], SECOND + 16, 0, 8, lambda k: big_hi(k)[:, 0, :], lambda k: pe.wait_ge(s("a_low"), k // 2 + 1))
            mean_squares(4)
            mean_squares(5)
            w = panel("gqk")
            project("gq0", w, 0, h, h_ready(5))
            project("gk0", w, 2, h, no_wait)
            pe.wait_ge(s("late"), 80)
            for name, c0, m in (("ga1r", 64, 16), ("ff", 0, 64)):
                begin(name)
                for k in range(KT):
                    last = mm(ps(name)[0:m, 0:T], wsm[:, k, c0:c0 + m], h[:, k, :], start=(k == 0), stop=(k == KT - 1))
                end(last)
            w = panel("gv")
            project_nat("gv0", w, 0, h)
            project_nat("gv1", w, 1, h)
            begin("la")
            pe.wait_ge(s("ga1c"), 1)
            for i in range(2):
                last = mm(ps2("la")[:, i, :], wa2[:, P * i:P * i + P], ga1_s, start=True, stop=True)
            end(last)
            for name, w_name in (("gg", "gg"), ("fq", "fq")):
                w = panel(w_name)
                for j in range(2):
                    project(f"{name}{j}", w, 2 * j, h, no_wait)
            begin("kot")
            pe.wait_ge(s("gin"), 3)
            for t in range(2):
                for m in range(2):
                    last = pe.transpose(ps("kot")[:, 256 * t + P * m:256 * t + P * m + P], gk_s[:, T * m + P * t:T * m + P * t + P], ident[:, :])
            end(last)
            pe.wait_ge(s("koc"), 1)
            pe.wait_ge(s("gvc"), 2)
            for name, chunks in (("cs0", (0, 2)), ("cs1", (1,))):
                begin(name)
                for c in chunks:
                    r0 = CHUNK * (c % 2)
                    for hd in range(4):
                        m, p0 = hd // 2, DK * (hd % 2)
                        o = 256 * (c // 2) + P * m
                        last = mm(ps(name)[p0:p0 + DK, o:o + P], ko_nat[r0:r0 + CHUNK, 256 * (c // 2) + DK * hd:256 * (c // 2) + DK * hd + DK],
                                  gv_nat[r0:r0 + CHUNK, c // 2, P * hd:P * hd + P], start=True, stop=True)
                end(last)

            def head_mean(i):
                pe.wait_ge(s("nsq"), i + 1)
                mean(f"nr{i}", inv128, sq[:, 512 * (i % 2):512 * (i % 2) + 512])

            head_mean(0)
            head_mean(1)
            for odd in range(2):
                begin(f"at{odd}")
                for t in range(2):
                    for m in range(2):
                        c = slice(T * m + P * t, T * m + P * t + P)
                        last = mm(ps(f"at{odd}")[:, 256 * t + P * m:256 * t + P * m + P], k_in[DK * odd:DK * odd + DK, c],
                                  gq_s[DK * odd:DK * odd + DK, c], start=True, stop=True)
                end(last)
            w = panel("fk")
            for j in range(2):
                project(f"fk{j}", w, 2 * j, h, no_wait)

            def gla_out(j):
                begin(f"go{j}")
                pe.wait_ge(s("atc"), 2)
                pe.wait_ge(s("gst"), 5)
                for i in range(2):
                    hd = j + 2 * i
                    m, p0 = i, DK * j
                    for t in range(2):
                        mm(ps2(f"go{j}")[:, i, P * t:P * t + P], gv_nat[:, t, P * hd:P * hd + P], att[:, 4 * j + 2 * t + i, :],
                           start=(i == 0 and t == 0), stop=False)
                    for c in range(1, 4):
                        last = mm(ps2(f"go{j}")[:, i, CHUNK * c:CHUNK * c + CHUNK], state[p0:p0 + DK, c - 1, m, :],
                                  gq_s[p0:p0 + DK, T * m + CHUNK * c:T * m + CHUNK * c + CHUNK], start=False, stop=(c == 3))
                end(last)
                pe.wait_ge(s("gosq"), j + 1)
                mean(f"gor{j}", inv128, go_sq[:, 512 * j:512 * j + 512])

            gla_out(0)
            head_mean(2)
            head_mean(3)
            gla_out(1)
            w = panel("fv")
            project_nat("fv0", w, 0, h)
            project_nat("fv1", w, 1, h)
            w = panel("mq")
            for j in range(2):
                project(f"mq{j}", w, 2 * j, h, no_wait)

            def gate(j):
                project(f"bg{j}", panel(f"bg{j // 2}"), 2 * (j % 2), h, no_wait)

            for u in range(10):
                if u < 8:
                    begin(f"us{u}")
                    if u < 4:
                        pe.wait_ge(s("nq"), 4)
                        pe.wait_ge(s("fa"), 2 * u + 2)
                        pe.wait_ge(s("fb"), 2)
                    else:
                        pe.wait_ge(s("nq"), 6)
                        pe.wait_ge(s("mkn"), 2)
                    for t in range(2):
                        o = ps2(f"us{u}")[:, t, :]
                        if u < 4:
                            mm(o, fq_n[:, u, P * t:P * t + P], fk_n[:, u, :], start=True, stop=False)
                            last = mm(o, fa[u % 2][:, P * t:P * t + P], fb, start=False, stop=True)
                        else:
                            last = mm(o, mq_n[:, u - 4, P * t:P * t + P], mk_n[:, u - 4, :], start=True, stop=True)
                    end(last)
                gate(u)
                if u == 0:
                    head_mean(4)
                    head_mean(5)
                if 1 <= u <= 8:
                    m = u - 1
                    begin(f"ut{m}")
                    pe.wait_ge(s("up"), 2 * m + 2)
                    for ks in range(2):
                        for t in range(2):
                            last = pe.transpose(ps(f"ut{m}")[:, 256 * ks + P * t:256 * ks + P * t + P], probs[m % 2][:, t, P * ks:P * ks + P], ident[:, :])
                    end(last)
                if u >= 3 and u % 2 == 1:
                    j = (u - 3) // 2
                    begin(f"uo{j}")
                    v = fv_nat if j < 2 else mv_nat
                    pe.wait_ge(s("fvc") if j < 2 else s("mvc"), 2)
                    for i in range(2):
                        m = 2 * j + i
                        hd = m % 4
                        pe.wait_ge(s("upt"), m + 1)
                        for ks in range(2):
                            last = mm(ps2(f"uo{j}")[:, i, :], v[:, ks, P * hd:P * hd + P], prob_t[m % 2][:, ks, :], start=(ks == 0), stop=(ks == 1))
                    end(last)
            gate(10)
            gate(11)
            for i in range(3):
                pe.wait_ge(s("ys_low"), i + 1)
                for half in range(2):
                    u = BRANCH + 2 * i + half
                    _, low, high = unit_parts(u)
                    for p in (2 * half, 2 * half + 1):
                        begin(f"br{i}.{p}")
                        pe.wait_ge(s("w_low"), u + 1)
                        for j in range(2):
                            o = P * (2 * (p - 2 * half) + j)
                            for k in range(4):
                                last = three(ps2(f"br{i}.{p}")[:, j, :], high[:, k, o:o + P], low[:, k, o:o + P],
                                             ys_hi[i][:, k, :], ys_lo[i][:, k, :], k == 0, k == 3)
                        end(last)
            for p in range(4):
                project_split(f"w2o.{p}", BRANCH + 6 + p, merged_hi, merged_lo, lambda k: pe.wait_ge(s("merged_low"), k // 2 + 1))
            mean_squares(6)
            for u, name in enumerate(last_jobs):
                project_split(name, LAST + u, h_hi, h_lo, (lambda k: pe.wait_ge(s("h_low"), 8 + k + 1)) if u == 0 else no_wait)
            rows_split([f"fd.{p}" for p in range(4)], DOWN, 0, 6, lambda k: big_hi(k)[:, 0, :], lambda k: pe.wait_ge(s("a_low"), 16 + k // 2 + 1))
            assert at[0] == len(JOBS)


def shape_constants():
    f = np.float32
    inv = (np.float64(10000.0) ** (-np.arange(0, P, 2) / P)).astype(f)
    ang = (np.arange(T, dtype=f)[:, None] * inv[None, :]).astype(f)
    cos, sin = np.cos(ang).astype(f).T, np.sin(ang).astype(f).T
    perm = np.zeros((P, P), f)
    half = P // 2
    perm[np.arange(half) + half, np.arange(half)] = -1.0
    perm[np.arange(half), np.arange(half) + half] = 1.0
    rope = np.concatenate([np.concatenate([cos, cos]), np.concatenate([sin, sin]), perm], 1)
    log_g = np.log1p(-np.exp2(-5.0 - np.arange(HEADS)))
    m = np.arange(T).reshape(2, P)
    dist = np.abs(m[:, :, None] - np.arange(T)[None, None, :])
    decay = np.exp(log_g[:, None, None, None] * dist[None]) * P ** -0.5
    decay = decay.transpose(2, 0, 1, 3).reshape(P, -1)
    q = np.arange(T).reshape(2, P)
    fox = np.where(np.arange(T)[None, None, :] <= q[:, :, None], 0.0, NEG).transpose(1, 0, 2).reshape(P, -1)
    i = np.arange(P)
    gla = (i[:, None] <= i[None, :]) & (i[:, None] // CHUNK == i[None, :] // CHUNK)
    scan = np.broadcast_to((np.arange(T) % CHUNK != 0), (P, T))
    return {"rope": rope.astype(f), "decay": decay.astype(f), "foxmask": fox.astype(f), "glamask": gla.astype(np.int32),
            "scanmask": scan.astype(f), "ident": np.eye(P, dtype=f)}


def kernel(**inp):
    import concourse.bacc as bacc
    from concourse.bass_utils import run_bass_kernel_spmd as run

    inp = {k: np.asarray(v) for k, v in inp.items()}

    def cols_of(v):
        return np.reshape(v, (-1, P)).T

    b_fox = np.zeros((P, 1), np.float32)
    b_fox[0:HEADS, 0] = inp["b_fox_f_2"][0]
    b_fox[32:32 + HEADS, 0] = inp["b_fox_f_2"][0]
    pack = {
        "c": cols_of(inp["c"]), "norm_g": cols_of(inp["norm_g"]), "ada_b": cols_of(inp["ada_b"]),
        "conv_w": inp["conv_w"][0].reshape(TAPS, 4, P).transpose(2, 1, 0).reshape(P, -1), "conv_b": cols_of(inp["conv_b"]),
        "cln_g": cols_of(inp["cln_g"]), "cln_b": cols_of(inp["cln_b"]), "s5_d": cols_of(inp["s5_d"]),
        "norm_f": cols_of(inp["norm_f"]), "g_mix": cols_of(inp["g_mix_2"]), "b_gla": cols_of(inp["b_gla_a_2"]),
        "g_gla": cols_of(inp["g_gla_out_2"]), "g_fq": cols_of(inp["g_fox_q_2"]), "g_fk": cols_of(inp["g_fox_k_2"]),
        "g_mem": cols_of(inp["g_mem_2"]), "g_mq": cols_of(inp["g_mem_q_2"]), "g_mk": cols_of(inp["g_mem_k_2"]),
        "b_gate": cols_of(inp["b_gate_2"]), "g_ffn": cols_of(inp["g_ffn_2"]), "b_fox": b_fox,
    }
    cols = np.concatenate([pack[name] for name in COLS], 1)

    def states(v):
        return v.reshape(2, 32, 2, 64).transpose(2, 3, 0, 1).reshape(P, 64)

    step = np.repeat(inp["s5_log_step"][0][:, :, None], 64, 2)
    scal = np.concatenate([states(inp["s5_lam_re"][0]), states(inp["s5_lam_im"][0]), states(step)], 1)
    bw = np.zeros((4, 2, 16, 8, 2, 2, 2, 64), np.float32)
    cw = np.zeros((2, 64, 2, 2, 32, 2, 16), np.float32)
    for r, (bn, cn) in enumerate((("s5_b_re", "s5_c_re"), ("s5_b_im", "s5_c_im"))):
        b = inp[bn][0].reshape(2, 8, 4, 2, 64, 16)
        c = inp[cn][0].reshape(2, 32, 2, 16, 64)
        for g in range(2):
            bw[:, g, :, :, :, r, g, :] = b[:, :, :, g].transpose(2, 4, 1, 0, 3)
            cw[g, :, r, :, :, g, :] = c[:, :, g].transpose(3, 0, 1, 2)
    w_fox = np.zeros((D, 64), np.float32)
    w_fox[:, 0:HEADS] = inp["w_in_2"][0][:, FFG:FFG + HEADS]
    w_fox[:, 32:32 + HEADS] = inp["w_in_2"][0][:, FFG:FFG + HEADS]
    arrays = {
        "x": inp["x"][0].T, "mem": inp["mem_2"][0].T, "cols": cols, "s5_scal": scal,
        "s5_b": bw.reshape(P, 4096), "s5_c": cw.reshape(P, 2, 2048), "w_fox_f": w_fox,
        "ada_w": inp["ada_w"], "w_in": inp["w_in"][0], "w_out": inp["w_out"][0], "w_fc1": inp["w_fc1"], "w_fc2": inp["w_fc2"],
        "w_glu_a": inp["w_glu_a"][0], "w_glu_b": inp["w_glu_b"][0], "w_in_2": inp["w_in_2"][0], "w_mem_kv": inp["w_mem_kv_2"][0],
        "w_gla_a2": inp["w_gla_a2_2"][0], "w_branch": inp["w_branch_2"][0], "w_out_2": inp["w_out_2"][0],
        "w_ffn_gate": inp["w_ffn_gate_2"][0], "w_ffn_up": inp["w_ffn_up_2"][0], "w_ffn_down": inp["w_ffn_down_2"][0],
    }
    arrays.update(shape_constants())
    arrays = {k: np.ascontiguousarray(v) for k, v in arrays.items()}
    nc = bacc.Bacc("TRN2", target_bir_lowering=False, num_devices=1)
    aps = {k: nc.dram_tensor(f"in_{k}", v.shape, mybir.dt.from_np(v.dtype), kind="ExternalInput").ap() for k, v in arrays.items()}
    out = nc.dram_tensor("out_t", (D, T), F32, kind="ExternalOutput").ap()
    build(nc, aps, out)
    r = run(nc, [{f"in_{k}": v for k, v in arrays.items()}], core_ids=[0])
    return np.ascontiguousarray(np.asarray(r.results[0]["out_t"]).T)[None]
```
